# Optimizing a Trainium2 kernel written in Bass

```python
import math
import jax
import jax.numpy as jnp
from jax import lax
import numpy as np
import jax, jax.numpy as jnp

D_MODEL = 1024
BATCH = 1
SEQ = 256
DEPTH = 1

F32 = jnp.float32
RMS_EPS = 1e-6
N_ATTN_HEADS = 8
ATTN_HEAD_DIM = 64
ATTN_W = N_ATTN_HEADS * ATTN_HEAD_DIM
IDX_HEADS = 16
IDX_DIM = 32
IDX_Q = IDX_HEADS * IDX_DIM
TOPK_MAX = 256
Q_BLOCK = 64
N_BUCKETS = 32
MAX_DISTANCE = 128
RWKV_HEADS = 8
RWKV_HEAD = 64
RWKV_W = RWKV_HEADS * RWKV_HEAD
DECAY_LORA = 64
ICLR_LORA = 64
GATE_LORA = 128
RWKV_IN = 3 * RWKV_W + DECAY_LORA + ICLR_LORA + GATE_LORA
GN_EPS = 64e-5
RWKV_START = 3 * ATTN_W + IDX_Q + IDX_DIM + IDX_HEADS
N_IN = RWKV_START + RWKV_IN + 2 * D_MODEL
IN_SPLITS = (ATTN_W, 2 * ATTN_W, 3 * ATTN_W, 3 * ATTN_W + IDX_Q,
             3 * ATTN_W + IDX_Q + IDX_DIM, RWKV_START,
             RWKV_START + RWKV_IN, RWKV_START + RWKV_IN + D_MODEL)
RWKV_SPLITS = (RWKV_W, 2 * RWKV_W, 3 * RWKV_W, 3 * RWKV_W + DECAY_LORA,
               3 * RWKV_W + DECAY_LORA + ICLR_LORA)
N_EXPERTS = 64
N_GROUPS = 8
TOPK_GROUPS = 4
MOE_TOPK = 8
EXPERT_FF = 256
ROUTED_SCALE = 2.5
EXPERT_BLOCK = 128


def rms_norm(x, g):
    xf = x.astype(F32)
    y = xf * lax.rsqrt(jnp.mean(xf * xf, axis=-1, keepdims=True) + RMS_EPS)
    return (y * g.astype(F32)).astype(x.dtype)

def t5_bucket(rel):
    n = jnp.maximum(rel, 0)
    max_exact = N_BUCKETS // 2
    nf = jnp.maximum(n, 1).astype(F32)
    large = max_exact + (jnp.log(nf / max_exact) / math.log(MAX_DISTANCE / max_exact)
                         * (N_BUCKETS - max_exact)).astype(jnp.int32)
    large = jnp.minimum(large, N_BUCKETS - 1)
    return jnp.where(n < max_exact, n, large)

def dsa_sparse_attention(q, k, v, q_idx, k_idx, w_idx, rel_bias):
    B, S = q.shape[0], q.shape[1]
    top_k = min(TOPK_MAX, S // 4)
    nb = S // Q_BLOCK
    k_flat = k.reshape(B, S, ATTN_W)
    v_flat = v.reshape(B, S, ATTN_W)
    key_pos = jnp.arange(S, dtype=jnp.int32)
    idx_scale = (IDX_HEADS ** -0.5) * (IDX_DIM ** -0.5)

    def to_blocks(t):
        return jnp.moveaxis(t.reshape((B, nb, Q_BLOCK) + t.shape[2:]), 1, 0)

    def block(args):
        qb, qib, wib, start = args
        q_pos = start + jnp.arange(Q_BLOCK, dtype=jnp.int32)
        dots = jnp.einsum('bqhd,bsd->bqhs', qib, k_idx, preferred_element_type=F32)
        idx_score = jnp.einsum('bqhs,bqh->bqs', jax.nn.relu(dots), wib.astype(F32)) * idx_scale
        causal = key_pos[None, :] <= q_pos[:, None]
        idx_score = jnp.where(causal[None], idx_score, -jnp.inf)
        _, sel = lax.top_k(idx_score, top_k)
        kg = jax.vmap(lambda kf, i: kf[i])(k_flat, sel).reshape(B, Q_BLOCK, top_k, N_ATTN_HEADS, ATTN_HEAD_DIM)
        vg = jax.vmap(lambda vf, i: vf[i])(v_flat, sel).reshape(B, Q_BLOCK, top_k, N_ATTN_HEADS, ATTN_HEAD_DIM)
        logits = jnp.einsum('bqhd,bqkhd->bqhk', qb, kg, preferred_element_type=F32) * (ATTN_HEAD_DIM ** -0.5)
        rel = q_pos[None, :, None] - sel
        bias = rel_bias[t5_bucket(rel)].astype(F32)
        logits = logits + jnp.moveaxis(bias, -1, 2)
        valid = sel <= q_pos[None, :, None]
        logits = jnp.where(valid[:, :, None, :], logits, -jnp.inf)
        p = jax.nn.softmax(logits, axis=-1).astype(vg.dtype)
        return jnp.einsum('bqhk,bqkhd->bqhd', p, vg)

    starts = jnp.arange(nb, dtype=jnp.int32) * Q_BLOCK
    out = lax.map(block, (to_blocks(q), to_blocks(q_idx), to_blocks(w_idx), starts))
    return jnp.moveaxis(out, 0, 1).reshape(B, S, ATTN_W)

def wkv7_scan(r, decay, k, v, a, b):
    B, S, H, N = r.shape

    def step(state, inp):
        r_t, w_t, k_t, v_t, a_t, b_t = inp
        sa = jnp.einsum('bhij,bhj->bhi', state, a_t)
        state = state * w_t[:, :, None, :] + sa[..., None] * b_t[:, :, None, :] + v_t[..., None] * k_t[:, :, None, :]
        y = jnp.einsum('bhij,bhj->bhi', state, r_t)
        return state, y

    xs = tuple(jnp.moveaxis(t, 1, 0) for t in (r, decay, k, v, a, b))
    _, ys = lax.scan(step, jnp.zeros((B, H, N, N), F32), xs)
    return jnp.moveaxis(ys, 0, 1)

def rwkv7_branch(z, tshift_mu, decay_w0, decay_up, iclr_a0, iclr_up, gate_up, k_k, k_a, r_k, lnx_g, lnx_b):
    B, S = z.shape[0], z.shape[1]
    z_prev = jnp.pad(z[:, :-1], ((0, 0), (1, 0), (0, 0)))
    z = (z + tshift_mu * (z_prev - z)).astype(F32)
    r, k, v, wd, ad, gd = jnp.split(z, RWKV_SPLITS, axis=-1)
    w_log = -jax.nn.softplus(-(decay_w0.astype(F32) + jnp.tanh(wd) @ decay_up.astype(F32))) - 0.5
    decay = jnp.exp(-jnp.exp(w_log))
    a = jax.nn.sigmoid(iclr_a0.astype(F32) + ad @ iclr_up.astype(F32))
    g = jax.nn.sigmoid(gd) @ gate_up.astype(F32)
    heads = lambda t: t.reshape(B, S, RWKV_HEADS, RWKV_HEAD)
    kk = heads(k * k_k.astype(F32))
    kk = kk / jnp.maximum(jnp.sqrt(jnp.sum(kk * kk, axis=-1, keepdims=True)), 1e-12)
    k = k * (1.0 + (a - 1.0) * k_a.astype(F32))
    r, k, v, decay, a = heads(r), heads(k), heads(v), heads(decay), heads(a)
    y = wkv7_scan(r, decay, k, v, -kk, kk * a)
    mu = jnp.mean(y, axis=-1, keepdims=True)
    var = jnp.mean(jnp.square(y - mu), axis=-1, keepdims=True)
    yn = ((y - mu) * lax.rsqrt(var + GN_EPS)).reshape(B, S, RWKV_W)
    yn = yn * lnx_g.astype(F32) + lnx_b.astype(F32)
    bonus = (jnp.sum(r * k * r_k.astype(F32), axis=-1, keepdims=True) * v).reshape(B, S, RWKV_W)
    return (yn + bonus) * g

def swiglu(h, wg, wu, wd):
    return (jax.nn.silu(h @ wg) * (h @ wu)) @ wd

def moe_ffn(h, router_w, router_bias, exp_gate, exp_up, exp_down, sh_gate, sh_up, sh_down):
    B, S, D = h.shape
    T = B * S
    hf = h.reshape(T, D)
    scores = jax.nn.sigmoid(jnp.einsum('td,de->te', hf, router_w, preferred_element_type=F32))
    choice = scores + router_bias.astype(F32)
    grp_score = lax.top_k(choice.reshape(T, N_GROUPS, N_EXPERTS // N_GROUPS), 2)[0].sum(-1)
    _, top_g = lax.top_k(grp_score, TOPK_GROUPS)
    gmask = jnp.any(top_g[:, :, None] == jnp.arange(N_GROUPS)[None, None, :], axis=1)
    emask = jnp.repeat(gmask, N_EXPERTS // N_GROUPS, axis=1)
    _, top_e = lax.top_k(jnp.where(emask, choice, -jnp.inf), MOE_TOPK)
    gw = jnp.take_along_axis(scores, top_e, axis=1)
    gw = gw / jnp.sum(gw, axis=-1, keepdims=True) * ROUTED_SCALE
    A = T * MOE_TOPK
    flat_e = top_e.reshape(A)
    order = jnp.argsort(flat_e)
    se = flat_e[order]
    counts = jnp.bincount(flat_e, length=N_EXPERTS)
    padded = (counts + EXPERT_BLOCK - 1) // EXPERT_BLOCK * EXPERT_BLOCK
    start = jnp.cumsum(counts) - counts
    pend = jnp.cumsum(padded)
    pstart = pend - padded
    dest = pstart[se] + jnp.arange(A, dtype=jnp.int32) - start[se]
    n_blocks = -(-A // EXPERT_BLOCK) + N_EXPERTS
    P = n_blocks * EXPERT_BLOCK
    slot_tok = jnp.zeros((P,), jnp.int32).at[dest].set((order // MOE_TOPK).astype(jnp.int32))
    slot_w = jnp.zeros((P,), F32).at[dest].set(gw.reshape(A)[order])
    block_start = jnp.arange(n_blocks, dtype=jnp.int32) * EXPERT_BLOCK
    block_e = jnp.minimum(jnp.sum(pend[None, :] <= block_start[:, None], axis=1), N_EXPERTS - 1)

    def step(y, blk):
        tok, wt, e = blk
        out = swiglu(hf[tok], exp_gate[e], exp_up[e], exp_down[e])
        return y.at[tok].add(out.astype(F32) * wt[:, None]), None

    y, _ = lax.scan(step, jnp.zeros((T, D), F32),
                    (slot_tok.reshape(n_blocks, EXPERT_BLOCK), slot_w.reshape(n_blocks, EXPERT_BLOCK), block_e))
    shared = swiglu(hf, sh_gate, sh_up, sh_down)
    return (y.astype(h.dtype) + shared).reshape(B, S, D)

def hybrid_layer(x, c, ada_w, ada_b, norm1_g, w_in, rel_bias, tshift_mu, decay_w0, decay_up,
                 iclr_a0, iclr_up, gate_up, k_k, k_a, r_k, lnx_g, lnx_b, w_attn_br, w_rwkv_br,
                 w_out, norm2_g, router_w, router_bias, exp_gate, exp_up, exp_down,
                 sh_gate, sh_up, sh_down):
    B, S, D = x.shape
    mod = (jax.nn.silu(c.astype(F32)) @ ada_w.astype(F32) + ada_b.astype(F32)).astype(x.dtype)
    sh1, sc1, g1, sh2, sc2, g2 = [m[:, None, :] for m in jnp.split(mod, 6, axis=-1)]
    h = rms_norm(x, norm1_g) * (1 + sc1) + sh1
    z = h @ w_in
    q, k, v, iq, ik, iw, zr, ga, gr = jnp.split(z, IN_SPLITS, axis=-1)
    hs = lambda t: t.reshape(B, S, N_ATTN_HEADS, ATTN_HEAD_DIM)
    attn = dsa_sparse_attention(hs(q), hs(k), hs(v), iq.reshape(B, S, IDX_HEADS, IDX_DIM), ik, iw, rel_bias)
    rw = rwkv7_branch(zr, tshift_mu, decay_w0, decay_up, iclr_a0, iclr_up, gate_up,
                      k_k, k_a, r_k, lnx_g, lnx_b).astype(x.dtype)
    mixed = jax.nn.sigmoid(ga) * (attn @ w_attn_br) + jax.nn.sigmoid(gr) * (rw @ w_rwkv_br)
    x = x + g1 * (mixed @ w_out)
    h2 = rms_norm(x, norm2_g) * (1 + sc2) + sh2
    x = x + g2 * moe_ffn(h2, router_w, router_bias, exp_gate, exp_up, exp_down, sh_gate, sh_up, sh_down)
    return x

def first_inputs(seed: int = 0) -> dict:
    key = jax.random.key(seed)
    ks = iter(jax.random.split(key, 40))
    L, D = DEPTH, D_MODEL

    def nrm(shape, scale):
        return jax.random.normal(next(ks), shape, F32) * scale

    def uni(shape, lo, hi):
        return jax.random.uniform(next(ks), shape, F32, lo, hi)

    return {
        'x': nrm((BATCH, SEQ, D), 1.0),
        'c': nrm((BATCH, D), 1.0),
        'ada_w': nrm((L, D, 6 * D), 0.5 * D ** -0.5),
        'ada_b': nrm((L, 6 * D), 0.02),
        'norm1_g': 1.0 + nrm((L, D), 0.02),
        'w_in': nrm((L, D, N_IN), D ** -0.5),
        'rel_bias': nrm((N_BUCKETS, N_ATTN_HEADS), 0.5),
        'tshift_mu': uni((L, RWKV_IN), 0.0, 1.0),
        'decay_w0': uni((L, RWKV_W), -3.0, 1.0),
        'decay_up': nrm((L, DECAY_LORA, RWKV_W), 0.1),
        'iclr_a0': nrm((L, RWKV_W), 0.5),
        'iclr_up': nrm((L, ICLR_LORA, RWKV_W), ICLR_LORA ** -0.5),
        'gate_up': nrm((L, GATE_LORA, RWKV_W), GATE_LORA ** -0.5),
        'k_k': 0.85 + nrm((L, RWKV_W), 0.02),
        'k_a': 1.0 + nrm((L, RWKV_W), 0.02),
        'r_k': nrm((L, RWKV_HEADS, RWKV_HEAD), 0.1),
        'lnx_g': 1.0 + nrm((L, RWKV_W), 0.02),
        'lnx_b': nrm((L, RWKV_W), 0.02),
        'w_attn_br': nrm((L, ATTN_W, D), ATTN_W ** -0.5),
        'w_rwkv_br': nrm((L, RWKV_W, D), RWKV_W ** -0.5),
        'w_out': nrm((L, D, D), D ** -0.5),
        'norm2_g': 1.0 + nrm((L, D), 0.02),
        'router_w': nrm((L, D, N_EXPERTS), D ** -0.5),
        'router_bias': nrm((L, N_EXPERTS), 0.01),
        'exp_gate': nrm((L, N_EXPERTS, D, EXPERT_FF), D ** -0.5),
        'exp_up': nrm((L, N_EXPERTS, D, EXPERT_FF), D ** -0.5),
        'exp_down': nrm((L, N_EXPERTS, EXPERT_FF, D), EXPERT_FF ** -0.5),
        'sh_gate': nrm((L, D, EXPERT_FF), D ** -0.5),
        'sh_up': nrm((L, D, EXPERT_FF), D ** -0.5),
        'sh_down': nrm((L, EXPERT_FF, D), EXPERT_FF ** -0.5),
        'final_g': 1.0 + nrm((D,), 0.02),
    }

def first_block(x, c, ada_w, ada_b, norm1_g, w_in, rel_bias, tshift_mu, decay_w0, decay_up,
              iclr_a0, iclr_up, gate_up, k_k, k_a, r_k, lnx_g, lnx_b, w_attn_br, w_rwkv_br,
              w_out, norm2_g, router_w, router_bias, exp_gate, exp_up, exp_down,
              sh_gate, sh_up, sh_down, final_g):
    for l in range(DEPTH):
        x = hybrid_layer(x, c, ada_w[l], ada_b[l], norm1_g[l], w_in[l], rel_bias, tshift_mu[l],
                         decay_w0[l], decay_up[l], iclr_a0[l], iclr_up[l], gate_up[l], k_k[l],
                         k_a[l], r_k[l], lnx_g[l], lnx_b[l], w_attn_br[l], w_rwkv_br[l], w_out[l],
                         norm2_g[l], router_w[l], router_bias[l], exp_gate[l], exp_up[l],
                         exp_down[l], sh_gate[l], sh_up[l], sh_down[l])
    return rms_norm(x, final_g)


DEPTH_2 = 2

CHUNK = 64
MEM_LEN = 256
QBLOCK = 128
EPS = 1e-6

DIFF_HEADS = 4
DIFF_DK = 64
DIFF_DV = 2 * DIFF_DK
DIFF_SCALE = DIFF_DK ** -0.5
MLA_HEADS = 4
MLA_NOPE = 128
MLA_ROPE = 64
MLA_DV = 128
MLA_Q_LORA = 256
MLA_KV_LORA = 128
MLA_SCALE = (MLA_NOPE + MLA_ROPE) ** -0.5
ROPE_BASE = 10000.0
EVEN_SPLITS = (DIFF_HEADS * 2 * DIFF_DK, DIFF_HEADS * 2 * DIFF_DK, DIFF_HEADS * DIFF_DV, MLA_Q_LORA, MLA_KV_LORA, MLA_ROPE)
EVEN_IN = sum(EVEN_SPLITS)
EVEN_MIX = DIFF_HEADS * DIFF_DV + MLA_HEADS * MLA_DV
SB_HEADS = 16
SB_DH = 64
SB_WIDTH = SB_HEADS * SB_DH
SB_SCALE = SB_DH ** -0.5
XA_HEADS = 4
XA_DH = D_MODEL // XA_HEADS
D_FF = 4 * D_MODEL

N_EVEN = (DEPTH_2 + 1) // 2
N_ODD = DEPTH_2 // 2


def _rms(x, g):
    xf = x.astype(jnp.float32)
    y = xf * lax.rsqrt(jnp.mean(xf * xf, axis=-1, keepdims=True) + EPS)
    return (y * g.astype(jnp.float32)).astype(x.dtype)

def _heads(x, h):
    b, s, _ = x.shape
    return x.reshape(b, s, h, -1).transpose(0, 2, 1, 3)

def _merge(x):
    b, h, s, d = x.shape
    return x.transpose(0, 2, 1, 3).reshape(b, s, h * d)

def _rope(x, pos):
    half = x.shape[-1] // 2
    inv = ROPE_BASE ** (-jnp.arange(half, dtype=jnp.float32) / half)
    ang = pos.astype(jnp.float32)[:, None] * inv[None, :]
    cos, sin = jnp.cos(ang), jnp.sin(ang)
    xf = x.astype(jnp.float32)
    x1, x2 = xf[..., :half], xf[..., half:]
    return jnp.concatenate([x1 * cos - x2 * sin, x2 * cos + x1 * sin], axis=-1).astype(x.dtype)

def _chunk_mask(t, s):
    return (s // CHUNK)[None, :] <= (t // CHUNK)[:, None]

def _sweep(block_fn, qs):
    b, _, s, _ = qs[0].shape
    nb = s // QBLOCK
    qs_b = tuple(jnp.moveaxis(q.reshape(b, q.shape[1], nb, QBLOCK, q.shape[-1]), 2, 0) for q in qs)
    out = lax.map(lambda a: block_fn(a[0], *a[1]), (jnp.arange(nb), qs_b))
    out = jnp.moveaxis(out, 0, 2)
    return out.reshape(b, out.shape[1], s, out.shape[-1])

def _even_mixer(h, w_in, lq1, lk1, lq2, lk2, g_sub, g_cq, w_uq, g_ckv, w_ukv, w_out, lambda_init):
    b, s, _ = h.shape
    pos = jnp.arange(s)
    proj = h @ w_in
    cuts = np.cumsum(EVEN_SPLITS)[:-1].tolist()
    aq, ak, av, cq, ckv, kr = jnp.split(proj, cuts, axis=-1)

    aq = aq.reshape(b, s, DIFF_HEADS, 2, DIFF_DK)
    ak = ak.reshape(b, s, DIFF_HEADS, 2, DIFF_DK)
    q1 = aq[:, :, :, 0].transpose(0, 2, 1, 3)
    q2 = aq[:, :, :, 1].transpose(0, 2, 1, 3)
    k1 = ak[:, :, :, 0].transpose(0, 2, 1, 3)
    k2 = ak[:, :, :, 1].transpose(0, 2, 1, 3)
    va = _heads(av, DIFF_HEADS)
    lam = (jnp.exp(jnp.sum(lq1.astype(jnp.float32) * lk1.astype(jnp.float32)))
           - jnp.exp(jnp.sum(lq2.astype(jnp.float32) * lk2.astype(jnp.float32))) + lambda_init)
    slopes = 2.0 ** (-8.0 * jnp.arange(1, DIFF_HEADS + 1, dtype=jnp.float32) / DIFF_HEADS)

    def diff_block(i, q1b, q2b):
        t = i * QBLOCK + jnp.arange(QBLOCK)
        mask = _chunk_mask(t, pos)
        dist = jnp.abs(t[:, None] - pos[None, :]).astype(jnp.float32)
        bias = -slopes[:, None, None] * dist[None]

        def probs(qb, kk):
            sc = jnp.einsum('bhqd,bhkd->bhqk', qb, kk).astype(jnp.float32) * DIFF_SCALE + bias
            return jax.nn.softmax(jnp.where(mask, sc, -jnp.inf), axis=-1)

        p = probs(q1b, k1) - lam * probs(q2b, k2)
        return jnp.einsum('bhqk,bhkd->bhqd', p.astype(va.dtype), va)

    o_a = _sweep(diff_block, (q1, q2))
    o_a = _rms(o_a, g_sub) * (1.0 - lambda_init)

    q = _heads(_rms(cq, g_cq) @ w_uq, MLA_HEADS)
    q_nope, q_rope = q[..., :MLA_NOPE], _rope(q[..., MLA_NOPE:], pos)
    kv = _heads(_rms(ckv, g_ckv) @ w_ukv, MLA_HEADS)
    k_nope, vb = kv[..., :MLA_NOPE], kv[..., MLA_NOPE:]
    k_rope = _rope(kr, pos)

    def mla_block(i, qnb, qrb):
        t = i * QBLOCK + jnp.arange(QBLOCK)
        mask = _chunk_mask(t, pos)
        sc = (jnp.einsum('bhqd,bhkd->bhqk', qnb, k_nope)
              + jnp.einsum('bhqr,bkr->bhqk', qrb, k_rope)).astype(jnp.float32) * MLA_SCALE
        p = jax.nn.softmax(jnp.where(mask, sc, -jnp.inf), axis=-1)
        return jnp.einsum('bhqk,bhkd->bhqd', p.astype(vb.dtype), vb)

    o_b = _sweep(mla_block, (q_nope, q_rope))

    return jnp.concatenate([_merge(o_a), _merge(o_b)], axis=-1) @ w_out

def _odd_mixer(h, w_in, w_out):
    s = h.shape[1]
    pos = jnp.arange(s)
    q, k, v = jnp.split(h @ w_in, 3, axis=-1)
    q, k, v = _heads(q, SB_HEADS), _heads(k, SB_HEADS), _heads(v, SB_HEADS)

    def sb_block(i, qb):
        t = i * QBLOCK + jnp.arange(QBLOCK)
        strict = pos[None, :] < t[:, None]
        z = jnp.einsum('bhqd,bhkd->bhqk', qb, k).astype(jnp.float32) * SB_SCALE
        log_beta = jax.nn.log_sigmoid(z)
        log_keep = jnp.where(strict, jax.nn.log_sigmoid(-z), 0.0)
        between = lax.cumsum(log_keep, axis=3, reverse=True) - log_keep
        a = jnp.where(strict, jnp.exp(log_beta + between), 0.0)
        return jnp.einsum('bhqk,bhkd->bhqd', a.astype(v.dtype), v)

    o = _sweep(sb_block, (q,))
    return _merge(o) @ w_out

def _cross(h, mem_n, wq, wkv, wo):
    q = _heads(h @ wq, XA_HEADS)
    k, v = jnp.split(mem_n @ wkv, 2, axis=-1)
    k, v = _heads(k, XA_HEADS), _heads(v, XA_HEADS)
    sc = jnp.einsum('bhqd,bhkd->bhqk', q, k).astype(jnp.float32) * (XA_DH ** -0.5)
    p = jax.nn.softmax(sc, axis=-1)
    return _merge(jnp.einsum('bhqk,bhkd->bhqd', p.astype(v.dtype), v)) @ wo

def _mlp(h, w1, w2):
    return jnp.square(jax.nn.relu(h @ w1)) @ w2

def second_inputs(seed: int = 0) -> dict:
    key = jax.random.key(seed)
    ks = iter(jax.random.split(key, 40))

    def nrm(shape, scale):
        return jax.random.normal(next(ks), shape, jnp.float32) * scale

    def gain(shape):
        return 1.0 + nrm(shape, 0.02)

    L, E, O, D = DEPTH_2, N_EVEN, N_ODD, D_MODEL
    return {
        'x': nrm((BATCH, SEQ, D), 1.0),
        'mem': nrm((BATCH, MEM_LEN, D), 1.0),
        'ev_norm': gain((E, D)),
        'ev_w_in': nrm((E, D, EVEN_IN), D ** -0.5),
        'diff_lq1': nrm((E, DIFF_DK), 0.1),
        'diff_lk1': nrm((E, DIFF_DK), 0.1),
        'diff_lq2': nrm((E, DIFF_DK), 0.1),
        'diff_lk2': nrm((E, DIFF_DK), 0.1),
        'diff_subln': gain((E, DIFF_DV)),
        'mla_g_cq': gain((E, MLA_Q_LORA)),
        'mla_w_uq': nrm((E, MLA_Q_LORA, MLA_HEADS * (MLA_NOPE + MLA_ROPE)), MLA_Q_LORA ** -0.5),
        'mla_g_ckv': gain((E, MLA_KV_LORA)),
        'mla_w_ukv': nrm((E, MLA_KV_LORA, MLA_HEADS * (MLA_NOPE + MLA_DV)), MLA_KV_LORA ** -0.5),
        'ev_w_out': nrm((E, EVEN_MIX, D), EVEN_MIX ** -0.5),
        'od_norm': gain((O, D)),
        'sb_w_in': nrm((O, D, 3 * SB_WIDTH), D ** -0.5),
        'sb_w_out': nrm((O, SB_WIDTH, D), SB_WIDTH ** -0.5),
        'xa_norm': gain((L, D)),
        'xa_mem_norm': gain((L, D)),
        'xa_wq': nrm((L, D, D), D ** -0.5),
        'xa_wkv': nrm((L, D, 2 * D), D ** -0.5),
        'xa_wo': nrm((L, D, D), D ** -0.5),
        'mlp_norm': gain((L, D)),
        'mlp_w1': nrm((L, D, D_FF), D ** -0.5),
        'mlp_w2': nrm((L, D_FF, D), D_FF ** -0.5),
        'final_norm': gain((D,)),
    }

def second_block(x, mem, ev_norm, ev_w_in, diff_lq1, diff_lk1, diff_lq2, diff_lk2, diff_subln,
              mla_g_cq, mla_w_uq, mla_g_ckv, mla_w_ukv, ev_w_out, od_norm, sb_w_in, sb_w_out,
              xa_norm, xa_mem_norm, xa_wq, xa_wkv, xa_wo, mlp_norm, mlp_w1, mlp_w2, final_norm):
    h = x
    for i in range(DEPTH_2):
        j = i // 2
        if i % 2 == 0:
            lambda_init = 0.8 - 0.6 * math.exp(-0.3 * i)
            h = h + _even_mixer(_rms(h, ev_norm[j]), ev_w_in[j], diff_lq1[j], diff_lk1[j], diff_lq2[j],
                                diff_lk2[j], diff_subln[j], mla_g_cq[j], mla_w_uq[j], mla_g_ckv[j],
                                mla_w_ukv[j], ev_w_out[j], lambda_init)
        else:
            h = h + _odd_mixer(_rms(h, od_norm[j]), sb_w_in[j], sb_w_out[j])
        h = h + _cross(_rms(h, xa_norm[i]), _rms(mem, xa_mem_norm[i]), xa_wq[i], xa_wkv[i], xa_wo[i])
        h = h + _mlp(_rms(h, mlp_norm[i]), mlp_w1[i], mlp_w2[i])
    return _rms(h, final_norm)


def setup_inputs(seed=0):
    out = dict(first_inputs(seed))
    for name, value in second_inputs(seed + 1).items():
        if name != "x":
            out[name + "_2"] = value
    return out


def reference(
    x, c, ada_w, ada_b, norm1_g, w_in, rel_bias, tshift_mu, decay_w0, decay_up, iclr_a0,
    iclr_up, gate_up, k_k, k_a, r_k, lnx_g, lnx_b, w_attn_br, w_rwkv_br, w_out, norm2_g,
    router_w, router_bias, exp_gate, exp_up, exp_down, sh_gate, sh_up, sh_down, final_g, mem_2,
    ev_norm_2, ev_w_in_2, diff_lq1_2, diff_lk1_2, diff_lq2_2, diff_lk2_2, diff_subln_2,
    mla_g_cq_2, mla_w_uq_2, mla_g_ckv_2, mla_w_ukv_2, ev_w_out_2, od_norm_2, sb_w_in_2,
    sb_w_out_2, xa_norm_2, xa_mem_norm_2, xa_wq_2, xa_wkv_2, xa_wo_2, mlp_norm_2, mlp_w1_2,
    mlp_w2_2, final_norm_2,
):
    x = first_block(
        x, c, ada_w, ada_b, norm1_g, w_in, rel_bias, tshift_mu, decay_w0, decay_up, iclr_a0,
        iclr_up, gate_up, k_k, k_a, r_k, lnx_g, lnx_b, w_attn_br, w_rwkv_br, w_out, norm2_g,
        router_w, router_bias, exp_gate, exp_up, exp_down, sh_gate, sh_up, sh_down, final_g,
    )
    return second_block(
        x, mem_2, ev_norm_2, ev_w_in_2, diff_lq1_2, diff_lk1_2, diff_lq2_2, diff_lk2_2,
        diff_subln_2, mla_g_cq_2, mla_w_uq_2, mla_g_ckv_2, mla_w_ukv_2, ev_w_out_2, od_norm_2,
        sb_w_in_2, sb_w_out_2, xa_norm_2, xa_mem_norm_2, xa_wq_2, xa_wkv_2, xa_wo_2, mlp_norm_2,
        mlp_w1_2, mlp_w2_2, final_norm_2,
    )


_drawn_inputs = setup_inputs


def setup_inputs(seed=0):
    import zlib

    import numpy as np

    out = dict(_drawn_inputs(seed))
    spreads = {}
    factors = {'k_k': 5.738,
     'k_a': 5.149,
     'lnx_g': 5.054,
     'lnx_b': 5.701,
     'ev_norm_2': 2.919,
     'diff_lq1_2': 8.0,
     'diff_subln_2': 5.138,
     'mla_g_cq_2': 8.0,
     'mla_g_ckv_2': 8.0,
     'od_norm_2': 6.136,
     'xa_norm_2': 8.0,
     'xa_mem_norm_2': 8.0,
     'final_norm_2': 2.819}
    for name, (base, spread) in spreads.items():
        noise = np.random.default_rng([zlib.crc32(name.encode()), seed]).standard_normal(out[name].shape)
        drawn = base * np.exp(spread * noise) if base else spread * noise
        out[name] = jnp.asarray(drawn.astype(out[name].dtype))
    for name, factor in factors.items():
        out[name] = (out[name] * factor).astype(out[name].dtype)
    return out
```

```python
import math
from contextlib import ExitStack

import numpy as np

import concourse.bass as bass
from concourse import mybir

F32 = mybir.dt.float32
ACT = mybir.ActivationFunctionType
ALU = mybir.AluOpType
AX = mybir.AxisListType

P = 128
S = 256
TT = S // P
D = 1024
DC = D // P
DH = 64
QH = 8
IH = 16
ID = 32
TOPK = 64
C = 64
NC = S // C
NE = 64
FF = 256
EC = FF // P
RING = 6
SLOT = 2048
BIG = 1.0e30
TAKEN = -3.0e38
DECAY = math.exp(-0.5)

W_Q, W_K, W_V, W_IQ, W_IK, W_IW = 0, 512, 1024, 1536, 2048, 2080
W_ZR, W_GA, W_GR = 2096, 3888, 4912

COLS = (("tshift_mu", 14), ("decay_w0", 4), ("iclr_a0", 4), ("k_k", 4), ("k_a", 4), ("r_k", 4),
        ("lnx_g", 4), ("lnx_b", 4), ("diff_subln_2", 1), ("mla_g_cq_2", 2), ("mla_g_ckv_2", 1))
COL = {}
_at = 0
for _name, _rows in COLS:
    COL[_name] = _at
    _at += _rows
NCOL = _at
LAMBDA_INIT = 0.8 - 0.6 * math.exp(0.0)


def shape_constants():
    t = np.arange(P)
    q = np.arange(S).reshape(TT, P).transpose(1, 0)
    k = np.arange(S)
    out = {}
    out["c_ident"] = np.eye(P, dtype=np.float32)
    out["c_blockones"] = (t[:, None] // DH == t[None, :] // DH).astype(np.float32)
    out["c_causal"] = (k[None, None, :] <= q[:, :, None]).astype(np.float32)
    out["c_chunk"] = np.where(k[None, None, :] // C <= q[:, :, None] // C, 0.0, -BIG).astype(np.float32)
    out["c_strict"] = (q[:, :, None] < k[None, None, :]).astype(np.float32)
    out["c_later"] = (t[:, None] >= t[None, :]).astype(np.float32)
    out["c_dist"] = -np.abs(q[:, :, None] - k[None, None, :]).astype(np.float32)
    s = np.arange(C)
    pair = np.stack([(s[:, None] < s[None, :]), (s[:, None] <= s[None, :])], 1)
    out["c_pair"] = pair.astype(np.float32)
    lev = []
    n = 1
    while n < C:
        lev.append((s[:, None] // (2 * n) == s[None, :] // (2 * n)) & (s[:, None] // n % 2 == 0)
                   & (s[None, :] // n % 2 == 1))
        n *= 2
    out["c_levels"] = np.stack(lev, 1).astype(np.float32)
    out["c_restart"] = np.broadcast_to((k % C != 0).astype(np.float32), (P, S)).copy()
    dist = np.arange(S)
    nf = np.maximum(dist, 1).astype(np.float32)
    large = 16 + (np.log(nf / np.float32(16)) / np.float32(math.log(8.0)) * np.float32(16)).astype(np.int32)
    bucket = np.where(dist < 16, dist, np.minimum(large, 31))
    rev = np.zeros((32, 2 * S), np.float32)
    rev[bucket, S - 1 + dist] = 1.0
    rev[0, :S - 1] = 1.0
    out["c_bucket"] = rev
    inv = np.float32(10000.0) ** (-np.arange(32, dtype=np.float32) / np.float32(32))
    ang = (np.arange(S, dtype=np.float32)[:, None] * inv[None, :].astype(np.float32)).reshape(TT, P, 32).transpose(1, 0, 2)
    out["c_rope"] = np.stack([np.cos(ang), np.sin(ang)], 1).astype(np.float32)
    return out


class Stage:

    def __init__(self, nc, name):
        self.nc, self.name = nc, name
        self.ctx = ExitStack()
        self.sems = []

    def __enter__(self):
        self.ctx.__enter__()
        return self

    def __exit__(self, *exc):
        if self.sems and exc[0] is None:
            for sem in self.sems:
                self.nc.gpsimd.sem_clear(sem)
        return self.ctx.__exit__(*exc)

    def sbuf(self, name, shape):
        return self.ctx.enter_context(self.nc.sbuf_tensor(f"{self.name}_{name}", shape, F32))

    def sem(self, name):
        sem = self.ctx.enter_context(self.nc.semaphore(f"{self.name}_{name}"))
        self.sems.append(sem)
        return sem

    def block(self):
        return self.nc.Block()


class Chain:

    def __init__(self, eng, sem):
        self.eng, self.sem, self.n = eng, sem, 0

    def step(self, ins):
        self.n += 1
        ins.then_inc(self.sem, 1)
        self.eng.wait_ge(self.sem, self.n)
        return ins


class Weights:

    def __init__(self, nc, ctx):
        self.slots = ctx.enter_context(nc.sbuf_tensor("weight_ring", [P, RING, SLOT], F32))
        self.landed = [ctx.enter_context(nc.semaphore(f"weights_landed_{i}")) for i in range(RING)]
        self.filled = ctx.enter_context(nc.semaphore("banks_filled"))
        self.n_filled = 0
        self.done_at = {}
        self.items = []
        self.index = {}
        self.issued = 0

    def plan(self, stage, key, source, chunks, cols):
        self.index[key] = len(self.items)
        self.items.append((stage, source, chunks, cols))

    def view(self, key):
        n = self.index[key]
        _, _, chunks, cols = self.items[n]
        return self.slots[:, n % RING, 0:chunks * cols].rearrange("p (c n) -> p c n", c=chunks)

    def arrived(self, pe, key):
        n = self.index[key]
        pe.wait_ge(self.landed[n % RING], 16 * (n // RING + 1))

    def load(self, sp, n):
        _, source, chunks, cols = self.items[n]
        if n >= RING:
            sp.wait_ge(self.filled, self.done_at[n - RING])
        dst = self.slots[:, n % RING, 0:chunks * cols].rearrange("p (c n) -> p c n", c=chunks)
        sp.dma_start(dst, source).then_inc(self.landed[n % RING], 16)


class Hybrid:
    def __init__(self, nc, dram, out):
        self.nc, self.dram, self.out = nc, dram, out
        self.ctx = ExitStack()
        self.layer = ExitStack()
        self.psum = self.ctx.enter_context(nc.psum_tensor("psum", [P, 8, 512], F32))
        self.w = Weights(nc, self.ctx)
        self.stage_no = 0
        self.plan_weights()

    def keep(self, name, shape, layer=False):
        t = (self.layer if layer else self.ctx).enter_context(self.nc.sbuf_tensor(name, shape, F32))
        return t

    def plan_weights(self):
        d, w = self.dram, self.w

        def wide(stage, name, src, rows_by_chunk, c0, ncols, step=None):
            rows = src.shape[0]
            nk = rows // P
            step = step or SLOT // nk
            how = "(c p) n -> p c n" if rows_by_chunk else "(p c) n -> p c n"
            for i in range(0, ncols, step):
                n = min(step, ncols - i)
                w.plan(stage, (name, i // step), src.rearrange(how, p=P)[:, :, c0 + i:c0 + i + n], nk, n)

        z = d["w_in"][0]
        wide("mod1", "mod1", d["ada_w"][0], False, 0, 2 * D)
        wide("zr", "w_zr", z, False, W_ZR, 1792)
        wide("mod2", "mod2", d["ada_w"][0], False, 2 * D, 4 * D)
        wide("z", "w_q", z, False, W_Q, 512)
        wide("z", "w_k", z, False, W_K, 512)
        wide("z", "w_v", z, False, W_V, 512)
        wide("z", "w_iq", z, False, W_IQ, 512)
        wide("z", "w_ikw", z, False, W_IK, 48)
        wide("z", "w_ga", z, False, W_GA, D)
        wide("z", "w_gr", z, False, W_GR, D)
        wide("mix", "w_attn_br", d["w_attn_br"][0], True, 0, D)
        wide("mix", "w_rwkv_br", d["w_rwkv_br"][0], True, 0, D)
        wide("out", "w_out", d["w_out"][0], True, 0, D)
        wide("router", "router_w", d["router_w"][0], False, 0, NE)
        wide("moe", "sh_gate", d["sh_gate"][0], False, 0, FF)
        wide("moe", "sh_up", d["sh_up"][0], False, 0, FF)
        for e in range(NE):
            wide("moe", ("exp_gate", e), d["exp_gate"][0, e], False, 0, FF)
            wide("moe", ("exp_up", e), d["exp_up"][0, e], False, 0, FF)
            if e == 0:
                wide("moe", "sh_down", d["sh_down"][0], True, 0, D)
            else:
                wide("moe", ("exp_down", e - 1), d["exp_down"][0, e - 1], True, 0, D)
        wide("moe", ("exp_down", NE - 1), d["exp_down"][0, NE - 1], True, 0, D)
        ev = d["ev_w_in_2"][0]
        wide("ev_in", "ev_in", ev, False, 0, 1984)
        wide("mla_up", "w_uq", d["mla_w_uq_2"][0], True, 0, 768)
        wide("mla_up", "w_ukv", d["mla_w_ukv_2"][0], True, 0, 1024)
        wide("ev_out", "ev_out", d["ev_w_out_2"][0], True, 0, D)
        for i in range(2):
            if i == 1:
                wide("sb_in", "sb_in", d["sb_w_in_2"][0], False, 0, 3 * D)
                wide("sb_out", "sb_out", d["sb_w_out_2"][0], True, 0, D)
            wide(f"xa_kv{i}", ("xa_wkv", i), d["xa_wkv_2"][i], False, 0, 2 * D)
            wide(f"xa_q{i}", ("xa_wq", i), d["xa_wq_2"][i], False, 0, D)
            wide(f"xa_o{i}", ("xa_wo", i), d["xa_wo_2"][i], True, 0, D)
            wide(f"mlp{i}", ("mlp_w1", i), d["mlp_w1_2"][i], False, 0, 4 * D)
            w2 = d["mlp_w2_2"][i].rearrange("(g c p) n -> g p c n", p=P, c=2)
            for g in range(16):
                w.plan(f"mlpd{i}", (("mlp_w2", i), g), w2[g], 2, D)

    def weight_loads(self, block, name):
        names = []
        for stage, *_ in self.w.items:
            if stage not in names:
                names.append(stage)
        done = set(names[:names.index(name) + 1]) if name in names else self.finished
        self.finished = done

        @block.sync
        def _(sp):
            w = self.w
            while w.issued < len(w.items) and (w.issued < RING or w.items[w.issued - RING][0] in done):
                w.load(sp, w.issued)
                w.issued += 1

    finished = frozenset()

    def products(self, name, units, extra=None):
        nc, w = self.nc, self.w
        BANKS = 8
        with Stage(nc, name) as st:
            filled, base = w.filled, w.n_filled
            drained = {"act": st.sem("drained_by_act"), "dve": st.sem("drained_by_dve")}
            steps = {"act": st.sem("act_steps"), "dve": st.sem("dve_steps")}
            extra_st = extra(st) if extra else {}
            before = {"act": [], "dve": []}
            n = {"act": 0, "dve": 0}
            for u in units:
                n[u["engine"]] += 1
                before[u["engine"]].append(n[u["engine"]])
                u["order"] = n[u["engine"]]
                if u.get("last", True):
                    w.done_at[w.index[u["key"]]] = base + len(before["act"]) + len(before["dve"])
            w.n_filled = base + len(units)
            with nc.Block() as block:
                self.weight_loads(block, name)

                @block.tensor
                def _(pe):
                    for i, u in enumerate(units):
                        if i >= BANKS:
                            old = units[i - BANKS]
                            pe.wait_ge(drained[old["engine"]], old["order"])
                        if u.get("first", True):
                            w.arrived(pe, u["key"])
                        bank = self.psum[:, i % BANKS, :]
                        for out, pairs in u["mms"](bank, w.view(u["key"])):
                            for j, (lhsT, rhs) in enumerate(pairs):
                                mm = nc.tensor.matmul(out, lhsT, rhs, start=(j == 0), stop=(j == len(pairs) - 1))
                        mm.then_inc(filled, 1)

                def drains(eng, who):
                    chain = Chain(eng, steps[who])
                    for i, u in enumerate(units):
                        if u["engine"] == who:
                            eng.wait_ge(filled, base + i + 1)
                            if u["order"] > 1:
                                eng.wait_ge(drained[who], u["order"] - 1)
                            u["drain"](eng, self.psum[:, i % BANKS, :], chain).then_inc(drained[who], 1)

                @block.scalar
                def _(act):
                    drains(act, "act")

                @block.vector
                def _(dve):
                    drains(dve, "dve")
    def load_constants(self):
        nc, d = self.nc, self.dram
        K = self.keep
        self.x = K("x_tokens", [P, TT, D])
        self.hT = K("h_features", [P, DC, S])
        self.ident = K("identity", [P, P])
        self.blockones = K("head_block_ones", [P, P])
        self.causal = K("causal_mask", [P, TT, S])
        self.strict = K("strict_mask", [P, TT, S])
        self.col = K("channel_columns", [P, NCOL])
        self.wsmall = K("lora_weights", [P, 3 * 512])
        self.c1 = K("c_silu", [P, DC])
        self.relb = K("rel_bias", [32, QH])
        self.bucket = K("bucket_onehot", [32, 2 * S])
        self.rwT = K("rwkv_out", [P, 4, S], layer=True)
        self.levels = K("level_masks", [C, 6, C], layer=True)
        self.pair = K("pair_masks", [C, 2, C], layer=True)
        self.restart = K("chunk_restart", [P, S], layer=True)
        self.rbias = K("router_bias", [P, NE], layer=True)
        with Stage(nc, "const") as st:
            rows = st.sbuf("param_rows", [NCOL, P])
            landed = st.sem("landed")
            turned = st.sem("turned")
            silu = st.sem("silu_done")
            loads = [
                (self.x[:], d["x"][0].rearrange("(t p) n -> p t n", p=P)),
                (self.c1[:], d["c"][0].rearrange("(p c) -> p c", p=P)),
                (self.ident[:], d["c_ident"]), (self.blockones[:], d["c_blockones"]),
                (self.causal[:], d["c_causal"]), (self.strict[:], d["c_strict"]),
                (self.levels[:], d["c_levels"]), (self.pair[:], d["c_pair"]), (self.restart[:], d["c_restart"]),
                (self.relb[:], d["rel_bias"]), (self.bucket[:], d["c_bucket"]),
                (self.rbias[:], d["router_bias"][0].partition_broadcast(P)),
                (self.wsmall[0:DH, 0:512], d["decay_up"][0]),
                (self.wsmall[DH:P, 512:1024], d["iclr_up"][0]),
                (self.wsmall[:, 1024:1536], d["gate_up"][0]),
            ]
            for name, n in COLS:
                src = d[name]
                src = src[0] if name != "r_k" else src[0].rearrange("h e -> (h e)")
                loads.append((rows[COL[name]:COL[name] + n, :], src.rearrange("(r p) -> r p", p=P)))
            with nc.Block() as block:
                self.weight_loads(block, "const")

                @block.scalar
                def _(act):
                    for dst, src in loads:
                        act.dma_start(dst, src).then_inc(landed, 16)
                    act.wait_ge(landed, 16 * len(loads))
                    nc.scalar.activation(self.c1[:], self.c1[:], ACT.Silu).then_inc(silu, 1)
                    act.wait_ge(silu, 1)

                @block.tensor
                def _(pe):
                    pe.wait_ge(landed, 16 * len(loads))
                    nc.tensor.transpose(self.psum[:, 0, 0:NCOL], rows[:, :], self.ident[0:NCOL, 0:NCOL]).then_inc(turned, 1)

                @block.vector
                def _(dve):
                    dve.wait_ge(turned, 1)
                    nc.vector.tensor_copy(self.col[:], self.psum[:, 0, 0:NCOL]).then_inc(turned, 1)
                    dve.wait_ge(turned, 2)

    def column(self, name, i=0, p0=0, p1=P):
        at = COL[name] + i
        return self.col[p0:p1, at:at + 1]

    def modulation(self, name, mod, c0, ncols):
        nc = self.nc
        with Stage(nc, name + "c") as st:
            cb = st.sbuf("c_repeated", [P, DC, P])
            made, landed = st.sem("made"), st.sem("bias_landed")
            with nc.Block() as block:
                @block.scalar
                def _(act):
                    act.dma_start(mod[:], self.dram["ada_b"][0, c0:c0 + ncols].partition_broadcast(P)).then_inc(landed, 16)
                    act.wait_ge(landed, 16)

                @block.vector
                def _(dve):
                    nc.vector.tensor_copy(cb[:], self.c1[:].unsqueeze(2).to_broadcast([P, DC, P])).then_inc(made, 1)
                    dve.wait_ge(made, 1)
            units = []
            for i in range(ncols // 256):
                def mms(bank, wv):
                    return [(bank[:, 0:256], [(cb[:, k, :], wv[:, k, :]) for k in range(DC)])]

                def drain(eng, bank, chain, i=i):
                    m = mod[:, i * 256:(i + 1) * 256]
                    return nc.vector.tensor_tensor(m, bank[:, 0:256], m, ALU.add)
                units.append(dict(key=(name, i), mms=mms, engine="dve", drain=drain))
            self.products(name, units)

    def norm(self, name, x, dst, gain_dram, modulate=None, out_dram=None, tokens=None):
        nc = self.nc
        with Stage(nc, name) as st:
            g = st.sbuf("gain", [P, D])
            y = st.sbuf("normed", [P, TT, D])
            done = tokens if tokens is not None else y
            stat = st.sbuf("stat", [P, 8])
            landed, stored = st.sem("gain_landed"), st.sem("stored")
            summed, rooted, ready, turned, drained = (st.sem(s) for s in ("summed", "rooted", "ready", "turned", "drained"))
            steps = st.sem("dve_steps")
            with nc.Block() as block:
                self.weight_loads(block, name)

                @block.scalar
                def _(act):
                    act.dma_start(g[:], gain_dram.partition_broadcast(P)).then_inc(landed, 16)
                    act.wait_ge(summed, 1)
                    nc.scalar.activation(stat[:, 2:4], stat[:, 0:2], ACT.Sqrt).then_inc(rooted, 1)
                    if out_dram is not None:
                        act.wait_ge(ready, 1)
                        act.dma_start(out_dram, y[:]).then_inc(stored, 16)
                        act.wait_ge(stored, 16)

                @block.vector
                def _(dve):
                    ch = Chain(dve, steps)
                    for t in range(TT):
                        ch.step(nc.vector.tensor_tensor_reduce(
                            out=y[:, t, :], in0=x[:, t, :], in1=x[:, t, :], scale=1.0, scalar=0.0,
                            op0=ALU.mult, op1=ALU.add, accum_out=stat[:, t:t + 1]))
                    nc.vector.tensor_scalar(stat[:, 0:2], stat[:, 0:2], 1.0 / D, 1e-6, ALU.mult, ALU.add).then_inc(summed, 1)
                    dve.wait_ge(rooted, 1)
                    ch.step(nc.vector.reciprocal(stat[:, 4:6], stat[:, 2:4]))
                    ch.step(nc.vector.tensor_tensor(stat[:, 6:8], stat[:, 4:6], stat[:, 4:6], ALU.mult))
                    ch.step(nc.vector.tensor_tensor(stat[:, 6:8], stat[:, 6:8], stat[:, 0:2], ALU.mult))
                    ch.step(nc.vector.tensor_scalar(stat[:, 6:8], stat[:, 6:8], -0.5, 1.5, ALU.mult, ALU.add))
                    ch.step(nc.vector.tensor_tensor(stat[:, 4:6], stat[:, 4:6], stat[:, 6:8], ALU.mult))
                    dve.wait_ge(landed, 16)
                    if modulate is not None:
                        ch.step(nc.vector.scalar_tensor_tensor(out=g[:], in0=modulate[1], scalar=1.0, in1=g[:],
                                                               op0=ALU.add, op1=ALU.mult))
                    for t in range(TT):
                        last = nc.vector.scalar_tensor_tensor(out=done[:, t, :], in0=x[:, t, :], scalar=stat[:, 4 + t:5 + t],
                                                              in1=g[:], op0=ALU.mult, op1=ALU.mult)
                        if modulate is not None:
                            ch.step(last)
                            last = nc.vector.tensor_tensor(y[:, t, :], y[:, t, :], modulate[0], ALU.add)
                        last.then_inc(ready, 1) if t == TT - 1 else ch.step(last)
                    dve.wait_ge(ready, 1)
                    if dst is not None:
                        for b in range(4):
                            dve.wait_ge(turned, b + 1)
                            nc.vector.tensor_copy(dst[:, 2 * b:2 * b + 2, :], self.psum[:, b, :].rearrange(
                                "p (c s) -> p c s", c=2)).then_inc(drained, 1)
                        dve.wait_ge(drained, 4)

                if dst is not None:
                    @block.tensor
                    def _(pe):
                        pe.wait_ge(ready, 1)
                        for b in range(4):
                            for c in range(2):
                                for t in range(TT):
                                    mm = nc.tensor.transpose(self.psum[:, b, c * S + t * P:c * S + (t + 1) * P],
                                                             y[:, t, bass.DynSlice(2 * b + c, P, DC)], self.ident[:, :])
                            mm.then_inc(turned, 1)

    def to_features(self, key, item_chunks, actT, nk, m0, dst, engine, first=True, last=True, func=None, cols=P):
        nc = self.nc

        def mms(bank, wv):
            return [(bank[0:cols, j * S:(j + 1) * S],
                     [(wv[:, k, m * cols:(m + 1) * cols], actT[:, k, :]) for k in range(nk)])
                    for j, m in enumerate(m0)]

        def drain(eng, bank, chain):
            src = bank[0:cols, 0:len(m0) * S].rearrange("p (c s) -> p c s", c=len(m0))
            if engine == "act":
                return nc.scalar.activation(dst, src, func or ACT.Copy)
            return nc.vector.tensor_copy(dst, src)
        return dict(key=key, mms=mms, engine=engine, drain=drain, first=first, last=last)

    def to_tokens(self, key, actT, nk, c0, ncols, dst, engine, first=True, last=True):
        nc = self.nc

        def mms(bank, wv):
            return [(bank[:, t * 256:t * 256 + ncols],
                     [(actT[:, k, t * P:(t + 1) * P], wv[:, k, c0:c0 + ncols]) for k in range(nk)])
                    for t in range(TT)]

        def drain(eng, bank, chain):
            src = bank.rearrange("p (t n) -> p t n", t=TT)[:, :, 0:ncols]
            if engine == "act":
                return nc.scalar.activation(dst, src, ACT.Copy)
            return nc.vector.tensor_copy(dst, src)
        return dict(key=key, mms=mms, engine=engine, drain=drain, first=first, last=last)

    def project_z(self):
        nc = self.nc
        L = lambda n, s: self.keep(n, s, layer=True)
        self.qT, self.kT, self.iqT = L("qT", [P, 4, S]), L("kT", [P, 4, S]), L("iqT", [P, 4, S])
        self.v, self.ikT, self.iw = L("v_tokens", [P, TT, 512]), L("ikT", [P, S]), L("iw", [P, TT, IH])
        self.ga, self.gr = L("gate_attn", [P, DC, S]), L("gate_rwkv", [P, DC, S])
        u = []
        for nm, dst in (("w_q", self.qT), ("w_k", self.kT)):
            for i in range(2):
                u.append(self.to_features((nm, i), 2, self.hT, DC, (0, 1), dst[:, 2 * i:2 * i + 2, :], ("act", "dve")[i]))
        for i in range(2):
            u.append(self.to_tokens(("w_v", i), self.hT, DC, 0, 256, self.v[:, :, i * 256:(i + 1) * 256], ("act", "dve")[i]))
        for i in range(2):
            u.append(self.to_features(("w_iq", i), 2, self.hT, DC, (0, 1), self.iqT[:, 2 * i:2 * i + 2, :], ("act", "dve")[i]))

        def mms_ik(bank, wv):
            return [(bank[32 * r:32 * r + 32, 0:S], [(wv[:, k, 0:ID], self.hT[:, k, :]) for k in range(DC)])
                    for r in range(4)]

        def drain_ik(eng, bank, chain):
            return nc.vector.tensor_copy(self.ikT[:, :], bank[:, 0:S])
        u.append(dict(key=("w_ikw", 0), mms=mms_ik, engine="dve", drain=drain_ik, last=False))
        u.append(self.to_tokens(("w_ikw", 0), self.hT, DC, ID, IH, self.iw[:, :, :], "dve", first=False))
        for nm, dst in (("w_ga", self.ga), ("w_gr", self.gr)):
            for i in range(4):
                u.append(self.to_features((nm, i), 2, self.hT, DC, (0, 1), dst[:, 2 * i:2 * i + 2, :], "act",
                                          func=ACT.Sigmoid))
        self.products("z", u)

    def rwkv(self):
        nc, col = self.nc, self.column
        with ExitStack() as keep:
            def T(name, shape):
                return keep.enter_context(nc.sbuf_tensor("rw_" + name, shape, F32))

            SC = [P, 4, S]
            gate, bonus, A, R, V, yT = (T(n, SC) for n in ("gate", "bonus", "A", "R", "V", "yT"))
            BK = T("BK", [P, 2, 4, S])
            B, K = BK[:, 0], BK[:, 1]
            odd = T("odd_heads", [DH, 4, 4, S])
            pend = T("chunk_decay", [P, 4, NC])
            pall = T("chunk_decay_heads", [DH, 4, 2, NC])
            self.rwkv_prepare(gate, bonus, A, B, K, R, V, odd, pend, pall)

            def half(i, h, t0, t1):
                src = (A, B, K, R)[i]
                return odd[:, (0, 2, 3, 1)[i], h // 2, t0:t1] if h % 2 else src[0:DH, h // 2, t0:t1]

            self.rwkv_chunks(half, B, K, V, BK, odd, pall, gate, bonus, yT)

    def rwkv_prepare(self, gate, bonus, A, B, K, R, V, odd, pend, pall):
        nc, col = self.nc, self.column
        SC = [P, 4, S]
        with ExitStack() as scope:
            z = scope.enter_context(nc.sbuf_tensor("zr", [P, 14, S + 1], F32))
            self.products("zr", [
                self.to_features(("w_zr", i), 2, self.hT, DC, (0, 1), z[:, 2 * i:2 * i + 2, 1:S + 1], ("act", "dve")[i % 2])
                for i in range(7)])
            with Stage(nc, "rwprep") as st:
                decay, iclr = st.sbuf("sig_decay", SC), st.sbuf("iclr", SC)
                cum, t1 = st.sbuf("cum", SC), st.sbuf("t1", SC)
                pp, pprev, pinv = st.sbuf("p", SC), st.sbuf("pprev", SC), st.sbuf("pinv", SC)
                steps, act_go, dve_go, pe_go = st.sem("dve_steps"), st.sem("act_to_dve"), st.sem("dve_to_act"), st.sem("pe_done")
                to_pe, act_steps, moved = st.sem("to_pe"), st.sem("act_steps"), st.sem("odd_moved")
                with nc.Block() as block:
                    self.weight_loads(block, "rwprep")

                    @block.vector
                    def _(dve):
                        ch = Chain(dve, steps)
                        v = nc.vector
                        ch.step(v.memset(z[:, :, 0:1], 0.0))
                        for c in (12, 13, 0, 1, 2, 3, 4, 5, 6, 7, 8, 9, 10, 11):
                            ch.step(v.tensor_tensor(t1[:, c % 4, :], z[:, c, 0:S], z[:, c, 1:S + 1], ALU.subtract))
                            dst = z[:, c, 1:S + 1]
                            last = v.scalar_tensor_tensor(out=dst, in0=t1[:, c % 4, :], scalar=col("tshift_mu", c),
                                                          in1=dst, op0=ALU.mult, op1=ALU.add)
                            last.then_inc(dve_go, 1) if c == 13 else ch.step(last)
                        r, k, vv = z[:, 0:4, 1:S + 1], z[:, 4:8, 1:S + 1], z[:, 8:12, 1:S + 1]
                        ch.step(v.tensor_copy(V[:], vv))
                        for c in range(4):
                            ch.step(v.tensor_scalar(A[:, c, :], z[:, 4 + c, 1:S + 1], col("k_k", c), None, ALU.mult))
                        v.tensor_tensor(t1[:], A[:], A[:], ALU.mult).then_inc(to_pe, 1)
                        dve.wait_ge(act_go, 2)
                        for c in range(4):
                            ch.step(v.tensor_tensor_scan(cum[:, c, :], self.restart[:], decay[:, c, :], 0.0, ALU.mult, ALU.add))
                        v.tensor_tensor(decay[:], cum[:], decay[:], ALU.subtract).then_inc(dve_go, 1)
                        for c in range(4):
                            ch.step(v.tensor_scalar(K[:, c, :], iclr[:, c, :], -1.0, None, ALU.add))
                            ch.step(v.tensor_scalar(K[:, c, :], K[:, c, :], col("k_a", c), 1.0, ALU.mult, ALU.add))
                        ch.step(v.tensor_tensor(K[:], K[:], k, ALU.mult))
                        dve.wait_ge(act_go, 3)
                        ch.step(v.tensor_scalar(t1[:], t1[:], 1e-12, None, ALU.max))
                        ch.step(v.reciprocal(t1[:], t1[:]))
                        ch.step(v.tensor_tensor(A[:], A[:], t1[:], ALU.mult))
                        ch.step(v.tensor_tensor(B[:], A[:], iclr[:], ALU.mult))
                        for c in range(4):
                            last = v.scalar_tensor_tensor(out=t1[:, c, :], in0=z[:, c, 1:S + 1], scalar=col("r_k", c),
                                                          in1=K[:, c, :], op0=ALU.mult, op1=ALU.mult)
                            last.then_inc(to_pe, 1) if c == 3 else ch.step(last)
                        dve.wait_ge(act_go, 6)
                        ch.step(v.scalar_tensor_tensor(out=A[:], in0=A[:], scalar=-1.0, in1=pprev[:], op0=ALU.mult, op1=ALU.mult))
                        ch.step(v.tensor_tensor(B[:], B[:], pinv[:], ALU.mult))
                        ch.step(v.tensor_tensor(K[:], K[:], pinv[:], ALU.mult))
                        ch.step(v.tensor_tensor(R[:], r, pp[:], ALU.mult))
                        ch.step(v.tensor_copy(pall[:, :, 0, :], pp[0:DH, :, C - 1:S:C]))
                        v.tensor_copy(pend[:], pp[:, :, C - 1:S:C]).then_inc(dve_go, 1)
                        dve.wait_ge(pe_go, 5)
                        for b in range(2):
                            last = v.tensor_tensor(bonus[:, 2 * b:2 * b + 2, :],
                                                   self.psum[:, 6 + b, :].rearrange("p (c s) -> p c s", c=2),
                                                   V[:, 2 * b:2 * b + 2, :], ALU.mult)
                            ch.step(last)

                    @block.tensor
                    def _(pe):
                        ps = self.psum

                        def lora(lo, hi, w0, src_chunk, b0, src=None):
                            for m in range(4):
                                rhs = z[lo:hi, src_chunk, 1:S + 1]
                                mm = nc.tensor.matmul(ps[:, b0 + m // 2, (m % 2) * S:(m % 2 + 1) * S],
                                                      self.wsmall[lo:hi, w0 + m * P:w0 + (m + 1) * P], rhs,
                                                      start=True, stop=True)
                            mm.then_inc(pe_go, 1)
                        pe.wait_ge(act_steps, 2)
                        lora(0, DH, 0, 12, 0)
                        lora(DH, P, 512, 12, 2)
                        lora(0, P, 1024, 13, 4)
                        pe.wait_ge(to_pe, 1)
                        for c in range(4):
                            mm = nc.tensor.matmul(ps[:, 6 + c // 2, (c % 2) * S:(c % 2 + 1) * S], self.blockones[:, :],
                                                  t1[:, c, :], start=True, stop=True)
                        mm.then_inc(pe_go, 1)
                        pe.wait_ge(to_pe, 2)
                        for c in range(4):
                            mm = nc.tensor.matmul(ps[:, 6 + c // 2, (c % 2) * S:(c % 2 + 1) * S], self.blockones[:, :],
                                                  t1[:, c, :], start=True, stop=True)
                        mm.then_inc(pe_go, 1)

                    @block.scalar
                    def _(act):
                        a = nc.scalar
                        chs = 0
                        act.wait_ge(dve_go, 1)
                        a.activation(z[0:DH, 12, 1:S + 1], z[0:DH, 12, 1:S + 1], ACT.Tanh).then_inc(act_steps, 1)
                        a.activation(z[:, 13, 1:S + 1], z[:, 13, 1:S + 1], ACT.Sigmoid).then_inc(act_steps, 1)
                        act.wait_ge(pe_go, 1)
                        for m in range(4):
                            i1 = a.activation(decay[:, m, :], self.psum[:, m // 2, (m % 2) * S:(m % 2 + 1) * S],
                                              ACT.Sigmoid, bias=col("decay_w0", m))
                        i1.then_inc(act_go, 1)
                        act.wait_ge(pe_go, 2)
                        for m in range(4):
                            i1 = a.activation(iclr[:, m, :], self.psum[:, 2 + m // 2, (m % 2) * S:(m % 2 + 1) * S],
                                              ACT.Sigmoid, bias=col("iclr_a0", m))
                        i1.then_inc(act_go, 1)
                        act.wait_ge(pe_go, 3)
                        for b in range(2):
                            a.activation(gate[:, 2 * b:2 * b + 2, :],
                                         self.psum[:, 4 + b, :].rearrange("p (c s) -> p c s", c=2), ACT.Copy)
                        act.wait_ge(pe_go, 4)
                        for b in range(2):
                            i1 = a.activation(t1[:, 2 * b:2 * b + 2, :],
                                              self.psum[:, 6 + b, :].rearrange("p (c s) -> p c s", c=2), ACT.Sqrt)
                        i1.then_inc(act_go, 1)
                        act.wait_ge(dve_go, 2)
                        a.activation(pprev[:], decay[:], ACT.Exp, scale=-DECAY).then_inc(act_go, 1)
                        a.activation(pinv[:], cum[:], ACT.Exp, scale=DECAY).then_inc(act_go, 1)
                        a.activation(pp[:], cum[:], ACT.Exp, scale=-DECAY).then_inc(act_go, 1)
                        act.wait_ge(dve_go, 3)
                        for i, src in enumerate((A, R, B, K)):
                            act.dma_start(odd[:, i, :, :], src[DH:P, :, :]).then_inc(moved, 16)
                        act.dma_start(pall[:, :, 1, :], pend[DH:P, :, :]).then_inc(moved, 16)
                        act.wait_ge(moved, 80)

    def rwkv_chunks(self, half, B, K, V, BK, odd, pall, gate, bonus, yT):
        nc = self.nc
        W = QH * DH
        with Stage(nc, "rwchunk") as st:
            tok = st.sbuf("tokens", [C, 3, NC, W])
            pairs = st.sbuf("pairs", [C, 4, NC, W])
            XT = st.sbuf("inverse_T", [C, NC, W])
            X = BK[0:C].rearrange("p i c s -> p (i c s)").rearrange("p (n w) -> p n w", n=NC)
            spare = odd[:, 2:4].rearrange("p i c s -> p (i c s)").rearrange("p (i n w) -> p i n w", i=2, n=2)
            t1, lm = spare[:, 0], spare[:, 1]
            ps = self.psum
            filled, act_done, steps = st.sem("filled"), st.sem("act_done"), st.sem("dve_steps")
            dve_done, lm_done, t1_done = st.sem("dve_done"), st.sem("level_done"), st.sem("t1_done")

            def H(ap, h):
                return ap[:, h * DH:(h + 1) * DH]

            jobs = [("tok", i, n) for i in range(3) for n in range(NC)] + [("pair", i, n) for n in range(NC) for i in range(4)]
            kinds = ((1, 0, 0), (2, 0, 0), (1, 3, 1), (2, 3, 1))
            with nc.Block() as block:
                self.weight_loads(block, "rwchunk1")

                @block.tensor
                def _(pe):
                    for j, (kind, i, n) in enumerate(jobs):
                        if j >= 8:
                            pe.wait_ge(dve_done, j - 7)
                        bank = ps[0:C, j % 8, :]
                        if kind == "tok":
                            for c in range(4):
                                mm = nc.tensor.transpose(bank[:, c * P:(c + 1) * P], (B, K, V)[i][:, c, n * C:(n + 1) * C],
                                                         self.ident[:, :])
                        else:
                            lt, rt, _ = kinds[i]
                            for h in range(QH):
                                mm = nc.tensor.matmul(H(bank, h), half(lt, h, n * C, (n + 1) * C),
                                                      half(rt, h, n * C, (n + 1) * C), start=True, stop=True)
                        mm.then_inc(filled, 1)

                @block.vector
                def _(dve):
                    for j, (kind, i, n) in enumerate(jobs):
                        dve.wait_ge(filled, j + 1)
                        bank = ps[0:C, j % 8, :]
                        if kind == "tok":
                            nc.vector.tensor_copy(tok[:, i, n, :], bank).then_inc(dve_done, 1)
                        else:
                            m = self.pair[:, kinds[i][2], :].unsqueeze(1).to_broadcast([C, QH, C])
                            nc.vector.tensor_tensor(pairs[:, i, n, :].rearrange("p (h c) -> p h c", h=QH),
                                                    bank.rearrange("p (h c) -> p h c", h=QH), m, ALU.mult).then_inc(dve_done, 1)
                    eye = self.ident[0:C, 0:C].unsqueeze(1).to_broadcast([C, NC * QH, C])
                    for buf in (X, XT[:]):
                        nc.vector.tensor_copy(buf.rearrange("p n (h c) -> p (n h) c", h=QH), eye).then_inc(dve_done, 1)
                    dve.wait_ge(dve_done, len(jobs) + 2)

            LEV = 6
            filled2, xdone = st.sem("filled_inv"), st.sem("x_done")
            with nc.Block() as block:
                self.weight_loads(block, "rwchunk2")

                @block.vector
                def _(dve):
                    def level(r):
                        if r >= 2:
                            dve.wait_ge(filled2, 3 * (r - 2) + 1)
                        m = self.levels[:, r // NC, :].unsqueeze(1).to_broadcast([C, QH, C])
                        nc.vector.tensor_tensor(lm[:, r % 2, :].rearrange("p (h c) -> p h c", h=QH),
                                                pairs[:, 0, r % NC, :].rearrange("p (h c) -> p h c", h=QH), m,
                                                ALU.mult).then_inc(lm_done, 1)

                    level(0)
                    for r in range(LEV * NC):
                        n = r % NC
                        if r + 1 < LEV * NC:
                            level(r + 1)
                        dve.wait_ge(filled2, 3 * r + 3)
                        nc.vector.tensor_tensor(X[:, n, :], X[:, n, :], ps[0:C, 2 + r % 2 * 3, :], ALU.add).then_inc(xdone, 1)
                        nc.vector.tensor_tensor(XT[:, n, :], XT[:, n, :], ps[0:C, 3 + r % 2 * 3, :], ALU.add).then_inc(xdone, 1)
                    dve.wait_ge(xdone, 2 * LEV * NC)

                @block.scalar
                def _(act):
                    for r in range(LEV * NC):
                        act.wait_ge(filled2, 3 * r + 1)
                        if r >= 2:
                            act.wait_ge(filled2, 3 * (r - 2) + 3)
                        nc.scalar.activation(t1[:, r % 2, :], ps[0:C, 1 + r % 2 * 3, :], ACT.Copy).then_inc(t1_done, 1)

                @block.tensor
                def _(pe):
                    for r in range(LEV * NC):
                        n, b = r % NC, 1 + r % 2 * 3
                        pe.wait_ge(lm_done, r + 1)
                        if r >= NC:
                            pe.wait_ge(xdone, 2 * (r - NC) + 2)
                        for h in range(QH):
                            mm = nc.tensor.matmul(H(ps[0:C, b, :], h), H(lm[:, r % 2, :], h), H(X[:, n, :], h), start=True, stop=True)
                        mm.then_inc(filled2, 1)
                        pe.wait_ge(t1_done, r + 1)
                        if r >= 2:
                            pe.wait_ge(xdone, 2 * (r - 2) + 2)
                        for h in range(QH):
                            mm = nc.tensor.matmul(H(ps[0:C, b + 1, :], h), H(XT[:, n, :], h), H(t1[:, r % 2, :], h), start=True, stop=True)
                        mm.then_inc(filled2, 1)
                        for h in range(QH):
                            mm = nc.tensor.matmul(H(ps[0:C, b + 2, :], h), H(t1[:, r % 2, :], h), H(XT[:, n, :], h), start=True, stop=True)
                        mm.then_inc(filled2, 1)

            with Stage(nc, "rwseq") as s2:
                state, rhs, sa = s2.sbuf("state", [DH, W]), s2.sbuf("rhs", [C, W]), s2.sbuf("sa", [C, W])
                Y = s2.sbuf("y", [DH, 2, W])
                pe_done, dve_d, act_d = s2.sem("pe_done"), s2.sem("dve_done"), s2.sem("act_done")
                moved = [s2.sem("even_chunks_moved"), s2.sem("odd_chunks_moved")]
                with nc.Block() as block:
                    self.weight_loads(block, "rwseq")

                    @block.tensor
                    def _(pe):
                        for n in range(NC):
                            t0, t1_ = n * C, (n + 1) * C
                            pe.wait_ge(dve_d, 4 * n + 1)
                            for h in range(QH):
                                nc.tensor.matmul(H(ps[0:C, 0, :], h), half(0, h, t0, t1_), H(state[:], h), start=True, stop=False)
                                mm = nc.tensor.matmul(H(ps[0:C, 0, :], h), H(pairs[:, 1, n, :], h), H(tok[:, 2, n, :], h),
                                                      start=False, stop=True)
                            mm.then_inc(pe_done, 1)
                            pe.wait_ge(dve_d, 4 * n + 2)
                            for h in range(QH):
                                mm = nc.tensor.matmul(H(ps[0:C, 1, :], h), H(XT[:, n, :], h), H(rhs[:], h), start=True, stop=True)
                            mm.then_inc(pe_done, 1)
                            pe.wait_ge(dve_d, 4 * n + 3)
                            for h in range(QH):
                                nc.tensor.matmul(H(ps[0:C, 2, :], h), H(tok[:, 0, n, :], h), H(sa[:], h), start=True, stop=False)
                                mm = nc.tensor.matmul(H(ps[0:C, 2, :], h), H(tok[:, 1, n, :], h), H(tok[:, 2, n, :], h),
                                                      start=False, stop=True)
                            mm.then_inc(pe_done, 1)
                            if n:
                                pe.wait_ge(act_d, n)
                            for h in range(QH):
                                o = H(ps[0:C, 3, :], h)
                                nc.tensor.matmul(o, H(state[:], h), half(3, h, t0, t1_), start=True, stop=False)
                                nc.tensor.matmul(o, H(sa[:], h), H(pairs[:, 2, n, :], h), start=False, stop=False)
                                mm = nc.tensor.matmul(o, H(tok[:, 2, n, :], h), H(pairs[:, 3, n, :], h), start=False, stop=True)
                            mm.then_inc(pe_done, 1)

                    @block.vector
                    def _(dve):
                        v = nc.vector
                        v.memset(state[:], 0.0).then_inc(dve_d, 1)
                        for n in range(NC):
                            dve.wait_ge(pe_done, 4 * n + 1)
                            v.tensor_copy(rhs[:], ps[0:C, 0, :]).then_inc(dve_d, 1)
                            dve.wait_ge(pe_done, 4 * n + 2)
                            v.tensor_copy(sa[:], ps[0:C, 1, :]).then_inc(dve_d, 1)
                            dve.wait_ge(pe_done, 4 * n + 4)
                            v.tensor_tensor(state[:], state[:], ps[0:C, 2, :], ALU.add).then_inc(dve_d, 1)
                            dve.wait_ge(dve_d, 4 * n + 4)
                            sv = state[:].rearrange("p (h e) -> p h e", h=QH)
                            v.tensor_tensor(sv, sv, pall[:, :, :, n:n + 1].rearrange("p c two n -> p (c two) n").to_broadcast(
                                [DH, QH, DH]), ALU.mult).then_inc(dve_d, 1)

                    @block.scalar
                    def _(act):
                        for n in range(NC):
                            act.wait_ge(pe_done, 4 * n + 4)
                            if n >= 2:
                                act.wait_ge(moved[n % 2], 32 * (n // 2))
                            nc.scalar.activation(Y[:, n % 2, :], ps[0:C, 3, :], ACT.Copy).then_inc(act_d, 1)
                            act.wait_ge(act_d, n + 1)
                            yv = Y[:, n % 2, :].rearrange("p (c two s) -> p c two s", two=2, s=C)
                            act.dma_start(yT[0:DH, :, n * C:(n + 1) * C], yv[:, :, 0, :]).then_inc(moved[n % 2], 16)
                            act.dma_start(yT[DH:P, :, n * C:(n + 1) * C], yv[:, :, 1, :]).then_inc(moved[n % 2], 16)
                        act.wait_ge(moved[0], 16 * NC)
                        act.wait_ge(moved[1], 16 * NC)

        with Stage(nc, "rwgn") as s2:
            mean, sq = s2.sbuf("mean", [P, 4, S]), s2.sbuf("sq", [P, 4, S])
            ps = self.psum
            with nc.Block() as block:
                self.weight_loads(block, "rwnorm")
                pe2, dve2, act2, st2 = s2.sem("pe2"), s2.sem("dve2"), s2.sem("act2"), s2.sem("steps2")

                @block.tensor
                def _(pe):
                    for c in range(4):
                        mm = nc.tensor.matmul(ps[:, c // 2, (c % 2) * S:(c % 2 + 1) * S], self.blockones[:, :], yT[:, c, :],
                                              start=True, stop=True)
                    mm.then_inc(pe2, 1)
                    pe.wait_ge(dve2, 1)
                    for c in range(4):
                        mm = nc.tensor.matmul(ps[:, 2 + c // 2, (c % 2) * S:(c % 2 + 1) * S], self.blockones[:, :], sq[:, c, :],
                                              start=True, stop=True)
                    mm.then_inc(pe2, 1)

                @block.vector
                def _(dve):
                    v, ch = nc.vector, Chain(dve, st2)
                    dve.wait_ge(pe2, 1)
                    for b in range(2):
                        ch.step(v.scalar_tensor_tensor(out=yT[:, 2 * b:2 * b + 2, :].rearrange("p c s -> p (c s)"),
                                                       in0=ps[:, b, :], scalar=-1.0 / DH,
                                                       in1=yT[:, 2 * b:2 * b + 2, :].rearrange("p c s -> p (c s)"),
                                                       op0=ALU.mult, op1=ALU.add))
                    v.tensor_tensor(sq[:], yT[:], yT[:], ALU.mult).then_inc(dve2, 1)
                    dve.wait_ge(pe2, 2)
                    for b in range(2):
                        last = v.tensor_scalar(mean[:, 2 * b:2 * b + 2, :].rearrange("p c s -> p (c s)"), ps[:, 2 + b, :],
                                               1.0 / DH, 64e-5, ALU.mult, ALU.add)
                        ch.step(last) if b == 0 else last.then_inc(dve2, 1)
                    dve.wait_ge(act2, 1)
                    ch.step(v.reciprocal(mean[:], mean[:]))
                    ch.step(v.tensor_tensor(yT[:], yT[:], mean[:], ALU.mult))
                    for c in range(4):
                        ch.step(v.tensor_scalar(yT[:, c, :], yT[:, c, :], self.column("lnx_g", c), self.column("lnx_b", c),
                                                ALU.mult, ALU.add))
                    ch.step(v.tensor_tensor(yT[:], yT[:], bonus[:], ALU.add))
                    ch.step(v.tensor_tensor(self.rwT[:], yT[:], gate[:], ALU.mult))

                @block.scalar
                def _(act):
                    act.wait_ge(dve2, 2)
                    nc.scalar.activation(mean[:], mean[:], ACT.Sqrt).then_inc(act2, 1)

    def attend(self, name, units, scale, ns=1, neg_lam=None):
        nc, ps = self.nc, self.psum
        n = len(units)
        with Stage(nc, name) as st:
            logit = st.sbuf("logits", [P, 2, ns * TT, S])
            prob = st.sbuf("probs", [P, 2, ns * TT, S])
            pT = st.sbuf("probs_T", [P, 2, TT, S])
            nmax, rsum, rinv = (st.sbuf(x, [P, 2, ns * TT]) for x in ("neg_max", "row_sum", "row_inv"))
            scored, maxed, exped, normed, turned, copied, valued, stored = (st.sem(x) for x in (
                "scored", "maxed", "exped", "normed", "turned", "copied", "valued", "stored"))
            steps = st.sem("dve_steps")
            with nc.Block() as block:
                self.weight_loads(block, name)

                @block.tensor
                def _(pe):
                    for i in range(n + 2):
                        if i < n:
                            if i >= 2:
                                pe.wait_ge(maxed, i - 1)
                            for out, pairs in units[i]["scores"]([ps[:, (i % 2) * ns + s, :] for s in range(ns)]):
                                for j, (a, b) in enumerate(pairs):
                                    mm = nc.tensor.matmul(out, a, b, start=(j == 0), stop=(j == len(pairs) - 1))
                            mm.then_inc(scored, 1)
                        if 1 <= i <= n:
                            u = i - 1
                            pe.wait_ge(normed, u + 1)
                            if u >= 2:
                                pe.wait_ge(copied, u - 1)
                            for kt in range(TT):
                                for t in range(TT):
                                    mm = nc.tensor.transpose(ps[:, 4 + u % 2, kt * S + t * P:kt * S + (t + 1) * P],
                                                             prob[:, u % 2, t, kt * P:(kt + 1) * P], self.ident[:, :])
                            mm.then_inc(turned, 1)
                        if i >= 2:
                            u = i - 2
                            pe.wait_ge(copied, u + 1)
                            if u >= 2:
                                pe.wait_ge(stored, u - 1)
                            for out, pairs in units[u]["values"](ps[:, 6 + u % 2, :], pT[:, u % 2]):
                                for j, (a, b) in enumerate(pairs):
                                    mm = nc.tensor.matmul(out, a, b, start=(j == 0), stop=(j == len(pairs) - 1))
                            mm.then_inc(valued, 1)

                @block.vector
                def _(dve):
                    v, ch = nc.vector, Chain(dve, steps)
                    for i in range(n + 2):
                        if i < n:
                            b = i % 2
                            dve.wait_ge(scored, i + 1)
                            if i >= 2:
                                dve.wait_ge(exped, i - 1)
                            for s in range(ns):
                                src = ps[:, b * ns + s, :].rearrange("p (t k) -> p t k", t=TT)
                                dst = logit[:, b, s * TT:(s + 1) * TT, :]
                                if units[i]["bias"] is None:
                                    ch.step(v.tensor_scalar(dst, src, scale, None, ALU.mult))
                                else:
                                    ch.step(v.scalar_tensor_tensor(out=dst, in0=src, scalar=scale, in1=units[i]["bias"],
                                                                   op0=ALU.mult, op1=ALU.add))
                            v.tensor_reduce(nmax[:, b, :], logit[:, b, :, :], AX.X, ALU.max, negate=True).then_inc(maxed, 1)
                        if 1 <= i <= n:
                            u = i - 1
                            b = u % 2
                            dve.wait_ge(exped, u + 1)
                            ch.step(v.reciprocal(rinv[:, b, :], rsum[:, b, :]))
                            inv = rinv[:, b, :].unsqueeze(2).to_broadcast([P, ns * TT, S])
                            last = v.tensor_tensor(prob[:, b], prob[:, b], inv, ALU.mult)
                            if ns == 2:
                                ch.step(last)
                                last = v.scalar_tensor_tensor(out=prob[:, b, 0:TT, :], in0=prob[:, b, TT:, :], scalar=neg_lam,
                                                              in1=prob[:, b, 0:TT, :], op0=ALU.mult, op1=ALU.add)
                            last.then_inc(normed, 1)
                        if i >= 2:
                            u = i - 2
                            dve.wait_ge(valued, u + 1)
                            dst, src = units[u]["result"](ps[:, 6 + u % 2, :])
                            v.tensor_copy(dst, src).then_inc(stored, 1)
                    dve.wait_ge(stored, n)

                @block.scalar
                def _(act):
                    for i in range(n + 1):
                        if i < n:
                            b = i % 2
                            act.wait_ge(maxed, i + 1)
                            if i >= 2:
                                act.wait_ge(turned, i - 1)
                            for t in range(ns * TT):
                                last = nc.scalar.activation(prob[:, b, t, :], logit[:, b, t, :], ACT.Exp,
                                                            bias=nmax[:, b, t:t + 1], accum_out=rsum[:, b, t:t + 1])
                            last.then_inc(exped, 1)
                        if i >= 1:
                            u = i - 1
                            act.wait_ge(turned, u + 1)
                            if u >= 2:
                                act.wait_ge(valued, u - 1)
                            nc.scalar.activation(pT[:, u % 2].rearrange("p k q -> p (k q)"), ps[:, 4 + u % 2, :],
                                                 ACT.Copy).then_inc(copied, 1)

    def sparse_attention(self):
        nc, ps = self.nc, self.psum
        L = lambda n, s: self.keep(n, s, layer=True)
        self.attnT = L("attn_out", [P, 4, S])
        rows = nc.dram_tensor("bias_rows", [QH, 2 * S], F32).ap()
        with Stage(nc, "dsa_keep") as keep:
            bias = keep.sbuf("bias", [P, QH, TT, S])
            with Stage(nc, "dsa") as st:
                rw = st.sbuf("weighted", [P, IH, S])
                shifted = st.sbuf("shifted_bias", [P, QH, TT, S])
                work, msk = st.sbuf("work", [P, TT, S]), st.sbuf("outside", [P, TT, S])
                best = st.sbuf("best", [P, TT, 8])
                brow = st.sbuf("bias_row", [QH, 2 * S])
                vals, vout, stored, landed = st.sem("bias_values"), st.sem("bias_out"), st.sem("stored"), st.sem("landed")
                dots, drained, steps = st.sem("dots"), st.sem("drained"), st.sem("steps")
                with nc.Block() as block:
                    self.weight_loads(block, "dsa")

                    @block.tensor
                    def _(pe):
                        nc.tensor.matmul(ps[0:QH, 0, :], self.relb[:, :], self.bucket[:, :], start=True, stop=True).then_inc(vals, 1)
                        pe.wait_ge(vout, 1)
                        for t in range(TT):
                            for b in range(8):
                                r, qd = b // 4, b % 4
                                if t:
                                    pe.wait_ge(drained, b + 1)
                                for j in range(2):
                                    lo = 32 * qd
                                    mm = nc.tensor.matmul(ps[:, b, j * S:(j + 1) * S],
                                                          self.iqT[lo:lo + 32, 2 * r + j, t * P:(t + 1) * P],
                                                          self.ikT[lo:lo + 32, :], start=True, stop=True)
                                mm.then_inc(dots, 1)

                    @block.scalar
                    def _(act):
                        act.wait_ge(vout, 1)
                        act.dma_start(rows, brow[:]).then_inc(stored, 16)
                        act.wait_ge(stored, 16)
                        for h in range(QH):
                            src = bass.AP(tensor=rows.tensor, offset=h * 2 * S, ap=[[1, P], [P, TT], [1, S]])
                            act.dma_start(shifted[:, h], src).then_inc(landed, 16)
                        act.wait_ge(landed, 16 * QH)

                    @block.vector
                    def _(dve):
                        v, ch = nc.vector, Chain(dve, steps)
                        dve.wait_ge(vals, 1)
                        v.tensor_copy(brow[:], ps[0:QH, 0, :]).then_inc(vout, 1)
                        ch.step(v.tensor_scalar(msk[:], self.causal[:], -1.0, BIG, ALU.add, ALU.mult))
                        for t in range(TT):
                            for b in range(8):
                                r, qd = b // 4, b % 4
                                dve.wait_ge(dots, 8 * t + b + 1)
                                h0 = qd + 8 * r
                                w = self.iw[:, t, h0:h0 + 5:4].unsqueeze(2).to_broadcast([P, 2, S])
                                v.scalar_tensor_tensor(out=rw[:, h0:h0 + 5:4, :], in0=ps[:, b, :].rearrange("p (j s) -> p j s", j=2),
                                                       scalar=0.0, in1=w, op0=ALU.max, op1=ALU.mult).then_inc(drained, 1)
                            dve.wait_ge(drained, 8 * t + 8)
                            ch.step(v.tensor_reduce(work[:, t, :], rw[:].rearrange("p h s -> p s h"), AX.X, ALU.add))
                        ch.step(v.scalar_tensor_tensor(out=work[:], in0=work[:], scalar=IH ** -0.5 * ID ** -0.5,
                                                       in1=self.causal[:], op0=ALU.mult, op1=ALU.mult))
                        ch.step(v.tensor_tensor(work[:], work[:], msk[:], ALU.add))
                        for _ in range(TOPK // 8):
                            for t in range(TT):
                                ch.step(v.max(best[:, t, :], work[:, t, :]))
                                ch.step(v.match_replace(work[:, t, :], best[:, t, :], work[:, t, :], TAKEN))
                        ch.step(v.scalar_tensor_tensor(out=work[:], in0=work[:], scalar=TAKEN / 1.5, in1=self.causal[:],
                                                       op0=ALU.is_lt, op1=ALU.mult))
                        ch.step(v.tensor_scalar(work[:], work[:], -1.0, BIG, ALU.add, ALU.mult))
                        dve.wait_ge(landed, 16 * QH)
                        for h in range(QH):
                            ch.step(v.tensor_tensor(bias[:, h], shifted[:, h, :, ::-1], work[:], ALU.add))
            units = []
            for h in range(QH):
                lo = DH * (h % 2)
                units.append(dict(
                    scores=lambda banks, h=h, lo=lo: [
                        (banks[0][:, t * S:(t + 1) * S],
                         [(self.qT[lo:lo + DH, h // 2, t * P:(t + 1) * P], self.kT[lo:lo + DH, h // 2, :])]) for t in range(TT)],
                    bias=bias[:, h],
                    values=lambda bank, pT, h=h, lo=lo: [
                        (bank[lo:lo + DH, 0:S], [(self.v[:, kt, h * DH:(h + 1) * DH], pT[:, kt, :]) for kt in range(TT)])],
                    result=lambda bank, h=h, lo=lo: (self.attnT[lo:lo + DH, h // 2, :], bank[lo:lo + DH, 0:S])))
            self.attend("dsa_heads", units, DH ** -0.5)

    def mix_and_project(self):
        nc = self.nc
        units = []
        with Stage(nc, "mixtmp") as st:
            tmp = st.sbuf("tmp", [P, 512])
            for src, gate, key in ((self.attnT, self.ga, "w_attn_br"), (self.rwT, self.gr, "w_rwkv_br")):
                for i in range(2):
                    for j in range(2):
                        m = 4 * i + 2 * j

                        def drain(eng, bank, chain, m=m, gate=gate, key=key):
                            b = bank.rearrange("p (c s) -> p c s", c=2)
                            t = tmp[:].rearrange("p (c s) -> p c s", c=2)
                            if key == "w_attn_br":
                                return nc.vector.tensor_tensor(self.hT[:, m:m + 2, :], b, gate[:, m:m + 2, :], ALU.mult)
                            chain.step(nc.vector.tensor_tensor(t, b, gate[:, m:m + 2, :], ALU.mult))
                            return nc.vector.tensor_tensor(self.hT[:, m:m + 2, :], self.hT[:, m:m + 2, :], t, ALU.add)
                        u = self.to_features((key, i), 4, src, 4, (2 * j, 2 * j + 1), None, "dve", first=(j == 0), last=(j == 1))
                        u["drain"] = drain
                        units.append(u)
            self.products("mix", units)
        self.residual("out", "w_out", self.hT, DC, 0, gate=self.mod_row(0))

    def residual(self, name, key, srcT, nk, c0, gate=None):
        nc = self.nc
        with Stage(nc, name + "tmp") as st:
            tmp = st.sbuf("tmp", [P, TT, 256])
            units = []
            for i in range(4):
                u = self.to_tokens((key, i), srcT, nk, 0, 256, None, "dve")

                def drain(eng, bank, chain, i=i):
                    b = bank.rearrange("p (t n) -> p t n", t=TT)
                    x = self.x[:, :, i * 256:(i + 1) * 256]
                    if gate is None:
                        return nc.vector.tensor_tensor(x, x, b, ALU.add)
                    g = gate[:, i * 256:(i + 1) * 256].unsqueeze(1).to_broadcast([P, TT, 256])
                    chain.step(nc.vector.tensor_tensor(tmp[:], b, g, ALU.mult))
                    return nc.vector.tensor_tensor(x, x, tmp[:], ALU.add)
                u["drain"] = drain
                units.append(u)
            self.products(name, units)

    def route(self):
        nc, ps = self.nc, self.psum
        NG, EG = 8, NE // 8
        self.comb = nc.dram_tensor("combine_rows", [NE, S], F32).ap()
        with Stage(nc, "route") as st:
            score, choice = st.sbuf("score", [P, TT, NE]), st.sbuf("choice", [P, TT, NE])
            sel = st.sbuf("selected", [P, TT, NE])
            top = st.sbuf("group_top", [P, TT, NG, 8])
            cand, best, repl = st.sbuf("cand", [P, TT, 16]), st.sbuf("best", [P, TT, 8]), st.sbuf("repl", [P, TT, 8])
            gsel, tot = st.sbuf("group_sel", [P, TT, NG]), st.sbuf("total", [P, TT])
            combT = st.sbuf("combT", [NE, S])
            u = self.to_tokens(("router_w", 0), self.hT, DC, 0, NE, score[:], "act")
            u["drain"] = lambda eng, bank, chain: nc.scalar.activation(
                score[:], bank.rearrange("p (t n) -> p t n", t=TT)[:, :, 0:NE], ACT.Sigmoid)
            self.products("router", [u])
            steps, ready, turned, copied, stored = (st.sem(x) for x in ("steps", "ready", "turned", "copied", "stored"))
            with nc.Block() as block:
                self.weight_loads(block, "route")

                @block.vector
                def _(dve):
                    v, ch = nc.vector, Chain(dve, steps)
                    ch.step(v.tensor_tensor(choice[:], score[:], self.rbias[:].unsqueeze(1).to_broadcast([P, TT, NE]), ALU.add))
                    ch.step(v.memset(cand[:], -BIG))
                    ch.step(v.memset(repl[:], -BIG))
                    for t in range(TT):
                        for g in range(NG):
                            ch.step(v.max(top[:, t, g, :], choice[:, t, g * EG:(g + 1) * EG]))
                    ch.step(v.tensor_tensor(cand[:, :, 0:NG], top[:, :, :, 0], top[:, :, :, 1], ALU.add))
                    for t in range(TT):
                        ch.step(v.max(best[:, t, :], cand[:, t, 0:NG]))
                    ch.step(v.tensor_copy(repl[:, :, 0:4], best[:, :, 0:4]))
                    for t in range(TT):
                        ch.step(v.match_replace(cand[:, t, :], repl[:, t, :], cand[:, t, :], TAKEN))
                    ch.step(v.tensor_scalar(gsel[:], cand[:, :, 0:NG], TAKEN / 1.5, None, ALU.is_lt))
                    gb = gsel[:].rearrange("p t g -> p (t g)").unsqueeze(2).to_broadcast([P, TT * NG, EG])
                    c3 = choice[:].rearrange("p t (g e) -> p (t g) e", e=EG)
                    s3 = sel[:].rearrange("p t (g e) -> p (t g) e", e=EG)
                    ch.step(v.tensor_tensor(c3, c3, gb, ALU.mult))
                    ch.step(v.tensor_scalar(gsel[:], gsel[:], -1.0, BIG, ALU.add, ALU.mult))
                    ch.step(v.tensor_tensor(c3, c3, gb, ALU.add))
                    for t in range(TT):
                        ch.step(v.max(best[:, t, :], choice[:, t, :]))
                        ch.step(v.match_replace(sel[:, t, :], best[:, t, :], choice[:, t, :], TAKEN))
                    ch.step(v.scalar_tensor_tensor(out=sel[:], in0=sel[:], scalar=TAKEN / 1.5, in1=score[:],
                                                   op0=ALU.is_lt, op1=ALU.mult))
                    ch.step(v.tensor_reduce(tot[:], sel[:], AX.X, ALU.add))
                    ch.step(v.reciprocal(tot[:], tot[:]))
                    ch.step(v.tensor_scalar(tot[:], tot[:], 2.5, None, ALU.mult))
                    v.tensor_tensor(sel[:], sel[:], tot[:].unsqueeze(2).to_broadcast([P, TT, NE]), ALU.mult).then_inc(ready, 1)
                    dve.wait_ge(turned, 1)
                    v.tensor_copy(combT[:], ps[0:NE, 0, 0:S]).then_inc(copied, 1)

                @block.tensor
                def _(pe):
                    pe.wait_ge(ready, 1)
                    for t in range(TT):
                        mm = nc.tensor.transpose(ps[0:NE, 0, t * P:(t + 1) * P], sel[:, t, :], self.ident[:, :])
                    mm.then_inc(turned, 1)

                @block.scalar
                def _(act):
                    act.wait_ge(copied, 1)
                    act.dma_start(self.comb, combT[:]).then_inc(stored, 16)
                    act.wait_ge(stored, 16)

    def experts(self):
        nc, ps, w, d = self.nc, self.psum, self.w, self.dram
        n0, base = w.index[("sh_gate", 0)], w.n_filled
        G = NE // 2
        for i in range(2 + 3 * NE + 1):
            w.done_at[n0 + i] = base + i + 1
        w.n_filled = base + 3 * NE + 3
        after = n0 + 3 * NE + 3
        down_of = lambda t, e: t[e].rearrange("(c p) n -> p c n", p=P)
        rows_of = lambda t, e: t[e].rearrange("(p c) n -> p c n", p=P)
        with Stage(nc, "moe") as st:
            silu, hid, cb = st.sbuf("silu", [P, 2, EC, S]), st.sbuf("hidden", [P, 2, EC, S]), st.sbuf("combine", [P, 2, S])
            tmp = st.sbuf("tmp", [P, D])
            silu_done, h_done, steps = st.sem("silu_done"), st.sem("hidden_done"), st.sem("dve_steps")
            cb_landed = [st.sem("combine_landed_even"), st.sem("combine_landed_odd")]
            y = [[ps[:, 4 + 2 * t + half, :] for half in range(2)] for t in range(TT)]

            def slot(n, chunks):
                return w.slots[:, n % RING, :].rearrange("p (c n) -> p c n", c=chunks)

            with nc.Block() as block:
                @block.sync
                def _(sp):
                    first_free = n0 + RING
                    while w.issued < first_free:
                        w.load(sp, w.issued)
                        w.issued += 1
                    def combine(e, par, free):
                        if free is not None:
                            sp.wait_ge(h_done, free)
                        sp.dma_start(cb[:, par, :], self.comb[e].partition_broadcast(P)).then_inc(cb_landed[par], 16)

                    def turn(g, first=False):
                        for q in range(RING):
                            n = first_free + q
                            e_off, j = divmod(n - n0 - 2, 3)
                            sp.wait_ge(w.filled, 6 * g + w.done_at[n - RING])
                            src = ((rows_of, "exp_gate", 0), (rows_of, "exp_up", 0), (down_of, "exp_down", -1))[j]
                            sp.dma_start(slot(n, 2 if j == 2 else 8),
                                         src[0](d[src[1]][0], 2 * g + e_off + src[2])).then_inc(w.landed[n % RING], 16)
                            if j == 1:
                                combine(2 * g + e_off, e_off % 2, None if first and e_off == 1 else 2 * g + e_off)
                    combine(0, 0, None)
                    turn(0, first=True)
                    with sp.Fori(1, G - 1) as g:
                        turn(g)
                    w.issued = first_free + RING * (G - 1)
                    while w.issued < len(w.items) and w.issued - RING < after:
                        w.load(sp, w.issued)
                        if w.issued == n0 + 2 + 3 * (NE - 1) + 1:
                            combine(NE - 1, 1, NE - 1)
                        w.issued += 1

                def pe_up(n, b, landed_turn):
                    for j in range(2):
                        nc.tensor.wait_ge(w.landed[(n + j) % RING], landed_turn(n + j))
                        wv = slot(n + j, DC)
                        for m in range(EC):
                            for k in range(DC):
                                mm = nc.tensor.matmul(ps[:, 2 * b + j, m * S:(m + 1) * S], wv[:, k, m * P:(m + 1) * P],
                                                      self.hT[:, k, :], start=(k == 0), stop=(k == DC - 1))
                        mm.then_inc(w.filled, 1)

                def pe_down(n, b, landed_turn, unit_done, first=False, last=False):
                    nc.tensor.wait_ge(w.landed[n % RING], landed_turn(n))
                    nc.tensor.wait_ge(h_done, unit_done)
                    wv = slot(n, EC)
                    for t in range(TT):
                        for k in range(EC):
                            for half in range(2):
                                mm = nc.tensor.matmul(y[t][half], hid[:, b, k, t * P:(t + 1) * P],
                                                      wv[:, k, half * 512:(half + 1) * 512], start=(first and k == 0),
                                                      stop=(last and k == EC - 1), skip_group_check=True)
                    mm.then_inc(w.filled, 1)

                @block.tensor
                def _(pe):
                    at = lambda g: (lambda n: 16 * (g + n // RING + 1))
                    pe_up(n0, 0, at(0))

                    def turn(g, first=False):
                        n = n0 + 2
                        pe_up(n, 1, at(g))
                        pe_down(n + 2, 0, at(g), 2 * g + 1, first=first)
                        pe_up(n + 3, 0, at(g))
                        pe_down(n + 5, 1, at(g), 2 * g + 2)
                    turn(0, first=True)
                    with pe.Fori(1, G) as g:
                        turn(g)
                    pe_down(after - 1, 0, at(0), NE + 1, last=True)

                @block.scalar
                def _(act):
                    def unit(b, filled_at, free):
                        act.wait_ge(w.filled, filled_at)
                        if free is not None:
                            act.wait_ge(h_done, free)
                        nc.scalar.activation(silu[:, b].rearrange("p c s -> p (c s)"), ps[:, 2 * b, :], ACT.Silu).then_inc(silu_done, 1)
                    unit(0, base + 1, None)
                    unit(1, base + 3, None)
                    unit(0, base + 6, 1)
                    with act.Fori(1, G) as g:
                        unit(1, 6 * g + base + 3, 2 * g)
                        unit(0, 6 * g + base + 6, 2 * g + 1)

                @block.vector
                def _(dve):
                    v = nc.vector
                    chain_n = [0]

                    def unit(b, filled_up, silu_at, down_before, step_at, comb=None):
                        dve.wait_ge(w.filled, filled_up)
                        dve.wait_ge(silu_done, silu_at)
                        if down_before is not None:
                            dve.wait_ge(w.filled, down_before)
                        h, s = hid[:, b], silu[:, b]
                        up = ps[:, 2 * b + 1, :].rearrange("p (c s) -> p c s", c=EC)
                        if comb is None:
                            v.tensor_tensor(h, up, s, ALU.mult).then_inc(h_done, 1)
                            return
                        par, cb_at = comb
                        v.tensor_tensor(h, up, s, ALU.mult).then_inc(steps, 1)
                        dve.wait_ge(steps, step_at)
                        dve.wait_ge(cb_landed[par], cb_at)
                        v.tensor_tensor(h, h, cb[:, par, :].unsqueeze(1).to_broadcast([P, EC, S]), ALU.mult).then_inc(h_done, 1)

                    unit(0, base + 2, 1, None, None)
                    unit(1, base + 4, 2, None, 1, comb=(0, 16))
                    unit(0, base + 7, 3, base + 5, 2, comb=(1, 16))
                    with dve.Fori(1, G) as g:
                        unit(1, 6 * g + base + 4, 2 * g + 2, 6 * g + base + 2, 2 * g + 1, comb=(0, 16 * g + 16))
                        unit(0, 6 * g + base + 7, 2 * g + 3, 6 * g + base + 5, 2 * g + 2, comb=(1, 16 * g + 16))
                    dve.wait_ge(w.filled, base + 3 * NE + 3)
                    ch = Chain(dve, st.sem("tail_steps"))
                    g2 = self.mod_row(3)
                    for t in range(TT):
                        for half in range(2):
                            ch.step(v.tensor_tensor(tmp[:, half * 512:(half + 1) * 512], y[t][half],
                                                    g2[:, half * 512:(half + 1) * 512], ALU.mult))
                        ch.step(v.tensor_tensor(self.x[:, t, :], self.x[:, t, :], tmp[:], ALU.add))
            self.finished = frozenset(s for s, *_ in w.items[:after])

    def hybrid_layer(self):
        d = self.dram
        with ExitStack() as m1:
            mod1 = m1.enter_context(self.nc.sbuf_tensor("modulation_1", [P, 2 * D], F32))
            self.modulation("mod1", mod1, 0, 2 * D)
            self.norm("norm1", self.x, self.hT, d["norm1_g"][0], modulate=(mod1[:, 0:D], mod1[:, D:2 * D]))
        self.rwkv()
        self.mod = self.keep("modulation_2", [P, 4 * D], layer=True)
        self.modulation("mod2", self.mod, 2 * D, 4 * D)
        self.project_z()
        self.sparse_attention()
        self.mix_and_project()
        self.norm("norm2", self.x, self.hT, d["norm2_g"][0], modulate=(self.mod_row(1), self.mod_row(2)))
        self.route()
        self.experts()

    def mod_row(self, i):
        return self.mod[:, i * D:(i + 1) * D]

    def unit(self, key, groups, dst, src_view, engine, first=True, last=True, scale=None, func=None):
        nc = self.nc

        def drain(eng, bank, chain):
            if engine == "act":
                return nc.scalar.activation(dst, src_view(bank), func or ACT.Copy, scale=scale or 1.0)
            if scale is not None:
                return nc.vector.tensor_scalar(dst, src_view(bank), scale, None, ALU.mult)
            return nc.vector.tensor_copy(dst, src_view(bank))
        return dict(key=key, mms=groups, engine=engine, drain=drain, first=first, last=last)

    def rope(self, v, ch, src, dst, tmp, cos, sin):
        lo, hi = slice(0, 32), slice(32, 64)
        ix = (slice(None),) * (len(src.shape) - 1)
        ch.step(v.tensor_tensor(dst[ix + (lo,)], src[ix + (lo,)], cos, ALU.mult))
        ch.step(v.tensor_tensor(dst[ix + (hi,)], src[ix + (hi,)], cos, ALU.mult))
        ch.step(v.tensor_tensor(tmp[ix + (lo,)], src[ix + (hi,)], sin, ALU.mult))
        ch.step(v.tensor_tensor(tmp[ix + (hi,)], src[ix + (lo,)], sin, ALU.mult))
        ch.step(v.tensor_tensor(dst[ix + (lo,)], dst[ix + (lo,)], tmp[ix + (lo,)], ALU.subtract))
        return v.tensor_tensor(dst[ix + (hi,)], dst[ix + (hi,)], tmp[ix + (hi,)], ALU.add)

    def inverse_root(self, dve, ch, act_sem, wait_at, ms, root, tmp):
        v = self.nc.vector
        dve.wait_ge(act_sem, wait_at)
        ch.step(v.reciprocal(root, root))
        ch.step(v.tensor_tensor(tmp, root, root, ALU.mult))
        ch.step(v.tensor_tensor(tmp, tmp, ms, ALU.mult))
        ch.step(v.tensor_scalar(tmp, tmp, -0.5, 1.5, ALU.mult, ALU.add))
        ch.step(v.tensor_tensor(root, root, tmp, ALU.mult))

    def even_mixer(self):
        nc, ps, d = self.nc, self.psum, self.dram
        QR, QN = 192, 128
        with Stage(nc, "even") as top:
            mixT = top.sbuf("mixT", [P, DC, S])
            aqT, akT, av = top.sbuf("aqT", [P, 4, S]), top.sbuf("akT", [P, 4, S]), top.sbuf("av", [P, TT, 512])
            cq, ckr = top.sbuf("cq", [P, TT, 256]), top.sbuf("ckv_kr", [P, TT, 192])
            qnT, knT, vb = top.sbuf("qnT", [P, 4, S]), top.sbuf("knT", [P, 4, S]), top.sbuf("vb", [P, TT, 512])
            qrT, krT = top.sbuf("qrT", [P, 4, S]), top.sbuf("krT", [P, S])
            chunk, dist, rope = top.sbuf("chunk_mask", [P, TT, S]), top.sbuf("distance", [P, TT, S]), top.sbuf("rope", [P, 2, TT, 32])
            dbias = top.sbuf("distance_bias", [P, 4, TT, S])
            lam, lv = top.sbuf("lambda", [P, 4]), top.sbuf("lambda_vectors", [P, 4, DH])
            self.norm("ev_norm", self.x, self.hT, d["ev_norm_2"][0])
            u = []
            for i in range(2):
                u.append(self.to_features(("ev_in", i), 2, self.hT, DC, (0, 1), aqT[:, 2 * i:2 * i + 2, :], ("act", "dve")[i]))
            for i in range(2):
                u.append(self.to_features(("ev_in", 2 + i), 2, self.hT, DC, (0, 1), akT[:, 2 * i:2 * i + 2, :], ("act", "dve")[i]))
            for i in range(2):
                u.append(self.to_tokens(("ev_in", 4 + i), self.hT, DC, 0, 256, av[:, :, i * 256:(i + 1) * 256], ("act", "dve")[i]))
            u.append(self.to_tokens(("ev_in", 6), self.hT, DC, 0, 256, cq[:], "act"))
            u.append(self.to_tokens(("ev_in", 7), self.hT, DC, 0, 192, ckr[:], "dve"))
            self.products("ev_in", u)

            with Stage(nc, "mlan") as st:
                cqT, ckvT = st.sbuf("cqT", [P, 2, S]), st.sbuf("ckvT", [P, S])
                sq, stat = st.sbuf("square", [P, TT, 256]), st.sbuf("stat", [P, 3, 4])
                kr, krt = st.sbuf("kr", [P, TT, DH]), st.sbuf("kr_tmp", [P, TT, DH])
                landed, summed, rooted, steps, ready, turned = (st.sem(x) for x in (
                    "landed", "summed", "rooted", "steps", "ready", "turned"))
                with nc.Block() as block:
                    self.weight_loads(block, "mlan")

                    @block.scalar
                    def _(act):
                        loads = [(chunk[:], d["c_chunk"]), (dist[:], d["c_dist"]), (rope[:], d["c_rope"])]
                        for i, name in enumerate(("diff_lq1_2", "diff_lk1_2", "diff_lq2_2", "diff_lk2_2")):
                            loads.append((lv[:, i, :], d[name][0].partition_broadcast(P)))
                        for dst, src in loads:
                            act.dma_start(dst, src).then_inc(landed, 16)
                        act.wait_ge(landed, 16 * len(loads))
                        act.wait_ge(summed, 1)
                        nc.scalar.activation(lam[:, 2:4], lam[:, 0:2], ACT.Exp).then_inc(rooted, 1)
                        nc.scalar.activation(stat[:, 1, :], stat[:, 0, :], ACT.Sqrt).then_inc(rooted, 1)

                    @block.vector
                    def _(dve):
                        v, ch = nc.vector, Chain(dve, steps)
                        for t in range(TT):
                            for j, (src, n) in enumerate(((cq[:, t, :], 256), (ckr[:, t, 0:P], P))):
                                ch.step(v.tensor_tensor_reduce(out=sq[:, t, 0:n], in0=src, in1=src, scale=1.0, scalar=0.0,
                                                               op0=ALU.mult, op1=ALU.add, accum_out=stat[:, 0, 2 * j + t:2 * j + t + 1]))
                        for j, n in enumerate((256, P)):
                            ch.step(v.tensor_scalar(stat[:, 0, 2 * j:2 * j + 2], stat[:, 0, 2 * j:2 * j + 2], 1.0 / n, 1e-6, ALU.mult, ALU.add))
                        dve.wait_ge(landed, 16 * 7)
                        for j in range(2):
                            last = v.tensor_tensor_reduce(out=sq[:, 0, 0:DH], in0=lv[:, 2 * j, :], in1=lv[:, 2 * j + 1, :], scale=1.0,
                                                          scalar=0.0, op0=ALU.mult, op1=ALU.add, accum_out=lam[:, j:j + 1])
                            ch.step(last) if j == 0 else last.then_inc(summed, 1)
                        dve.wait_ge(summed, 1)
                        for h in range(4):
                            ch.step(v.scalar_tensor_tensor(out=dbias[:, h], in0=dist[:], scalar=2.0 ** (-2.0 * (h + 1)), in1=chunk[:],
                                                           op0=ALU.mult, op1=ALU.add))
                        ch.step(self.rope(v, ch, ckr[:, :, P:P + DH], kr, krt, rope[:, 0], rope[:, 1]))
                        self.inverse_root(dve, ch, rooted, 2, stat[:, 0, :], stat[:, 1, :], stat[:, 2, :])
                        ch.step(v.tensor_tensor(lam[:, 0:1], lam[:, 3:4], lam[:, 2:3], ALU.subtract))
                        ch.step(v.tensor_scalar(lam[:, 0:1], lam[:, 0:1], -LAMBDA_INIT, None, ALU.add))
                        for t in range(TT):
                            ch.step(v.tensor_scalar(cq[:, t, :], cq[:, t, :], stat[:, 1, t:t + 1], None, ALU.mult))
                            last = v.tensor_scalar(ckr[:, t, 0:P], ckr[:, t, 0:P], stat[:, 1, 2 + t:3 + t], None, ALU.mult)
                            ch.step(last) if t == 0 else last.then_inc(ready, 1)
                        dve.wait_ge(turned, 1)
                        for c in range(2):
                            ch.step(v.tensor_scalar(cqT[:, c, :], ps[:, 0, c * S:(c + 1) * S], self.column("mla_g_cq_2", c), None, ALU.mult))
                        ch.step(v.tensor_scalar(ckvT[:], ps[:, 1, 0:S], self.column("mla_g_ckv_2"), None, ALU.mult))
                        ch.step(v.tensor_copy(krT[0:DH, :], ps[0:DH, 2, 0:S]))
                        ch.step(v.memset(krT[DH:P, :], 0.0))
                        ch.step(v.memset(qrT[DH:P, :, :], 0.0))

                    @block.tensor
                    def _(pe):
                        pe.wait_ge(ready, 1)
                        for t in range(TT):
                            for c in range(2):
                                nc.tensor.transpose(ps[:, 0, c * S + t * P:c * S + (t + 1) * P], cq[:, t, c * P:(c + 1) * P], self.ident[:, :])
                            nc.tensor.transpose(ps[:, 1, t * P:(t + 1) * P], ckr[:, t, 0:P], self.ident[:, :])
                            mm = nc.tensor.transpose(ps[0:DH, 2, t * P:(t + 1) * P], kr[:, t, :], self.ident[:, :])
                        mm.then_inc(turned, 1)

                qr, qrt = st.sbuf("qr", [P, TT, 4, DH]), st.sbuf("qr_tmp", [P, TT, 4, DH])
                u = []
                two = lambda b: b.rearrange("p (c s) -> p c s", c=2)
                for i in range(2):
                    u.append(self.unit(("w_uq", 0), lambda bank, wv, i=i: [
                        (bank[:, j * S:(j + 1) * S], [(wv[:, k, (2 * i + j) * QR:(2 * i + j) * QR + QN], cqT[:, k, :]) for k in range(2)])
                        for j in range(2)], qnT[:, 2 * i:2 * i + 2, :], two, ("act", "dve")[i], first=(i == 0), last=False))
                u.append(self.unit(("w_uq", 0), lambda bank, wv: [
                    (bank[:, (4 * t + h) * DH:(4 * t + h + 1) * DH],
                     [(cqT[:, k, t * P:(t + 1) * P], wv[:, k, h * QR + QN:(h + 1) * QR]) for k in range(2)])
                    for t in range(TT) for h in range(4)],
                    qr[:].rearrange("p t h e -> p (t h e)"), lambda b: b, "act", first=False))
                for i in range(2):
                    u.append(self.unit(("w_ukv", 0), lambda bank, wv, i=i: [
                        (bank[:, j * S:(j + 1) * S], [(wv[:, 0, (2 * i + j) * 256:(2 * i + j) * 256 + P], ckvT[:, :])])
                        for j in range(2)], knT[:, 2 * i:2 * i + 2, :], two, ("act", "dve")[i], first=(i == 0), last=False))
                for t in range(TT):
                    u.append(self.unit(("w_ukv", 0), lambda bank, wv, t=t: [
                        (bank[:, h * P:(h + 1) * P], [(ckvT[:, t * P:(t + 1) * P], wv[:, 0, h * 256 + P:(h + 1) * 256])])
                        for h in range(4)], vb[:, t, :], lambda b: b, ("act", "dve")[t], first=False, last=(t == 1)))
                self.products("mla_up", u)
                out = st.sbuf("qr_turned", [P, TT, 4, DH])
                s3, r3, t3 = st.sem("rope_steps"), st.sem("rope_ready"), st.sem("rope_turned")
                with nc.Block() as block:
                    self.weight_loads(block, "qrope")

                    @block.vector
                    def _(dve):
                        v, ch = nc.vector, Chain(dve, s3)
                        for t in range(TT):
                            cos, sin = (rope[:, i, t, :].unsqueeze(1).to_broadcast([P, 4, 32]) for i in range(2))
                            last = self.rope(v, ch, qr[:, t], out[:, t], qrt[:, t], cos, sin)
                            last.then_inc(r3, 1)
                            dve.wait_ge(r3, t + 1)
                        dve.wait_ge(t3, 1)
                        for b in range(2):
                            ch.step(v.tensor_copy(qrT[0:DH, 2 * b:2 * b + 2, :], two(ps[0:DH, b, :])))

                    @block.tensor
                    def _(pe):
                        for t in range(TT):
                            pe.wait_ge(r3, t + 1)
                            for h in range(4):
                                o = (h % 2) * S + t * P
                                mm = nc.tensor.transpose(ps[0:DH, h // 2, o:o + P], out[:, t, h, :], self.ident[:, :])
                        mm.then_inc(t3, 1)

            with Stage(nc, "diffo") as st:
                od = st.sbuf("diff_out", [P, TT, 512])
                units = []
                for h in range(4):
                    units.append(dict(
                        scores=lambda banks, h=h: [
                            (banks[s][:, t * S:(t + 1) * S],
                             [(aqT[s * DH:(s + 1) * DH, h, t * P:(t + 1) * P], akT[s * DH:(s + 1) * DH, h, :])])
                            for s in range(2) for t in range(TT)],
                        bias=dbias[:, h],
                        values=lambda bank, pT, h=h: [
                            (bank[:, t * P:(t + 1) * P],
                             [(pT[:, kt, t * P:(t + 1) * P], av[:, kt, h * P:(h + 1) * P]) for kt in range(TT)]) for t in range(TT)],
                        result=lambda bank, h=h: (od[:, :, h * P:(h + 1) * P], bank[:, 0:S].rearrange("p (t e) -> p t e", t=TT))))
                self.attend("diff", units, DH ** -0.5, ns=2, neg_lam=lam[:, 0:1])
                sq, stat = st.sbuf("square", [P, TT * 4, P]), st.sbuf("stat", [P, 3, TT * 4])
                steps, summed, rooted, ready, turned = (st.sem(x) for x in ("steps", "summed", "rooted", "ready", "turned"))
                o8 = od[:].rearrange("p t (h e) -> p (t h) e", h=4)
                with nc.Block() as block:
                    self.weight_loads(block, "diffn")

                    @block.scalar
                    def _(act):
                        act.wait_ge(summed, 1)
                        nc.scalar.activation(stat[:, 1, :], stat[:, 0, :], ACT.Sqrt).then_inc(rooted, 1)

                    @block.vector
                    def _(dve):
                        v, ch = nc.vector, Chain(dve, steps)
                        ch.step(v.tensor_tensor(sq[:], o8, o8, ALU.mult))
                        ch.step(v.tensor_reduce(stat[:, 0, :], sq[:], AX.X, ALU.add))
                        v.tensor_scalar(stat[:, 0, :], stat[:, 0, :], 1.0 / P, 1e-6, ALU.mult, ALU.add).then_inc(summed, 1)
                        self.inverse_root(dve, ch, rooted, 1, stat[:, 0, :], stat[:, 1, :], stat[:, 2, :])
                        v.tensor_tensor(o8, o8, stat[:, 1, :].unsqueeze(2).to_broadcast([P, TT * 4, P]), ALU.mult).then_inc(ready, 1)
                        dve.wait_ge(turned, 1)
                        for b in range(2):
                            ch.step(v.tensor_scalar(mixT[:, 2 * b:2 * b + 2, :], ps[:, b, :].rearrange("p (c s) -> p c s", c=2),
                                                    self.column("diff_subln_2"), 1.0 - LAMBDA_INIT, ALU.mult, ALU.mult))

                    @block.tensor
                    def _(pe):
                        pe.wait_ge(ready, 1)
                        for h in range(4):
                            for t in range(TT):
                                o = (h % 2) * S + t * P
                                mm = nc.tensor.transpose(ps[:, h // 2, o:o + P], od[:, t, h * P:(h + 1) * P], self.ident[:, :])
                        mm.then_inc(turned, 1)
            units = []
            for h in range(4):
                units.append(dict(
                    scores=lambda banks, h=h: [
                        (banks[0][:, t * S:(t + 1) * S],
                         [(qnT[:, h, t * P:(t + 1) * P], knT[:, h, :]), (qrT[:, h, t * P:(t + 1) * P], krT[:, :])]) for t in range(TT)],
                    bias=chunk[:],
                    values=lambda bank, pT, h=h: [(bank[:, 0:S], [(vb[:, kt, h * P:(h + 1) * P], pT[:, kt, :]) for kt in range(TT)])],
                    result=lambda bank, h=h: (mixT[:, 4 + h, :], bank[:, 0:S])))
            self.attend("mla", units, QR ** -0.5)
            self.residual("ev_out", "ev_out", mixT, DC, 0)

    def odd_mixer(self):
        nc, ps = self.nc, self.psum
        NH = 16
        with Stage(nc, "odd") as top:
            qT, kT, vt = top.sbuf("qT", [P, DC, S]), top.sbuf("kT", [P, DC, S]), top.sbuf("v", [P, TT, D])
            oT = top.sbuf("oT", [P, DC, S])
            later, ones, outside = top.sbuf("later", [P, P]), top.sbuf("ones", [P, P]), top.sbuf("outside", [P, TT, S])
            self.norm("od_norm", self.x, self.hT, self.dram["od_norm_2"][0])
            u = []
            two = lambda b: b.rearrange("p (c s) -> p c s", c=2)
            for i in range(4):
                x = self.to_features(("sb_in", i), 2, self.hT, DC, (0, 1), qT[:, 2 * i:2 * i + 2, :], "act")
                x["drain"] = lambda eng, bank, chain, i=i: nc.scalar.activation(
                    qT[:, 2 * i:2 * i + 2, :], two(bank), ACT.Copy, scale=DH ** -0.5)
                u.append(x)
            for i in range(4):
                u.append(self.to_features(("sb_in", 4 + i), 2, self.hT, DC, (0, 1), kT[:, 2 * i:2 * i + 2, :], "dve"))
            for i in range(4):
                u.append(self.to_tokens(("sb_in", 8 + i), self.hT, DC, 0, 256, vt[:, :, i * 256:(i + 1) * 256], ("act", "dve")[i % 2]))
            self.products("sb_in", u)
            with Stage(nc, "sb") as st:
                W = [P, 2, TT * S]
                ln, zm, sp, pr = st.sbuf("ln", W), st.sbuf("z_masked", W), st.sbuf("softplus", W), st.sbuf("prob", W)
                scored, lned, spd, summed, argd, exped, valued, stored, steps, asteps, cl, made = (st.sem(x) for x in (
                    "scored", "ln_done", "softplus_done", "summed", "arg_done", "exped", "valued", "stored", "steps", "act_steps",
                    "const_landed", "const_made"))
                flat = lambda t: t[:].rearrange("p t s -> p (t s)")
                with nc.Block() as block:
                    self.weight_loads(block, "sb")

                    @block.tensor
                    def _(pe):
                        for i in range(NH + 2):
                            if i < NH:
                                lo = DH * (i % 2)
                                if i >= 2:
                                    pe.wait_ge(spd, i - 1)
                                for kt in range(TT):
                                    mm = nc.tensor.matmul(ps[:, i % 2, kt * S:(kt + 1) * S],
                                                          kT[lo:lo + DH, i // 2, kt * P:(kt + 1) * P], qT[lo:lo + DH, i // 2, :],
                                                          start=True, stop=True)
                                mm.then_inc(scored, 1)
                            if 1 <= i <= NH:
                                u = i - 1
                                pe.wait_ge(spd, u + 1)
                                if u == 0:
                                    pe.wait_ge(made, 1)
                                    pe.wait_ge(cl, 16)
                                if u >= 2:
                                    pe.wait_ge(argd, u - 1)
                                s = sp[:, u % 2, :]
                                b = ps[:, 2 + u % 2, :]
                                nc.tensor.matmul(b[:, 0:S], later[:, :], s[:, 0:S], start=True, stop=False)
                                nc.tensor.matmul(b[:, 0:S], ones[:, :], s[:, S:2 * S], start=False, stop=True)
                                nc.tensor.matmul(b[:, S:2 * S], later[:, :], s[:, S:2 * S], start=True, stop=True).then_inc(summed, 1)
                            if i >= 2:
                                u = i - 2
                                lo = DH * (u % 2)
                                pe.wait_ge(exped, u + 1)
                                if u >= 2:
                                    pe.wait_ge(stored, u - 1)
                                for kt in range(TT):
                                    mm = nc.tensor.matmul(ps[lo:lo + DH, 4 + u % 2, 0:S], vt[:, kt, u * DH:(u + 1) * DH],
                                                          pr[:, u % 2, kt * S:(kt + 1) * S], start=(kt == 0), stop=(kt == TT - 1))
                                mm.then_inc(valued, 1)

                    @block.scalar
                    def _(act):
                        act.dma_start(later[:], self.dram["c_later"]).then_inc(cl, 16)
                        ch = Chain(act, asteps)
                        for i in range(NH + 1):
                            if i < NH:
                                b = i % 2
                                act.wait_ge(scored, i + 1)
                                if i >= 2:
                                    act.wait_ge(spd, i - 1)
                                ch.step(nc.scalar.activation(ln[:, b, :], ps[:, b, :], ACT.Abs))
                                ch.step(nc.scalar.activation(ln[:, b, :], ln[:, b, :], ACT.Exp, scale=-1.0))
                                nc.scalar.activation(ln[:, b, :], ln[:, b, :], ACT.Ln, bias=1.0).then_inc(lned, 1)
                            if i >= 1:
                                u = i - 1
                                act.wait_ge(argd, u + 1)
                                if u >= 2:
                                    act.wait_ge(valued, u - 1)
                                nc.scalar.activation(pr[:, u % 2, :], zm[:, u % 2, :], ACT.Exp).then_inc(exped, 1)

                    @block.vector
                    def _(dve):
                        v, ch = nc.vector, Chain(dve, steps)
                        v.memset(ones[:], 1.0).then_inc(made, 1)
                        ch.step(v.tensor_scalar(outside[:], self.strict[:], -1.0, BIG, ALU.add, ALU.mult))
                        for i in range(NH + 2):
                            if i < NH:
                                b = i % 2
                                dve.wait_ge(lned, i + 1)
                                if i >= 2:
                                    dve.wait_ge(exped, i - 1)
                                    dve.wait_ge(summed, i - 1)
                                ch.step(v.tensor_tensor(zm[:, b, :], ps[:, b, :], flat(outside), ALU.add))
                                ch.step(v.scalar_tensor_tensor(out=sp[:, b, :], in0=ps[:, b, :], scalar=0.0, in1=ln[:, b, :],
                                                               op0=ALU.max, op1=ALU.add))
                                v.tensor_tensor(sp[:, b, :], sp[:, b, :], flat(self.strict), ALU.mult).then_inc(spd, 1)
                            if 1 <= i <= NH:
                                u = i - 1
                                dve.wait_ge(summed, u + 1)
                                v.tensor_tensor(zm[:, u % 2, :], zm[:, u % 2, :], ps[:, 2 + u % 2, :], ALU.subtract).then_inc(argd, 1)
                            if i >= 2:
                                u = i - 2
                                lo = DH * (u % 2)
                                dve.wait_ge(valued, u + 1)
                                v.tensor_copy(oT[lo:lo + DH, u // 2, :], ps[lo:lo + DH, 4 + u % 2, 0:S]).then_inc(stored, 1)
                        dve.wait_ge(stored, NH)
            self.residual("sb_out", "sb_out", oT, DC, 0)

    def cross(self, i):
        nc, d = self.nc, self.dram
        with Stage(nc, f"cross{i}") as top:
            memT, mkT = top.sbuf("memT", [P, DC, S]), top.sbuf("kT", [P, DC, S])
            mv, qT, oT = top.sbuf("v", [P, TT, D]), top.sbuf("qT", [P, DC, S]), top.sbuf("oT", [P, DC, S])
            self.norm(f"mem_norm{i}", self.mem, memT, d["xa_mem_norm_2"][i])
            u = []
            for j in range(4):
                u.append(self.to_features((("xa_wkv", i), j), 2, memT, DC, (0, 1), mkT[:, 2 * j:2 * j + 2, :], ("act", "dve")[j % 2]))
            for j in range(4):
                u.append(self.to_tokens((("xa_wkv", i), 4 + j), memT, DC, 0, 256, mv[:, :, j * 256:(j + 1) * 256], ("act", "dve")[j % 2]))
            self.products(f"xa_kv{i}", u)
            self.norm(f"xa_norm{i}", self.x, self.hT, d["xa_norm_2"][i])
            self.products(f"xa_q{i}", [
                self.to_features((("xa_wq", i), j), 2, self.hT, DC, (0, 1), qT[:, 2 * j:2 * j + 2, :], ("act", "dve")[j % 2])
                for j in range(4)])
            units = []
            for h in range(4):
                units.append(dict(
                    scores=lambda banks, h=h: [
                        (banks[0][:, t * S:(t + 1) * S],
                         [(qT[:, 2 * h + c, t * P:(t + 1) * P], mkT[:, 2 * h + c, :]) for c in range(2)]) for t in range(TT)],
                    bias=None,
                    values=lambda bank, pT, h=h: [
                        (bank[:, c * S:(c + 1) * S],
                         [(mv[:, kt, h * 256 + c * P:h * 256 + (c + 1) * P], pT[:, kt, :]) for kt in range(TT)]) for c in range(2)],
                    result=lambda bank, h=h: (oT[:, 2 * h:2 * h + 2, :], bank.rearrange("p (c s) -> p c s", c=2))))
            self.attend(f"xa{i}", units, 256 ** -0.5)
            self.residual(f"xa_o{i}", ("xa_wo", i), oT, DC, 0)

    def mlp(self, i):
        nc, ps, w = self.nc, self.psum, self.w
        NG = 16
        with Stage(nc, f"mlps{i}") as st:
            hid = st.sbuf("hidden", [P, 2 * NG, S])
            self.norm(f"mlp_norm{i}", self.x, self.hT, self.dram["mlp_norm_2"][i])
            units = []
            for g in range(NG):
                u = self.to_features((("mlp_w1", i), g), 2, self.hT, DC, (0, 1), None, "act")

                def drain(eng, bank, chain, g=g):
                    h = hid[:, 2 * g:2 * g + 2, :]
                    chain.step(nc.scalar.activation(h, bank.rearrange("p (c s) -> p c s", c=2), ACT.Relu))
                    return nc.scalar.activation(h, h, ACT.Square)
                u["drain"] = drain
                units.append(u)
            self.products(f"mlp{i}", units)
            base, n0 = w.n_filled, w.index[(("mlp_w2", i), 0)]
            for g in range(NG):
                w.done_at[n0 + g] = base + g + 1
            w.n_filled = base + NG
            added = st.sem("added")
            with nc.Block() as block:
                self.weight_loads(block, f"mlpd{i}")

                @block.tensor
                def _(pe):
                    for g in range(NG):
                        key = (("mlp_w2", i), g)
                        w.arrived(pe, key)
                        wv = w.view(key)
                        for t in range(TT):
                            for c in range(2):
                                for half in range(2):
                                    mm = nc.tensor.matmul(ps[:, 2 * t + half, :], hid[:, 2 * g + c, t * P:(t + 1) * P],
                                                          wv[:, c, half * 512:(half + 1) * 512], start=(g == 0 and c == 0),
                                                          stop=(g == NG - 1 and c == 1), skip_group_check=True)
                        mm.then_inc(w.filled, 1)

                @block.vector
                def _(dve):
                    dve.wait_ge(w.filled, base + NG)
                    for t in range(TT):
                        for half in range(2):
                            x = self.x[:, t, half * 512:(half + 1) * 512]
                            nc.vector.tensor_tensor(x, x, ps[:, 2 * t + half, :], ALU.add).then_inc(added, 1)
                    dve.wait_ge(added, 4)

    def run(self):
        nc, d = self.nc, self.dram
        self.load_constants()
        self.hybrid_layer()
        self.layer.close()
        self.norm("final_g", self.x, None, d["final_g"], tokens=self.x)
        self.mem = self.keep("memory", [P, TT, D])
        with Stage(nc, "memory") as st:
            landed = st.sem("landed")
            with nc.Block() as block:
                @block.scalar
                def _(act):
                    act.dma_start(self.mem[:], d["mem_2"][0].rearrange("(t p) n -> p t n", p=P)).then_inc(landed, 16)
                    act.wait_ge(landed, 16)
        self.even_mixer()
        for i in range(2):
            if i == 1:
                self.odd_mixer()
            self.cross(i)
            self.mlp(i)
        self.norm("final", self.x, None, d["final_norm_2"], out_dram=self.out[0].rearrange("(t p) n -> p t n", p=P))


def hybrid_program(nc, dram, out):
    k = Hybrid(nc, dram, out)
    k.run()
    k.layer.close()
    k.ctx.close()


def kernel(**inputs):
    import concourse.bacc as bacc
    from concourse.bass_utils import run_bass_kernel_spmd

    nc = bacc.Bacc("TRN2", target_bir_lowering=False, num_devices=1)
    arrays, dram = {}, {}
    for name, a in list(inputs.items()) + list(shape_constants().items()):
        a = np.ascontiguousarray(a)
        arrays[f"in_{name}"] = a
        dram[name] = nc.dram_tensor(f"in_{name}", a.shape, mybir.dt.from_np(a.dtype), kind="ExternalInput").ap()
    out = nc.dram_tensor("out_0", (1, S, D), F32, kind="ExternalOutput").ap()
    hybrid_program(nc, dram, out)
    r = run_bass_kernel_spmd(nc, [arrays], core_ids=[0])
    return r.results[0]["out_0"]
```

```python
import math
from contextlib import ExitStack

import numpy as np

import concourse.bass as bass
from concourse import mybir

F32 = mybir.dt.float32
FR = mybir.dt.float32r
ACT = mybir.ActivationFunctionType
ALU = mybir.AluOpType
AX = mybir.AxisListType

P = 128
S = 256
TT = S // P
D = 1024
DC = D // P
DH = 64
QH = 8
IH = 16
ID = 32
TOPK = 64
C = 64
NC = S // C
NE = 64
FF = 256
EC = FF // P
RING = 6
SLOT = 2048
BIG = 1.0e30
TAKEN = -3.0e38
DECAY = math.exp(-0.5)

W_Q, W_K, W_V, W_IQ, W_IK, W_IW = 0, 512, 1024, 1536, 2048, 2080
W_ZR, W_GA, W_GR = 2096, 3888, 4912

COLS = (("tshift_mu", 14), ("decay_w0", 4), ("iclr_a0", 4), ("k_k", 4), ("k_a", 4), ("r_k", 4),
        ("lnx_g", 4), ("lnx_b", 4), ("diff_subln_2", 1), ("mla_g_cq_2", 2), ("mla_g_ckv_2", 1))
COL = {}
_at = 0
for _name, _rows in COLS:
    COL[_name] = _at
    _at += _rows
NCOL = _at
LAMBDA_INIT = 0.8 - 0.6 * math.exp(0.0)


def shape_constants():
    t = np.arange(P)
    q = np.arange(S).reshape(TT, P).transpose(1, 0)
    k = np.arange(S)
    out = {}
    out["c_ident"] = np.eye(P, dtype=np.float32)
    out["c_blockones"] = (t[:, None] // DH == t[None, :] // DH).astype(np.float32)
    out["c_causal"] = (k[None, None, :] <= q[:, :, None]).astype(np.float32)
    out["c_chunk"] = np.where(k[None, None, :] // C <= q[:, :, None] // C, 0.0, -BIG).astype(np.float32)
    out["c_strict"] = (q[:, :, None] < k[None, None, :]).astype(np.float32)
    out["c_later"] = (t[:, None] >= t[None, :]).astype(np.float32)
    out["c_dist"] = -np.abs(q[:, :, None] - k[None, None, :]).astype(np.float32)
    s = np.arange(C)
    pair = np.stack([(s[:, None] < s[None, :]), (s[:, None] <= s[None, :])], 1)
    out["c_pair"] = np.concatenate([pair, pair]).astype(np.float32)
    lev = []
    n = 1
    while n < C:
        lev.append((t[:, None] // (2 * n) == t[None, :] // (2 * n)) & (t[:, None] // n % 2 == 0)
                   & (t[None, :] // n % 2 == 1))
        n *= 2
    out["c_levels"] = np.stack(lev, 1).astype(np.float32)
    out["c_restart"] = np.broadcast_to((k % C != 0).astype(np.float32), (P, S)).copy()
    dist = np.arange(S)
    nf = np.maximum(dist, 1).astype(np.float32)
    large = 16 + (np.log(nf / np.float32(16)) / np.float32(math.log(8.0)) * np.float32(16)).astype(np.int32)
    bucket = np.where(dist < 16, dist, np.minimum(large, 31))
    rev = np.zeros((32, 2 * S), np.float32)
    rev[bucket, S - 1 + dist] = 1.0
    rev[0, :S - 1] = 1.0
    out["c_bucket"] = rev
    inv = np.float32(10000.0) ** (-np.arange(32, dtype=np.float32) / np.float32(32))
    ang = (np.arange(S, dtype=np.float32)[:, None] * inv[None, :].astype(np.float32)).reshape(TT, P, 32).transpose(1, 0, 2)
    out["c_rope"] = np.stack([np.cos(ang), np.sin(ang)], 1).astype(np.float32)
    return out


class Stage:

    def __init__(self, nc, name):
        self.nc, self.name = nc, name
        self.ctx = ExitStack()
        self.sems = []

    def __enter__(self):
        self.ctx.__enter__()
        return self

    def __exit__(self, *exc):
        if self.sems and exc[0] is None:
            for sem in self.sems:
                self.nc.gpsimd.sem_clear(sem)
        return self.ctx.__exit__(*exc)

    def sbuf(self, name, shape, dtype=F32):
        return self.ctx.enter_context(self.nc.sbuf_tensor(f"{self.name}_{name}", shape, dtype))

    def sem(self, name):
        sem = self.ctx.enter_context(self.nc.semaphore(f"{self.name}_{name}"))
        self.sems.append(sem)
        return sem

    def block(self):
        return self.nc.Block()


class Chain:

    def __init__(self, eng, sem):
        self.eng, self.sem, self.n = eng, sem, 0

    def step(self, ins):
        self.n += 1
        ins.then_inc(self.sem, 1)
        self.eng.wait_ge(self.sem, self.n)
        return ins


class Weights:

    def __init__(self, nc, ctx):
        self.slots = ctx.enter_context(nc.sbuf_tensor("weight_ring", [P, RING, SLOT], F32))
        self.landed = [ctx.enter_context(nc.semaphore(f"weights_landed_{i}")) for i in range(RING)]
        self.filled = ctx.enter_context(nc.semaphore("banks_filled"))
        self.n_filled = 0
        self.done_at = {}
        self.items = []
        self.index = {}
        self.issued = 0

    def plan(self, stage, key, source, chunks, cols):
        self.index[key] = len(self.items)
        self.items.append((stage, source, chunks, cols))

    def view(self, key):
        n = self.index[key]
        _, _, chunks, cols = self.items[n]
        return self.slots[:, n % RING, 0:chunks * cols].rearrange("p (c n) -> p c n", c=chunks)

    def arrived(self, pe, key):
        n = self.index[key]
        pe.wait_ge(self.landed[n % RING], 16 * (n // RING + 1))

    def load(self, sp, n):
        _, source, chunks, cols = self.items[n]
        if n >= RING:
            sp.wait_ge(self.filled, self.done_at[n - RING])
        dst = self.slots[:, n % RING, 0:chunks * cols].rearrange("p (c n) -> p c n", c=chunks)
        sp.dma_start(dst, source).then_inc(self.landed[n % RING], 16)


class Hybrid:
    def __init__(self, nc, dram, out):
        self.nc, self.dram, self.out = nc, dram, out
        self.ctx = ExitStack()
        self.layer = ExitStack()
        self.psum = self.ctx.enter_context(nc.psum_tensor("psum", [P, 8, 512], F32))
        self.w = Weights(nc, self.ctx)
        self.plan_weights()

    def keep(self, name, shape, layer=False):
        t = (self.layer if layer else self.ctx).enter_context(self.nc.sbuf_tensor(name, shape, F32))
        return t

    def plan_weights(self):
        d, w = self.dram, self.w

        def wide(stage, name, src, rows_by_chunk, c0, ncols, step=None):
            rows = src.shape[0]
            nk = rows // P
            step = step or SLOT // nk
            how = "(c p) n -> p c n" if rows_by_chunk else "(p c) n -> p c n"
            for i in range(0, ncols, step):
                n = min(step, ncols - i)
                w.plan(stage, (name, i // step), src.rearrange(how, p=P)[:, :, c0 + i:c0 + i + n], nk, n)

        z = d["w_in"][0]
        wide("mod1", "mod1", d["ada_w"][0], False, 0, 2 * D)
        wide("zr", "w_zr", z, False, W_ZR, 1792)
        wide("mod2", "mod2", d["ada_w"][0], False, 2 * D, 4 * D)
        wide("z", "w_ikw", z, False, W_IK, 48)
        wide("z", "w_q", z, False, W_Q, 512)
        wide("z", "w_k", z, False, W_K, 512)
        wide("z", "w_v", z, False, W_V, 512)
        wide("z", "w_iq", z, False, W_IQ, 512)
        wide("dsa", "w_ga", z, False, W_GA, D)
        wide("dsa", "w_gr", z, False, W_GR, D)
        wide("mix", "w_attn_br", d["w_attn_br"][0], True, 0, D)
        wide("mix", "w_rwkv_br", d["w_rwkv_br"][0], True, 0, D)
        wide("out", "w_out", d["w_out"][0], True, 0, D)
        wide("router", "router_w", d["router_w"][0], False, 0, NE)
        wide("moe", "sh_gate", d["sh_gate"][0], False, 0, FF)
        wide("moe", "sh_up", d["sh_up"][0], False, 0, FF)
        for e in range(NE):
            wide("moe", ("exp_gate", e), d["exp_gate"][0, e], False, 0, FF)
            wide("moe", ("exp_up", e), d["exp_up"][0, e], False, 0, FF)
            if e == 0:
                wide("moe", "sh_down", d["sh_down"][0], True, 0, D)
            else:
                wide("moe", ("exp_down", e - 1), d["exp_down"][0, e - 1], True, 0, D)
        wide("moe", ("exp_down", NE - 1), d["exp_down"][0, NE - 1], True, 0, D)
        ev = d["ev_w_in_2"][0]
        wide("ev_in", "ev_in", ev, False, 0, 1984)
        wide("mla_up", "w_uq", d["mla_w_uq_2"][0], True, 0, 768)
        wide("mla_up", "w_ukv", d["mla_w_ukv_2"][0], True, 0, 1024)
        wide("ev_out", "ev_out", d["ev_w_out_2"][0], True, 0, D)
        for i in range(2):
            if i == 1:
                wide("sb_in", "sb_in", d["sb_w_in_2"][0], False, 0, 3 * D)
                wide("sb_out", "sb_out", d["sb_w_out_2"][0], True, 0, D)
            wide(f"xa_kv{i}", ("xa_wkv", i), d["xa_wkv_2"][i], False, 0, 2 * D)
            wide(f"xa_q{i}", ("xa_wq", i), d["xa_wq_2"][i], False, 0, D)
            wide(f"xa_o{i}", ("xa_wo", i), d["xa_wo_2"][i], True, 0, D)
            wide(f"mlp{i}", ("mlp_w1", i), d["mlp_w1_2"][i], False, 0, 4 * D)
            w2 = d["mlp_w2_2"][i].rearrange("(g c p) n -> g p c n", p=P, c=2)
            for g in range(16):
                w.plan(f"mlpd{i}", (("mlp_w2", i), g), w2[g], 2, D)

    def weight_loads(self, block, name):
        names = []
        for stage, *_ in self.w.items:
            if stage not in names:
                names.append(stage)
        done = set(names[:names.index(name) + 1]) if name in names else self.finished
        self.finished = done

        @block.sync
        def _(sp):
            w = self.w
            while w.issued < len(w.items) and (w.issued < RING or w.items[w.issued - RING][0] in done):
                w.load(sp, w.issued)
                w.issued += 1

    finished = frozenset()

    def products(self, name, units):
        nc, w = self.nc, self.w
        BANKS = 8
        items = []
        for u in units:
            if u["key"] not in items:
                items.append(u["key"])
            u["item"] = items.index(u["key"])
        operand = units[-1].get("operand")
        whole = {u["item"] for u in units if u.get("operand") is not operand or operand is None}
        first_split = max(max(whole, default=-1) + 1, 1)
        if len(items) - first_split < 2:
            first_split = len(items)
        with Stage(nc, name) as st:
            filled, base = w.filled, w.n_filled
            drained = {"act": st.sem("drained_by_act"), "dve": st.sem("drained_by_dve")}
            steps = {"act": st.sem("act_steps"), "dve": st.sem("dve_steps")}
            n = {"act": 0, "dve": 0}
            done = {}
            for i, u in enumerate(units):
                n[u["engine"]] += 1
                u["order"] = n[u["engine"]]
                done[u["item"]] = w.done_at[w.index[u["key"]]] = base + i + 1
            w.n_filled = base + len(units)
            if first_split < len(items):
                wh, wl = st.sbuf("weights_high", [P, 2, SLOT], FR), st.sbuf("weights_low", [P, 2, SLOT], FR)
                shape = list(operand.shape)
                oh, ol = st.sbuf("operand_high", shape, FR), st.sbuf("operand_low", shape, FR)
                nk = shape[1]
                parts = [(0, nk // 2), (nk // 2, nk)]
                op_high, op_low, high_made, low_made = (st.sem(x) for x in (
                    "operand_high_made", "operand_low_made", "weights_high_made", "weights_low_made"))

            def halves(t, item):
                _, _, chunks, cols = w.items[w.index[items[item]]]
                return t[:, item % 2, 0:chunks * cols].rearrange("p (c n) -> p c n", c=chunks)

            def splits(eng, who):
                at = [first_split]

                def upto(item):
                    while at[0] <= min(item, len(items) - 1):
                        i, k = at[0], at[0] - first_split
                        if who == "act":
                            w.arrived(eng, items[i])
                            if k >= 2:
                                eng.wait_ge(filled, done[i - 2])
                            nc.scalar.activation(halves(wh, i), w.view(items[i]), ACT.Copy).then_inc(high_made, 1)
                        else:
                            eng.wait_ge(high_made, k + 1)
                            nc.vector.tensor_tensor(halves(wl, i), w.view(items[i]), halves(wh, i).bitcast(F32),
                                                    ALU.subtract).then_inc(low_made, 1)
                        at[0] += 1
                return upto

            with nc.Block() as block:
                self.weight_loads(block, name)

                @block.tensor
                def _(pe):
                    for i, u in enumerate(units):
                        if i >= BANKS:
                            old = units[i - BANKS]
                            pe.wait_ge(drained[old["engine"]], old["order"])
                        bank, it = self.psum[:, i % BANKS, :], u["item"]
                        if it < first_split:
                            if u.get("first", True):
                                w.arrived(pe, u["key"])
                            groups = [u["mms"](bank, w.view(u["key"]), u.get("operand"))]
                        else:
                            if it == first_split:
                                pe.wait_ge(op_low, len(parts))
                            pe.wait_ge(low_made, it - first_split + 1)
                            h, l = halves(wh, it), halves(wl, it)
                            groups = [u["mms"](bank, h, oh), u["mms"](bank, l, oh), u["mms"](bank, h, ol)]
                        for same in zip(*groups):
                            pairs = [p for step in zip(*(g[1] for g in same)) for p in step]
                            for j, (lhsT, rhs) in enumerate(pairs):
                                mm = nc.tensor.matmul(same[0][0], lhsT, rhs, start=(j == 0), stop=(j == len(pairs) - 1))
                        mm.then_inc(filled, 1)

                def drains(eng, who):
                    chain = Chain(eng, steps[who])
                    upto = splits(eng, who)
                    if first_split < len(items):
                        for i, (a, b) in enumerate(parts):
                            if who == "act":
                                nc.scalar.activation(oh[:, a:b], operand[:, a:b], ACT.Copy).then_inc(op_high, 1)
                            else:
                                eng.wait_ge(op_high, i + 1)
                                nc.vector.tensor_tensor(ol[:, a:b], operand[:, a:b], oh[:, a:b].bitcast(F32),
                                                        ALU.subtract).then_inc(op_low, 1)
                        upto(1)
                    for i, u in enumerate(units):
                        upto(u["item"] + 1)
                        if u["engine"] == who:
                            eng.wait_ge(filled, base + i + 1)
                            if u["order"] > 1:
                                eng.wait_ge(drained[who], u["order"] - 1)
                            u["drain"](eng, self.psum[:, i % BANKS, :], chain).then_inc(drained[who], 1)

                @block.scalar
                def _(act):
                    drains(act, "act")

                @block.vector
                def _(dve):
                    drains(dve, "dve")
    def load_constants(self):
        nc, d = self.nc, self.dram
        K = self.keep
        self.x = K("x_tokens", [P, TT, D])
        self.hT = K("h_features", [P, DC, S])
        self.ident = K("identity", [P, P])
        self.blockones = K("head_block_ones", [P, P])
        self.causal = K("causal_mask", [P, TT, S])
        self.strict = K("strict_mask", [P, TT, S])
        self.col = K("channel_columns", [P, NCOL])
        self.wsmall = K("lora_weights", [P, 3 * 512])
        self.c1 = K("c_silu", [P, DC])
        self.relb = K("rel_bias", [32, QH])
        self.bucket = K("bucket_onehot", [32, 2 * S])
        self.rwT = K("rwkv_out", [P, 4, S], layer=True)
        self.levels = K("level_masks", [P, 6, P], layer=True)
        self.pair = K("pair_masks", [P, 2, C], layer=True)
        self.restart = K("chunk_restart", [P, S], layer=True)
        self.rbias = K("router_bias", [P, NE], layer=True)
        self.later_landed = self.ctx.enter_context(nc.semaphore("later_constants_landed"))
        with Stage(nc, "const") as st:
            rows = st.sbuf("param_rows", [NCOL, P])
            landed = st.sem("landed")
            turned = st.sem("turned")
            silu = st.sem("silu_done")
            loads = [
                (self.c1[:], d["c"][0].rearrange("(p c) -> p c", p=P)),
                (self.ident[:], d["c_ident"]),
            ]
            later = [
                (self.x[:], d["x"][0].rearrange("(t p) n -> p t n", p=P)), (self.blockones[:], d["c_blockones"]),
                (self.causal[:], d["c_causal"]), (self.strict[:], d["c_strict"]),
                (self.levels[:], d["c_levels"]), (self.pair[:], d["c_pair"]), (self.restart[:], d["c_restart"]),
                (self.relb[:], d["rel_bias"]), (self.bucket[:], d["c_bucket"]),
                (self.rbias[:], d["router_bias"][0].partition_broadcast(P)),
                (self.wsmall[0:DH, 0:512], d["decay_up"][0]),
                (self.wsmall[DH:P, 512:1024], d["iclr_up"][0]),
                (self.wsmall[:, 1024:1536], d["gate_up"][0]),
            ]
            for name, n in COLS:
                src = d[name]
                src = src[0] if name != "r_k" else src[0].rearrange("h e -> (h e)")
                loads.append((rows[COL[name]:COL[name] + n, :], src.rearrange("(r p) -> r p", p=P)))
            self.n_later = len(later)
            with nc.Block() as block:
                self.weight_loads(block, "const")

                @block.scalar
                def _(act):
                    for dst, src in loads:
                        act.dma_start(dst, src).then_inc(landed, 16)
                    for dst, src in later:
                        act.dma_start(dst, src).then_inc(self.later_landed, 16)
                    act.wait_ge(landed, 16 * len(loads))
                    nc.scalar.activation(self.c1[:], self.c1[:], ACT.Silu).then_inc(silu, 1)
                    act.wait_ge(silu, 1)

                @block.tensor
                def _(pe):
                    pe.wait_ge(landed, 16 * len(loads))
                    nc.tensor.transpose(self.psum[:, 0, 0:NCOL], rows[:, :], self.ident[0:NCOL, 0:NCOL]).then_inc(turned, 1)

                @block.vector
                def _(dve):
                    dve.wait_ge(turned, 1)
                    nc.vector.tensor_copy(self.col[:], self.psum[:, 0, 0:NCOL]).then_inc(turned, 1)
                    dve.wait_ge(turned, 2)

    def await_constants(self):
        with self.nc.Block() as block:
            @block.scalar
            def _(act):
                act.wait_ge(self.later_landed, 16 * self.n_later)

    def column(self, name, i=0, p0=0, p1=P):
        at = COL[name] + i
        return self.col[p0:p1, at:at + 1]

    def modulation(self, name, mod, c0, ncols):
        nc = self.nc
        with Stage(nc, name + "c") as st:
            cb = st.sbuf("c_repeated", [P, DC, P])
            made, landed = st.sem("made"), st.sem("bias_landed")
            with nc.Block() as block:
                @block.scalar
                def _(act):
                    act.dma_start(mod[:], self.dram["ada_b"][0, c0:c0 + ncols].partition_broadcast(P)).then_inc(landed, 16)

                @block.vector
                def _(dve):
                    nc.vector.tensor_copy(cb[:], self.c1[:].unsqueeze(2).to_broadcast([P, DC, P])).then_inc(made, 1)
                    dve.wait_ge(made, 1)
            units = []
            for i in range(ncols // 256):
                def mms(bank, wv, c):
                    return [(bank[:, 0:256], [(c[:, k, :], wv[:, k, :]) for k in range(DC)])]

                def drain(eng, bank, chain, i=i):
                    m = mod[:, i * 256:(i + 1) * 256]
                    if i == 0:
                        eng.wait_ge(landed, 16)
                    return nc.vector.tensor_tensor(m, bank[:, 0:256], m, ALU.add)
                units.append(dict(key=(name, i), operand=cb, mms=mms, engine="dve", drain=drain))
            self.products(name, units)

    def norm(self, name, x, dst, gain_dram, modulate=None, out_dram=None, tokens=None):
        nc = self.nc
        with Stage(nc, name) as st:
            g = st.sbuf("gain", [P, D])
            y = st.sbuf("normed", [P, TT, D])
            done = tokens if tokens is not None else y
            stat = st.sbuf("stat", [P, 8])
            landed, stored = st.sem("gain_landed"), st.sem("stored")
            half_sum, summed, rooted, ready, turned = (st.sem(s) for s in ("half_summed", "summed", "rooted", "ready", "turned"))
            drained, steps = {"act": st.sem("drained_by_act"), "dve": st.sem("drained_by_dve")}, st.sem("dve_steps")
            with nc.Block() as block:
                self.weight_loads(block, name)

                def drain(eng, who, copy):
                    for b in range(0 if who == "dve" else 1, 4, 2):
                        eng.wait_ge(turned, b + 1)
                        copy(dst[:, 2 * b:2 * b + 2, :],
                             self.psum[:, b, :].rearrange("p (c s) -> p c s", c=2)).then_inc(drained[who], 1)
                    eng.wait_ge(drained[who], 2)

                @block.scalar
                def _(act):
                    act.dma_start(g[:], gain_dram.partition_broadcast(P)).then_inc(landed, 16)
                    nc.scalar.activation(y[:, 1, :], x[:, 1, :], ACT.Square, accum_out=stat[:, 1:2]).then_inc(half_sum, 1)
                    nc.scalar.activation(stat[:, 7:8], self.ident[:, 0:1], ACT.Sqrt)
                    act.wait_ge(summed, 1)
                    nc.scalar.activation(stat[:, 2:4], stat[:, 0:2], ACT.Sqrt).then_inc(rooted, 1)
                    if out_dram is not None:
                        for t in range(TT):
                            act.wait_ge(ready, t + 1)
                            act.dma_start(out_dram[:, t, :], y[:, t, :]).then_inc(stored, 16)
                        act.wait_ge(stored, 16 * TT)
                    if dst is not None:
                        drain(act, "act", lambda out, src: nc.scalar.activation(out, src, ACT.Copy))

                @block.vector
                def _(dve):
                    ch = Chain(dve, steps)
                    ch.step(nc.vector.tensor_tensor_reduce(
                        out=y[:, 0, :], in0=x[:, 0, :], in1=x[:, 0, :], scale=1.0, scalar=0.0,
                        op0=ALU.mult, op1=ALU.add, accum_out=stat[:, 0:1]))
                    dve.wait_ge(half_sum, 1)
                    nc.vector.tensor_scalar(stat[:, 0:2], stat[:, 0:2], 1.0 / D, 1e-6, ALU.mult, ALU.add).then_inc(summed, 1)
                    dve.wait_ge(summed, 1)
                    dve.wait_ge(landed, 16)
                    if modulate is not None:
                        ch.step(nc.vector.scalar_tensor_tensor(out=g[:], in0=modulate[1], scalar=1.0, in1=g[:],
                                                               op0=ALU.add, op1=ALU.mult))
                    self.inverse_root(dve, ch, rooted, 1, stat[:, 0:2], stat[:, 2:4], stat[:, 4:6])
                    for t in range(TT):
                        last = nc.vector.scalar_tensor_tensor(out=done[:, t, :], in0=x[:, t, :], scalar=stat[:, 2 + t:3 + t],
                                                              in1=g[:], op0=ALU.mult, op1=ALU.mult)
                        if modulate is not None:
                            ch.step(last)
                            last = nc.vector.tensor_tensor(y[:, t, :], y[:, t, :], modulate[0], ALU.add)
                        last.then_inc(ready, 1)
                    dve.wait_ge(ready, TT)
                    if dst is not None:
                        drain(dve, "dve", nc.vector.tensor_copy)

                if dst is not None:
                    @block.tensor
                    def _(pe):
                        for t in range(TT):
                            pe.wait_ge(ready, t + 1)
                            for b in range(4):
                                for c in range(2):
                                    mm = nc.tensor.transpose(self.psum[:, b, c * S + t * P:c * S + (t + 1) * P],
                                                             y[:, t, bass.DynSlice(2 * b + c, P, DC)], self.ident[:, :])
                                if t == TT - 1:
                                    mm.then_inc(turned, 1)

    def norm_features(self, name, x, dst, gain_dram):
        nc, ps = self.nc, self.psum
        with Stage(nc, name) as st:
            g, stat, sq = st.sbuf("gain", [P, DC]), st.sbuf("stat", [P, 8]), st.sbuf("square", [P, TT, D])
            diag, factor = st.sbuf("diagonal", [P, TT, P]), st.sbuf("factor", [P, S])
            landed, summed, rooted, diag_made, turned, spread, steps, half_sum = (st.sem(s) for s in (
                "gain_landed", "summed", "rooted", "diagonal_made", "turned", "factors_spread", "dve_steps", "half_summed"))
            ones = self.strict[:, 0, P:S]
            with nc.Block() as block:
                self.weight_loads(block, name)

                @block.tensor
                def _(pe):
                    for c in range(DC):
                        for t in range(TT):
                            o = (c % 2) * S + t * P
                            mm = nc.tensor.transpose(ps[:, c // 2, o:o + P], x[:, t, bass.DynSlice(c, P, DC)], self.ident[:, :])
                    mm.then_inc(turned, 1)
                    pe.wait_ge(diag_made, 2)
                    nc.tensor.matmul(ps[:, 4, 0:S], ones, diag[:].rearrange("p t q -> p (t q)"), start=True,
                                     stop=True).then_inc(spread, 1)

                @block.scalar
                def _(act):
                    act.dma_start(g[:], gain_dram.rearrange("(p c) -> p c", p=P)).then_inc(landed, 16)
                    nc.scalar.activation(sq[:, 1, :], x[:, 1, :], ACT.Square, accum_out=stat[:, 1:2]).then_inc(half_sum, 1)
                    nc.scalar.activation(stat[:, 7:8], self.ident[:, 0:1], ACT.Sqrt)
                    act.wait_ge(summed, 1)
                    nc.scalar.activation(stat[:, 2:4], stat[:, 0:2], ACT.Sqrt).then_inc(rooted, 1)

                @block.vector
                def _(dve):
                    v, ch = nc.vector, Chain(dve, steps)
                    ch.step(v.tensor_tensor_reduce(out=sq[:, 0, :], in0=x[:, 0, :], in1=x[:, 0, :], scale=1.0, scalar=0.0,
                                                   op0=ALU.mult, op1=ALU.add, accum_out=stat[:, 0:1]))
                    dve.wait_ge(half_sum, 1)
                    v.tensor_scalar(stat[:, 0:2], stat[:, 0:2], 1.0 / D, 1e-6, ALU.mult, ALU.add).then_inc(summed, 1)
                    dve.wait_ge(summed, 1)
                    self.inverse_root(dve, ch, rooted, 1, stat[:, 0:2], stat[:, 2:4], stat[:, 4:6])
                    for t in range(TT):
                        v.tensor_scalar(diag[:, t, :], self.ident[:], stat[:, 2 + t:3 + t], None, ALU.mult).then_inc(diag_made, 1)
                    dve.wait_ge(spread, 1)
                    ch.step(v.tensor_copy(factor[:], ps[:, 4, 0:S]))
                    dve.wait_ge(landed, 16)
                    dve.wait_ge(turned, 1)
                    for c in range(DC):
                        o = (c % 2) * S
                        last = v.scalar_tensor_tensor(out=dst[:, c, :], in0=ps[:, c // 2, o:o + S], scalar=g[:, c:c + 1],
                                                      in1=factor[:], op0=ALU.mult, op1=ALU.mult)
                        last.then_inc(steps, 1)
                    dve.wait_ge(steps, ch.n + DC)

    def to_features(self, key, item_chunks, actT, nk, m0, dst, engine, first=True, last=True, func=None, cols=P):
        nc = self.nc

        def mms(bank, wv, xT):
            return [(bank[0:cols, j * S:(j + 1) * S],
                     [(wv[:, k, m * cols:(m + 1) * cols], xT[:, k, :]) for k in range(nk)])
                    for j, m in enumerate(m0)]

        def drain(eng, bank, chain):
            src = bank[0:cols, 0:len(m0) * S].rearrange("p (c s) -> p c s", c=len(m0))
            if engine == "act":
                return nc.scalar.activation(dst, src, func or ACT.Copy)
            return nc.vector.tensor_copy(dst, src)
        return dict(key=key, operand=actT, mms=mms, engine=engine, drain=drain, first=first, last=last)

    def to_tokens(self, key, actT, nk, c0, ncols, dst, engine, first=True, last=True):
        nc = self.nc

        def mms(bank, wv, xT):
            return [(bank[:, t * 256:t * 256 + ncols],
                     [(xT[:, k, t * P:(t + 1) * P], wv[:, k, c0:c0 + ncols]) for k in range(nk)])
                    for t in range(TT)]

        def drain(eng, bank, chain):
            src = bank.rearrange("p (t n) -> p t n", t=TT)[:, :, 0:ncols]
            if engine == "act":
                return nc.scalar.activation(dst, src, ACT.Copy)
            return nc.vector.tensor_copy(dst, src)
        return dict(key=key, operand=actT, mms=mms, engine=engine, drain=drain, first=first, last=last)

    def project_z(self):
        nc = self.nc
        L = lambda n, s: self.keep(n, s, layer=True)
        self.qT, self.kT, self.iqT = L("qT", [P, 4, S]), L("kT", [P, 4, S]), L("iqT", [P, 4, S])
        self.v, self.ikT, self.iw = L("v_tokens", [P, TT, 512]), L("ikT", [P, S]), L("iw", [P, TT, IH])
        self.ga, self.gr = L("gate_attn", [P, DC, S]), L("gate_rwkv", [P, DC, S])
        u = []

        def mms_ik(bank, wv, _):
            return [(bank[32 * r:32 * r + 32, 0:S], [(wv[:, k, 0:ID], self.hT[:, k, :]) for k in range(DC)])
                    for r in range(4)]

        def drain_ik(eng, bank, chain):
            return nc.vector.tensor_copy(self.ikT[:, :], bank[:, 0:S])
        u.append(dict(key=("w_ikw", 0), mms=mms_ik, engine="dve", drain=drain_ik, last=False))
        u.append(self.to_tokens(("w_ikw", 0), self.hT, DC, ID, IH, self.iw[:, :, :], "dve", first=False))
        for nm, dst in (("w_q", self.qT), ("w_k", self.kT)):
            for i in range(2):
                u.append(self.to_features((nm, i), 2, self.hT, DC, (0, 1), dst[:, 2 * i:2 * i + 2, :], ("act", "dve")[i]))
        for i in range(2):
            u.append(self.to_tokens(("w_v", i), self.hT, DC, 0, 256, self.v[:, :, i * 256:(i + 1) * 256], ("act", "dve")[i]))
        for i in range(2):
            u.append(self.to_features(("w_iq", i), 2, self.hT, DC, (0, 1), self.iqT[:, 2 * i:2 * i + 2, :], ("act", "dve")[i]))

        self.products("z", u)

    def rwkv(self):
        nc, col = self.nc, self.column
        with ExitStack() as keep:
            def T(name, shape):
                return keep.enter_context(nc.sbuf_tensor("rw_" + name, shape, F32))

            SC = [P, 4, S]
            gate, bonus, A, R, V, yT = (T(n, SC) for n in ("gate", "bonus", "A", "R", "V", "yT"))
            BK = T("BK", [P, 2, 4, S])
            B, K = BK[:, 0], BK[:, 1]
            odd = T("odd_heads", [DH, 4, 4, S])
            pend = T("chunk_decay", [P, 4, NC])
            pall = T("chunk_decay_heads", [DH, 4, 2, NC])
            self.rwkv_prepare(gate, bonus, A, B, K, R, V, odd, pend, pall)

            def half(i, h, t0, t1):
                src = (A, B, K, R)[i]
                return odd[:, (0, 2, 3, 1)[i], h // 2, t0:t1] if h % 2 else src[0:DH, h // 2, t0:t1]

            self.rwkv_chunks(half, B, K, V, BK, odd, pall, gate, bonus, yT)

    def rwkv_prepare(self, gate, bonus, A, B, K, R, V, odd, pend, pall):
        nc, col = self.nc, self.column
        SC = [P, 4, S]
        with ExitStack() as scope:
            z = scope.enter_context(nc.sbuf_tensor("zr", [P, 14, S + 1], F32))
            self.products("zr", [
                self.to_features(("w_zr", i), 2, self.hT, DC, (0, 1), z[:, 2 * i:2 * i + 2, 1:S + 1], ("act", "dve")[i % 2])
                for i in range(7)])
            with Stage(nc, "rwprep") as st:
                decay, iclr = st.sbuf("sig_decay", SC), st.sbuf("iclr", SC)
                cum, t1 = st.sbuf("cum", SC), st.sbuf("t1", SC)
                pp, pprev, pinv = st.sbuf("p", SC), st.sbuf("pprev", SC), st.sbuf("pinv", SC)
                steps, act_go, dve_go, pe_go = st.sem("dve_steps"), st.sem("act_to_dve"), st.sem("dve_to_act"), st.sem("pe_done")
                to_pe, act_steps, moved = st.sem("to_pe"), st.sem("act_steps"), st.sem("odd_moved")
                with nc.Block() as block:
                    self.weight_loads(block, "rwprep")

                    @block.vector
                    def _(dve):
                        ch = Chain(dve, steps)
                        v = nc.vector
                        ch.step(v.memset(z[:, :, 0:1], 0.0))
                        for c in (12, 13, 0, 1, 2, 3, 4, 5, 6, 7, 8, 9, 10, 11):
                            ch.step(v.tensor_tensor(t1[:, c % 4, :], z[:, c, 0:S], z[:, c, 1:S + 1], ALU.subtract))
                            dst = z[:, c, 1:S + 1]
                            last = v.scalar_tensor_tensor(out=dst, in0=t1[:, c % 4, :], scalar=col("tshift_mu", c),
                                                          in1=dst, op0=ALU.mult, op1=ALU.add)
                            last.then_inc(dve_go, 1) if c == 13 else ch.step(last)
                        r, k, vv = z[:, 0:4, 1:S + 1], z[:, 4:8, 1:S + 1], z[:, 8:12, 1:S + 1]
                        ch.step(v.tensor_copy(V[:], vv))
                        for c in range(4):
                            ch.step(v.tensor_scalar(A[:, c, :], z[:, 4 + c, 1:S + 1], col("k_k", c), None, ALU.mult))
                        v.tensor_tensor(t1[:], A[:], A[:], ALU.mult).then_inc(to_pe, 1)
                        dve.wait_ge(act_go, 2)
                        for c in range(4):
                            ch.step(v.tensor_tensor_scan(cum[:, c, :], self.restart[:], decay[:, c, :], 0.0, ALU.mult, ALU.add))
                        v.tensor_tensor(decay[:], cum[:], decay[:], ALU.subtract).then_inc(dve_go, 1)
                        for c in range(4):
                            ch.step(v.tensor_scalar(K[:, c, :], iclr[:, c, :], -1.0, None, ALU.add))
                            ch.step(v.tensor_scalar(K[:, c, :], K[:, c, :], col("k_a", c), 1.0, ALU.mult, ALU.add))
                        ch.step(v.tensor_tensor(K[:], K[:], k, ALU.mult))
                        dve.wait_ge(act_go, 3)
                        ch.step(v.tensor_scalar(t1[:], t1[:], 1e-12, None, ALU.max))
                        ch.step(v.reciprocal(t1[:], t1[:]))
                        ch.step(v.tensor_tensor(A[:], A[:], t1[:], ALU.mult))
                        ch.step(v.tensor_tensor(B[:], A[:], iclr[:], ALU.mult))
                        for c in range(4):
                            last = v.scalar_tensor_tensor(out=t1[:, c, :], in0=z[:, c, 1:S + 1], scalar=col("r_k", c),
                                                          in1=K[:, c, :], op0=ALU.mult, op1=ALU.mult)
                            last.then_inc(to_pe, 1) if c == 3 else ch.step(last)
                        dve.wait_ge(act_go, 6)
                        ch.step(v.scalar_tensor_tensor(out=A[:], in0=A[:], scalar=-1.0, in1=pprev[:], op0=ALU.mult, op1=ALU.mult))
                        ch.step(v.tensor_tensor(B[:], B[:], pinv[:], ALU.mult))
                        ch.step(v.tensor_tensor(K[:], K[:], pinv[:], ALU.mult))
                        ch.step(v.tensor_tensor(R[:], r, pp[:], ALU.mult))
                        ch.step(v.tensor_copy(pall[:, :, 0, :], pp[0:DH, :, C - 1:S:C]))
                        v.tensor_copy(pend[:], pp[:, :, C - 1:S:C]).then_inc(dve_go, 1)
                        dve.wait_ge(pe_go, 5)
                        for b in range(2):
                            last = v.tensor_tensor(bonus[:, 2 * b:2 * b + 2, :],
                                                   self.psum[:, 6 + b, :].rearrange("p (c s) -> p c s", c=2),
                                                   V[:, 2 * b:2 * b + 2, :], ALU.mult)
                            ch.step(last)

                    @block.tensor
                    def _(pe):
                        ps = self.psum

                        def lora(lo, hi, w0, src_chunk, b0, src=None):
                            for m in range(4):
                                rhs = z[lo:hi, src_chunk, 1:S + 1]
                                mm = nc.tensor.matmul(ps[:, b0 + m // 2, (m % 2) * S:(m % 2 + 1) * S],
                                                      self.wsmall[lo:hi, w0 + m * P:w0 + (m + 1) * P], rhs,
                                                      start=True, stop=True)
                            mm.then_inc(pe_go, 1)
                        pe.wait_ge(act_steps, 2)
                        lora(0, DH, 0, 12, 0)
                        lora(DH, P, 512, 12, 2)
                        lora(0, P, 1024, 13, 4)
                        pe.wait_ge(to_pe, 1)
                        for c in range(4):
                            mm = nc.tensor.matmul(ps[:, 6 + c // 2, (c % 2) * S:(c % 2 + 1) * S], self.blockones[:, :],
                                                  t1[:, c, :], start=True, stop=True)
                        mm.then_inc(pe_go, 1)
                        pe.wait_ge(to_pe, 2)
                        for c in range(4):
                            mm = nc.tensor.matmul(ps[:, 6 + c // 2, (c % 2) * S:(c % 2 + 1) * S], self.blockones[:, :],
                                                  t1[:, c, :], start=True, stop=True)
                        mm.then_inc(pe_go, 1)

                    @block.scalar
                    def _(act):
                        a = nc.scalar
                        chs = 0
                        act.wait_ge(dve_go, 1)
                        a.activation(z[0:DH, 12, 1:S + 1], z[0:DH, 12, 1:S + 1], ACT.Tanh).then_inc(act_steps, 1)
                        a.activation(z[:, 13, 1:S + 1], z[:, 13, 1:S + 1], ACT.Sigmoid).then_inc(act_steps, 1)
                        act.wait_ge(pe_go, 1)
                        for m in range(4):
                            i1 = a.activation(decay[:, m, :], self.psum[:, m // 2, (m % 2) * S:(m % 2 + 1) * S],
                                              ACT.Sigmoid, bias=col("decay_w0", m))
                        i1.then_inc(act_go, 1)
                        act.wait_ge(pe_go, 2)
                        for m in range(4):
                            i1 = a.activation(iclr[:, m, :], self.psum[:, 2 + m // 2, (m % 2) * S:(m % 2 + 1) * S],
                                              ACT.Sigmoid, bias=col("iclr_a0", m))
                        i1.then_inc(act_go, 1)
                        act.wait_ge(pe_go, 3)
                        for b in range(2):
                            a.activation(gate[:, 2 * b:2 * b + 2, :],
                                         self.psum[:, 4 + b, :].rearrange("p (c s) -> p c s", c=2), ACT.Copy)
                        act.wait_ge(pe_go, 4)
                        for b in range(2):
                            i1 = a.activation(t1[:, 2 * b:2 * b + 2, :],
                                              self.psum[:, 6 + b, :].rearrange("p (c s) -> p c s", c=2), ACT.Sqrt)
                        i1.then_inc(act_go, 1)
                        act.wait_ge(dve_go, 2)
                        a.activation(pprev[:], decay[:], ACT.Exp, scale=-DECAY).then_inc(act_go, 1)
                        a.activation(pinv[:], cum[:], ACT.Exp, scale=DECAY).then_inc(act_go, 1)
                        a.activation(pp[:], cum[:], ACT.Exp, scale=-DECAY).then_inc(act_go, 1)
                        act.wait_ge(dve_go, 3)
                        for i, src in enumerate((A, R, B, K)):
                            act.dma_start(odd[:, i, :, :], src[DH:P, :, :]).then_inc(moved, 16)
                        act.dma_start(pall[:, :, 1, :], pend[DH:P, :, :]).then_inc(moved, 16)
                        act.wait_ge(moved, 80)

    def rwkv_chunks(self, half, B, K, V, BK, odd, pall, gate, bonus, yT):
        nc = self.nc
        W = QH * DH
        with Stage(nc, "rwchunk") as st:
            tok, pairs = st.sbuf("tokens", [P, 3, 2, W]), st.sbuf("pairs", [P, 3, 2, W])
            LT, XT = st.sbuf("L_T", [P, 2, QH * P]), st.sbuf("inverse_T", [P, 2, QH * P])
            X = BK[:].rearrange("p i c s -> p i (c s)")
            t1 = [buf[:].rearrange("p c s -> p (c s)") for buf in (V, yT)]
            ps = self.psum
            filled, act_done, steps = st.sem("filled"), st.sem("act_done"), st.sem("dve_steps")
            dve_done, lm_done, t1_done = st.sem("dve_done"), st.sem("level_done"), st.sem("t1_done")

            def H(ap, h):
                return ap[:, h * DH:(h + 1) * DH]

            toks = [("lt", b, q) for q in range(2) for b in range(2)] + [("tok", i, q) for i in range(3) for q in range(2)]
            pair_jobs = [("pair", (i, b), q) for q in range(2) for i in range(3) for b in range(2)]
            jobs = toks[:4]
            for j, job in enumerate(pair_jobs):
                jobs += [job] + ([toks[4 + j // 2]] if j % 2 else [])
            order, count = [], {"act": 0, "dve": 0}
            for kind, *_ in jobs:
                who, n = ("dve", 2) if kind == "pair" else ("act", 1)
                count[who] += n
                order.append(({"act": act_done, "dve": dve_done}[who], count[who]))
            kinds = ((2, 0, 0), (1, 3, 1), (2, 3, 1))
            with nc.Block() as block:
                self.weight_loads(block, "rwchunk1")

                @block.tensor
                def _(pe):
                    for j, (kind, i, q) in enumerate(jobs):
                        if j >= 8:
                            pe.wait_ge(*order[j - 8])
                        if kind == "tok":
                            for c in range(4):
                                mm = nc.tensor.transpose(ps[:, j % 8, c * P:(c + 1) * P], (B, K, V)[i][:, c, q * P:(q + 1) * P],
                                                         self.ident[:, :])
                        else:
                            lt, rt, b = (1, 0, i) if kind == "lt" else (*kinds[i[0]][:2], i[1])
                            for h in range(4):
                                mm = nc.tensor.matmul(ps[:, j % 8, h * P:(h + 1) * P], half(lt, 4 * b + h, q * P, (q + 1) * P),
                                                      half(rt, 4 * b + h, q * P, (q + 1) * P), start=True, stop=True)
                        mm.then_inc(filled, 1)

                @block.scalar
                def _(act):
                    for j, (kind, i, q) in enumerate(jobs):
                        if kind != "pair":
                            act.wait_ge(filled, j + 1)
                            dst = tok[:, i, q, :] if kind == "tok" else LT[:, q, i * 512:(i + 1) * 512]
                            nc.scalar.activation(dst, ps[:, j % 8, :], ACT.Copy).then_inc(act_done, 1)

                @block.vector
                def _(dve):
                    for j, (kind, i, q) in enumerate(jobs):
                        if kind == "pair":
                            dve.wait_ge(filled, j + 1)
                            i, b = i
                            for lo in (0, C):
                                rows = slice(lo, lo + C)
                                m = self.pair[rows, kinds[i][2], :].unsqueeze(1).to_broadcast([C, 4, C])
                                nc.vector.tensor_tensor(
                                    pairs[rows, i, q, b * 256:(b + 1) * 256].rearrange("p (h c) -> p h c", h=4),
                                    ps[rows, j % 8, :].rearrange("p (h c) -> p h c", h=4)[:, :, lo:lo + C], m,
                                    ALU.mult).then_inc(dve_done, 1)
                    dve.wait_ge(dve_done, 2 * len(pair_jobs))

            LEV = 6
            K_ALL, K_X = 2 * (LEV - 1), 2 * (LEV - 2)
            xt_made, x_turned, x_made = st.sem("xt_made"), st.sem("x_turned"), st.sem("x_made")
            lx, xlx, xlx_t, xdone, xtdone = (st.sem(s) for s in ("lx_filled", "xlx_filled", "xlx_T_filled", "x_done", "x_T_done"))
            heads = lambda ap: ap.rearrange("p (h c) -> p h c", h=QH)
            both = lambda b: ps[:, b:b + 2, :].rearrange("p b n -> p (b n)")
            B128 = lambda ap, h: ap[:, h * P:(h + 1) * P]
            with ExitStack() as scope, nc.Block() as block:
                lm = scope.enter_context(nc.sbuf_tensor("rw_level_matrix", [P, 2, QH * P], F32))
                self.weight_loads(block, "rwchunk2")

                def product(b, a, x, sem):
                    for h in range(QH):
                        o = (h % 4) * P
                        mm = nc.tensor.matmul(ps[:, b + h // 4, o:o + P], B128(a, h), B128(x, h), start=True, stop=True)
                    mm.then_inc(sem, 1)

                @block.tensor
                def _(pe):
                    for q in range(2):
                        pe.wait_ge(xt_made, q + 1)
                        for h in range(QH):
                            o = (h % 4) * P
                            mm = nc.tensor.transpose(ps[:, 4 + 2 * q + h // 4, o:o + P], B128(XT[:, q, :], h), self.ident[:, :])
                        mm.then_inc(x_turned, 1)
                    pe.wait_ge(x_made, 2)
                    for k0 in range(0, K_ALL, 2):
                        for k in (k0, k0 + 1):
                            pe.wait_ge(lm_done, k + 1)
                            if k >= 2:
                                pe.wait_ge(xdone, k - 1)
                            product(2 * (k % 2), lm[:, k % 2, :], X[:, k % 2, :], lx)
                        for k in (k0, k0 + 1):
                            q = k % 2
                            pe.wait_ge(t1_done, k + 1)
                            if k < K_X:
                                if k >= 2:
                                    pe.wait_ge(xtdone, k - 1)
                                if k >= 1:
                                    pe.wait_ge(xdone, k)
                                product(4, XT[:, q, :], t1[q], xlx)
                            if k >= 1:
                                pe.wait_ge(xtdone, k)
                            product(6, t1[q], XT[:, q, :], xlx_t)

                @block.scalar
                def _(act):
                    for q in range(2):
                        act.wait_ge(x_turned, q + 1)
                        nc.scalar.activation(X[:, q, :], both(4 + 2 * q), ACT.Copy).then_inc(x_made, 1)
                    for k in range(K_ALL):
                        act.wait_ge(lx, k + 1)
                        if k >= 2:
                            act.wait_ge(xlx_t, k - 1)
                        nc.scalar.activation(t1[k % 2], both(2 * (k % 2)), ACT.Copy).then_inc(t1_done, 1)

                @block.vector
                def _(dve):
                    v = nc.vector
                    ch = Chain(dve, steps)
                    mask = lambda lev: self.levels[:, lev, :].unsqueeze(1).to_broadcast([P, QH, P])
                    for q in range(2):
                        ch.step(v.tensor_tensor(heads(XT[:, q, :]), heads(LT[:, q, :]), mask(0), ALU.mult))
                        v.tensor_tensor(heads(XT[:, q, :]), heads(XT[:, q, :]),
                                        self.ident[:].unsqueeze(1).to_broadcast([P, QH, P]), ALU.add).then_inc(xt_made, 1)

                    def level(k):
                        if k >= 2:
                            dve.wait_ge(lx, k - 1)
                        v.tensor_tensor(heads(lm[:, k % 2, :]), heads(LT[:, k % 2, :]), mask(1 + k // 2), ALU.mult).then_inc(lm_done, 1)

                    level(0)
                    level(1)
                    dve.wait_ge(x_made, 2)
                    for k in range(K_ALL):
                        q = k % 2
                        if k + 2 < K_ALL:
                            level(k + 2)
                        if k < K_X:
                            dve.wait_ge(xlx, k + 1)
                            if k >= 2:
                                dve.wait_ge(xdone, k - 1)
                            v.tensor_tensor(X[:, q, :], X[:, q, :], both(4), ALU.add).then_inc(xdone, 1)
                        dve.wait_ge(xlx_t, k + 1)
                        v.tensor_tensor(XT[:, q, :], XT[:, q, :], both(6), ALU.add).then_inc(xtdone, 1)
                    dve.wait_ge(xtdone, K_ALL)

            with Stage(nc, "rwseq") as s2:
                state, rhs, sa = s2.sbuf("state", [DH, W]), s2.sbuf("rhs", [P, W]), s2.sbuf("sa", [P, W])
                Y = LT[0:DH, 0, :].rearrange("p (n w) -> p n w", n=2)
                pe_done, dve_d, act_d = s2.sem("pe_done"), s2.sem("dve_done"), s2.sem("act_done")
                free_parts, state_part = s2.sem("free_parts"), s2.sem("state_part")
                moved = [s2.sem("even_chunks_moved"), s2.sem("odd_chunks_moved")]
                with nc.Block() as block:
                    self.weight_loads(block, "rwseq")

                    @block.tensor
                    def _(pe):
                        low = lambda n: C * (n % 2)

                        def of(t, i, n):
                            return t[low(n):low(n) + C, i, n // 2, :]

                        def place(n, kind):
                            at = low(n) if kind == 0 else 0
                            return ps[at:at + C, kind + 4 * (n % 2), :]

                        def free(n, kind):
                            if n == NC:
                                return
                            bank = place(n, kind)
                            if kind == 3 and n >= 2:
                                pe.wait_ge(act_d, n - 1)
                            for h in range(QH):
                                value = of(tok, 2, n)
                                a, x = ((of(pairs, 0, n), value), None, (of(tok, 1, n), value), (value, of(pairs, 2, n)))[kind]
                                mm = nc.tensor.matmul(H(bank, h), H(a, h), H(x, h), start=(h == 0), stop=False, skip_group_check=True)
                            mm.then_inc(free_parts, 1)

                        def with_state(n, kind, a, x, stop=True):
                            bank = place(n, kind)
                            for h in range(QH):
                                mm = nc.tensor.matmul(H(bank, h), a(h), x(h), start=False, stop=stop, skip_group_check=True)
                            return mm

                        for kind in (0, 2, 3):
                            free(0, kind)
                        for n in range(NC):
                            t0, t1_ = n * C, (n + 1) * C
                            S_ = lambda h: H(state[:], h)
                            pe.wait_ge(dve_d, 4 * n + 1)
                            pe.wait_ge(free_parts, 3 * n + 3)
                            with_state(n, 0, lambda h: half(0, h, t0, t1_), S_).then_inc(pe_done, 1)
                            with_state(n, 3, S_, lambda h: half(3, h, t0, t1_), stop=False).then_inc(state_part, 1)
                            free(n + 1, 0)
                            pe.wait_ge(dve_d, 4 * n + 2)
                            lo = low(n)
                            for h in range(QH):
                                mm = nc.tensor.matmul(H(ps[lo:lo + C, 1, :], h), XT[lo:lo + C, n // 2, h * P + lo:h * P + lo + C],
                                                      H(rhs[lo:lo + C, :], h), start=True, stop=True)
                            mm.then_inc(pe_done, 1)
                            free(n + 1, 2)
                            pe.wait_ge(dve_d, 4 * n + 3)
                            with_state(n, 2, lambda h: H(of(tok, 0, n), h), lambda h: H(sa[lo:lo + C, :], h)).then_inc(pe_done, 1)
                            pe.wait_ge(state_part, n + 1)
                            with_state(n, 3, lambda h: H(sa[lo:lo + C, :], h), lambda h: H(of(pairs, 1, n), h)).then_inc(pe_done, 1)
                            free(n + 1, 3)

                    @block.vector
                    def _(dve):
                        v = nc.vector
                        v.memset(state[:], 0.0).then_inc(dve_d, 1)
                        for n in range(NC):
                            dve.wait_ge(pe_done, 4 * n + 1)
                            lo = C * (n % 2)
                            v.tensor_copy(rhs[lo:lo + C, :], ps[lo:lo + C, 4 * (n % 2), :]).then_inc(dve_d, 1)
                            dve.wait_ge(pe_done, 4 * n + 2)
                            v.tensor_copy(sa[lo:lo + C, :], ps[lo:lo + C, 1, :]).then_inc(dve_d, 1)
                            dve.wait_ge(pe_done, 4 * n + 3)
                            v.tensor_tensor(state[:], state[:], ps[0:C, 2 + 4 * (n % 2), :], ALU.add).then_inc(dve_d, 1)
                            dve.wait_ge(dve_d, 4 * n + 4)
                            sv = state[:].rearrange("p (h e) -> p h e", h=QH)
                            v.tensor_tensor(sv, sv, pall[:, :, :, n:n + 1].rearrange("p c two n -> p (c two) n").to_broadcast(
                                [DH, QH, DH]), ALU.mult).then_inc(dve_d, 1)

                    @block.scalar
                    def _(act):
                        for n in range(NC):
                            act.wait_ge(pe_done, 4 * n + 4)
                            if n >= 2:
                                act.wait_ge(moved[n % 2], 32 * (n // 2))
                            nc.scalar.activation(Y[:, n % 2, :], ps[0:C, 3 + 4 * (n % 2), :], ACT.Copy).then_inc(act_d, 1)
                            act.wait_ge(act_d, n + 1)
                            yv = Y[:, n % 2, :].rearrange("p (c two s) -> p c two s", two=2, s=C)
                            act.dma_start(yT[0:DH, :, n * C:(n + 1) * C], yv[:, :, 0, :]).then_inc(moved[n % 2], 16)
                            act.dma_start(yT[DH:P, :, n * C:(n + 1) * C], yv[:, :, 1, :]).then_inc(moved[n % 2], 16)
                        act.wait_ge(moved[0], 16 * NC)
                        act.wait_ge(moved[1], 16 * NC)

        with Stage(nc, "rwgn") as s2:
            mean, sq = s2.sbuf("mean", [P, 4, S]), s2.sbuf("sq", [P, 4, S])
            ps = self.psum
            with nc.Block() as block:
                self.weight_loads(block, "rwnorm")
                pe2, dve2, act2, st2 = s2.sem("pe2"), s2.sem("dve2"), s2.sem("act2"), s2.sem("steps2")

                @block.tensor
                def _(pe):
                    for c in range(4):
                        mm = nc.tensor.matmul(ps[:, c // 2, (c % 2) * S:(c % 2 + 1) * S], self.blockones[:, :], yT[:, c, :],
                                              start=True, stop=True)
                    mm.then_inc(pe2, 1)
                    pe.wait_ge(dve2, 1)
                    for c in range(4):
                        mm = nc.tensor.matmul(ps[:, 2 + c // 2, (c % 2) * S:(c % 2 + 1) * S], self.blockones[:, :], sq[:, c, :],
                                              start=True, stop=True)
                    mm.then_inc(pe2, 1)

                @block.vector
                def _(dve):
                    v, ch = nc.vector, Chain(dve, st2)
                    dve.wait_ge(pe2, 1)
                    for b in range(2):
                        ch.step(v.scalar_tensor_tensor(out=yT[:, 2 * b:2 * b + 2, :].rearrange("p c s -> p (c s)"),
                                                       in0=ps[:, b, :], scalar=-1.0 / DH,
                                                       in1=yT[:, 2 * b:2 * b + 2, :].rearrange("p c s -> p (c s)"),
                                                       op0=ALU.mult, op1=ALU.add))
                    v.tensor_tensor(sq[:], yT[:], yT[:], ALU.mult).then_inc(dve2, 1)
                    dve.wait_ge(pe2, 2)
                    for b in range(2):
                        last = v.tensor_scalar(mean[:, 2 * b:2 * b + 2, :].rearrange("p c s -> p (c s)"), ps[:, 2 + b, :],
                                               1.0 / DH, 64e-5, ALU.mult, ALU.add)
                        ch.step(last) if b == 0 else last.then_inc(dve2, 1)
                    dve.wait_ge(act2, 1)
                    ch.step(v.reciprocal(mean[:], mean[:]))
                    ch.step(v.tensor_tensor(yT[:], yT[:], mean[:], ALU.mult))
                    for c in range(4):
                        ch.step(v.tensor_scalar(yT[:, c, :], yT[:, c, :], self.column("lnx_g", c), self.column("lnx_b", c),
                                                ALU.mult, ALU.add))
                    ch.step(v.tensor_tensor(yT[:], yT[:], bonus[:], ALU.add))
                    ch.step(v.tensor_tensor(self.rwT[:], yT[:], gate[:], ALU.mult))

                @block.scalar
                def _(act):
                    act.wait_ge(dve2, 2)
                    nc.scalar.activation(mean[:], mean[:], ACT.Sqrt).then_inc(act2, 1)

    def attend(self, name, units, scale, ns=1, neg_lam=None):
        nc, ps = self.nc, self.psum
        n = len(units)
        with Stage(nc, name) as st:
            logit = st.sbuf("logits", [P, 2, ns * TT, S])
            prob = st.sbuf("probs", [P, 2, ns * TT, S])
            pT = st.sbuf("probs_T", [P, 2, TT, S])
            nmax, rsum, rinv = (st.sbuf(x, [P, 2, ns * TT]) for x in ("neg_max", "row_sum", "row_inv"))
            scored, maxed, exped, normed, turned, copied, valued, stored = (st.sem(x) for x in (
                "scored", "maxed", "exped", "normed", "turned", "copied", "valued", "stored"))
            steps = st.sem("dve_steps")
            with nc.Block() as block:
                self.weight_loads(block, name)

                @block.tensor
                def _(pe):
                    for i in range(-1, n + 2):
                        if i + 1 < n:
                            if i >= 1:
                                pe.wait_ge(maxed, i)
                            b0 = (i + 1) % 2 * ns
                            for out, pairs in units[i + 1]["scores"]([ps[:, b0 + s, :] for s in range(ns)]):
                                for j, (a, b) in enumerate(pairs):
                                    mm = nc.tensor.matmul(out, a, b, start=(j == 0), stop=(j == len(pairs) - 1))
                            mm.then_inc(scored, 1)
                        if 1 <= i <= n:
                            u = i - 1
                            pe.wait_ge(normed, u + 1)
                            if u >= 2:
                                pe.wait_ge(copied, u - 1)
                            for kt in range(TT):
                                for t in range(TT):
                                    mm = nc.tensor.transpose(ps[:, 4 + u % 2, kt * S + t * P:kt * S + (t + 1) * P],
                                                             prob[:, u % 2, t, kt * P:(kt + 1) * P], self.ident[:, :])
                            mm.then_inc(turned, 1)
                        if i >= 2:
                            u = i - 2
                            pe.wait_ge(copied, u + 1)
                            if u >= 2:
                                pe.wait_ge(stored, u - 1)
                            for out, pairs in units[u]["values"](ps[:, 6 + u % 2, :], pT[:, u % 2]):
                                for j, (a, b) in enumerate(pairs):
                                    mm = nc.tensor.matmul(out, a, b, start=(j == 0), stop=(j == len(pairs) - 1))
                            mm.then_inc(valued, 1)

                @block.vector
                def _(dve):
                    v, ch = nc.vector, Chain(dve, steps)
                    for i in range(n + 2):
                        if i < n:
                            b = i % 2
                            dve.wait_ge(scored, i + 1)
                            if i >= 2:
                                dve.wait_ge(exped, i - 1)
                            for s in range(ns):
                                src = ps[:, b * ns + s, :].rearrange("p (t k) -> p t k", t=TT)
                                dst = logit[:, b, s * TT:(s + 1) * TT, :]
                                if units[i]["bias"] is None:
                                    ch.step(v.tensor_scalar(dst, src, scale, None, ALU.mult))
                                else:
                                    ch.step(v.scalar_tensor_tensor(out=dst, in0=src, scalar=scale, in1=units[i]["bias"],
                                                                   op0=ALU.mult, op1=ALU.add))
                            v.tensor_reduce(nmax[:, b, :], logit[:, b, :, :], AX.X, ALU.max, negate=True).then_inc(maxed, 1)
                        if 1 <= i <= n:
                            u = i - 1
                            b = u % 2
                            dve.wait_ge(exped, u + 1)
                            ch.step(v.reciprocal(rinv[:, b, :], rsum[:, b, :]))
                            inv = rinv[:, b, :].unsqueeze(2).to_broadcast([P, ns * TT, S])
                            last = v.tensor_tensor(prob[:, b], prob[:, b], inv, ALU.mult)
                            if ns == 2:
                                ch.step(last)
                                last = v.scalar_tensor_tensor(out=prob[:, b, 0:TT, :], in0=prob[:, b, TT:, :], scalar=neg_lam,
                                                              in1=prob[:, b, 0:TT, :], op0=ALU.mult, op1=ALU.add)
                            last.then_inc(normed, 1)
                        if i >= 2:
                            u = i - 2
                            dve.wait_ge(valued, u + 1)
                            dst, src = units[u]["result"](ps[:, 6 + u % 2, :])
                            v.tensor_copy(dst, src).then_inc(stored, 1)
                    dve.wait_ge(stored, n)

                @block.scalar
                def _(act):
                    for i in range(n + 1):
                        if i < n:
                            b = i % 2
                            act.wait_ge(maxed, i + 1)
                            if i >= 2:
                                act.wait_ge(turned, i - 1)
                            for t in range(ns * TT):
                                last = nc.scalar.activation(prob[:, b, t, :], logit[:, b, t, :], ACT.Exp,
                                                            bias=nmax[:, b, t:t + 1], accum_out=rsum[:, b, t:t + 1])
                            last.then_inc(exped, 1)
                        if i >= 1:
                            u = i - 1
                            act.wait_ge(turned, u + 1)
                            if u >= 2:
                                act.wait_ge(valued, u - 1)
                            nc.scalar.activation(pT[:, u % 2].rearrange("p k q -> p (k q)"), ps[:, 4 + u % 2, :],
                                                 ACT.Copy).then_inc(copied, 1)

    def sparse_attention(self):
        nc, ps = self.nc, self.psum
        L = lambda n, s: self.keep(n, s, layer=True)
        self.attnT = L("attn_out", [P, 4, S])
        rows = nc.dram_tensor("bias_rows", [QH, 2 * S], F32).ap()
        with Stage(nc, "dsa_keep") as keep:
            bias = keep.sbuf("bias", [P, QH, TT, S])
            with Stage(nc, "dsa") as st:
                rw = st.sbuf("weighted", [P, IH, S])
                shifted = st.sbuf("shifted_bias", [P, QH, TT, S])
                work, msk = st.sbuf("work", [P, TT, S]), st.sbuf("outside", [P, TT, S])
                best = st.sbuf("best", [P, TT, 8])
                brow = st.sbuf("bias_row", [QH, 2 * S])
                vals, vout, stored, landed = st.sem("bias_values"), st.sem("bias_out"), st.sem("stored"), st.sem("landed")
                dots, drained, steps = st.sem("dots"), st.sem("drained"), st.sem("steps")
                w, gates = self.w, [("w_ga", i, self.ga) for i in range(4)] + [("w_gr", i, self.gr) for i in range(4)]
                base = w.n_filled
                for g, (name, i, _) in enumerate(gates):
                    w.done_at[w.index[(name, i)]] = base + g + 1
                w.n_filled = base + len(gates)
                gated = st.sem("gated")
                with nc.Block() as block:
                    self.weight_loads(block, "dsa")

                    @block.tensor
                    def _(pe):
                        nc.tensor.matmul(ps[0:QH, 0, :], self.relb[:, :], self.bucket[:, :], start=True, stop=True).then_inc(vals, 1)
                        pe.wait_ge(vout, 1)
                        for t in range(TT):
                            for b in range(8):
                                r, qd = b // 4, b % 4
                                if t:
                                    pe.wait_ge(drained, b + 1)
                                for j in range(2):
                                    lo = 32 * qd
                                    mm = nc.tensor.matmul(ps[:, b, j * S:(j + 1) * S],
                                                          self.iqT[lo:lo + 32, 2 * r + j, t * P:(t + 1) * P],
                                                          self.ikT[lo:lo + 32, :], start=True, stop=True)
                                mm.then_inc(dots, 1)
                        for g, (name, i, _) in enumerate(gates):
                            pe.wait_ge(drained, 8 + g + 1)
                            w.arrived(pe, (name, i))
                            wv = w.view((name, i))
                            for j in range(2):
                                for k in range(DC):
                                    mm = nc.tensor.matmul(ps[:, g, j * S:(j + 1) * S], wv[:, k, j * P:(j + 1) * P],
                                                          self.hT[:, k, :], start=(k == 0), stop=(k == DC - 1))
                            mm.then_inc(w.filled, 1)

                    @block.scalar
                    def _(act):
                        act.wait_ge(vout, 1)
                        act.dma_start(rows, brow[:]).then_inc(stored, 16)
                        act.wait_ge(stored, 16)
                        for h in range(QH):
                            src = bass.AP(tensor=rows.tensor, offset=h * 2 * S, ap=[[1, P], [P, TT], [1, S]])
                            act.dma_start(shifted[:, h], src).then_inc(landed, 16)
                        act.wait_ge(landed, 16 * QH)
                        for g, (_, i, dst) in enumerate(gates):
                            act.wait_ge(w.filled, base + g + 1)
                            nc.scalar.activation(dst[:, 2 * i:2 * i + 2, :], ps[:, g, :].rearrange("p (c s) -> p c s", c=2),
                                                 ACT.Sigmoid).then_inc(gated, 1)
                        act.wait_ge(gated, len(gates))

                    @block.vector
                    def _(dve):
                        v, ch = nc.vector, Chain(dve, steps)
                        dve.wait_ge(vals, 1)
                        v.tensor_copy(brow[:], ps[0:QH, 0, :]).then_inc(vout, 1)
                        ch.step(v.tensor_scalar(msk[:], self.causal[:], -1.0, BIG, ALU.add, ALU.mult))
                        for t in range(TT):
                            for b in range(8):
                                r, qd = b // 4, b % 4
                                dve.wait_ge(dots, 8 * t + b + 1)
                                h0 = qd + 8 * r
                                w = self.iw[:, t, h0:h0 + 5:4].unsqueeze(2).to_broadcast([P, 2, S])
                                v.scalar_tensor_tensor(out=rw[:, h0:h0 + 5:4, :], in0=ps[:, b, :].rearrange("p (j s) -> p j s", j=2),
                                                       scalar=0.0, in1=w, op0=ALU.max, op1=ALU.mult).then_inc(drained, 1)
                            dve.wait_ge(drained, 8 * t + 8)
                            ch.step(v.tensor_reduce(work[:, t, :], rw[:].rearrange("p h s -> p s h"), AX.X, ALU.add))
                        ch.step(v.scalar_tensor_tensor(out=work[:], in0=work[:], scalar=IH ** -0.5 * ID ** -0.5,
                                                       in1=self.causal[:], op0=ALU.mult, op1=ALU.mult))
                        ch.step(v.tensor_tensor(work[:], work[:], msk[:], ALU.add))
                        for _ in range(TOPK // 8):
                            for t in range(TT):
                                ch.step(v.max(best[:, t, :], work[:, t, :]))
                                ch.step(v.match_replace(work[:, t, :], best[:, t, :], work[:, t, :], TAKEN))
                        ch.step(v.scalar_tensor_tensor(out=work[:], in0=work[:], scalar=TAKEN / 1.5, in1=self.causal[:],
                                                       op0=ALU.is_lt, op1=ALU.mult))
                        ch.step(v.tensor_scalar(work[:], work[:], -1.0, BIG, ALU.add, ALU.mult))
                        dve.wait_ge(landed, 16 * QH)
                        for h in range(QH):
                            ch.step(v.tensor_tensor(bias[:, h], shifted[:, h, :, ::-1], work[:], ALU.add))
            units = []
            for h in range(QH):
                lo = DH * (h % 2)
                units.append(dict(
                    scores=lambda banks, h=h, lo=lo: [
                        (banks[0][:, t * S:(t + 1) * S],
                         [(self.qT[lo:lo + DH, h // 2, t * P:(t + 1) * P], self.kT[lo:lo + DH, h // 2, :])]) for t in range(TT)],
                    bias=bias[:, h],
                    values=lambda bank, pT, h=h, lo=lo: [
                        (bank[lo:lo + DH, 0:S], [(self.v[:, kt, h * DH:(h + 1) * DH], pT[:, kt, :]) for kt in range(TT)])],
                    result=lambda bank, h=h, lo=lo: (self.attnT[lo:lo + DH, h // 2, :], bank[lo:lo + DH, 0:S])))
            self.attend("dsa_heads", units, DH ** -0.5)

    def mix_and_project(self):
        nc = self.nc
        units = []
        with Stage(nc, "mixtmp") as st:
            tmp = st.sbuf("tmp", [P, 512])
            for src, gate, key in ((self.attnT, self.ga, "w_attn_br"), (self.rwT, self.gr, "w_rwkv_br")):
                for i in range(2):
                    for j in range(2):
                        m = 4 * i + 2 * j

                        def drain(eng, bank, chain, m=m, gate=gate, key=key):
                            b = bank.rearrange("p (c s) -> p c s", c=2)
                            t = tmp[:].rearrange("p (c s) -> p c s", c=2)
                            if key == "w_attn_br":
                                return nc.vector.tensor_tensor(self.hT[:, m:m + 2, :], b, gate[:, m:m + 2, :], ALU.mult)
                            chain.step(nc.vector.tensor_tensor(t, b, gate[:, m:m + 2, :], ALU.mult))
                            return nc.vector.tensor_tensor(self.hT[:, m:m + 2, :], self.hT[:, m:m + 2, :], t, ALU.add)
                        u = self.to_features((key, i), 4, src, 4, (2 * j, 2 * j + 1), None, "dve", first=(j == 0), last=(j == 1))
                        u["drain"] = drain
                        units.append(u)
            self.products("mix", units)
        self.residual("out", "w_out", self.hT, DC, 0, gate=self.mod_row(0))

    def residual(self, name, key, srcT, nk, c0, gate=None):
        nc = self.nc
        with Stage(nc, name + "tmp") as st:
            tmp = st.sbuf("tmp", [P, TT, 256])
            units = []
            for i in range(4):
                u = self.to_tokens((key, i), srcT, nk, 0, 256, None, "dve")

                def drain(eng, bank, chain, i=i):
                    b = bank.rearrange("p (t n) -> p t n", t=TT)
                    x = self.x[:, :, i * 256:(i + 1) * 256]
                    if gate is None:
                        return nc.vector.tensor_tensor(x, x, b, ALU.add)
                    g = gate[:, i * 256:(i + 1) * 256].unsqueeze(1).to_broadcast([P, TT, 256])
                    chain.step(nc.vector.tensor_tensor(tmp[:], b, g, ALU.mult))
                    return nc.vector.tensor_tensor(x, x, tmp[:], ALU.add)
                u["drain"] = drain
                units.append(u)
            self.products(name, units)

    def route(self):
        nc, ps = self.nc, self.psum
        NG, EG = 8, NE // 8
        self.comb = nc.dram_tensor("combine_rows", [NE, S], F32).ap()
        with Stage(nc, "route") as st:
            score, choice = st.sbuf("score", [P, TT, NE]), st.sbuf("choice", [P, TT, NE])
            sel = st.sbuf("selected", [P, TT, NE])
            top = st.sbuf("group_top", [P, TT, NG, 8])
            cand, best, repl = st.sbuf("cand", [P, TT, 16]), st.sbuf("best", [P, TT, 8]), st.sbuf("repl", [P, TT, 8])
            gsel, tot = st.sbuf("group_sel", [P, TT, NG]), st.sbuf("total", [P, TT])
            combT = st.sbuf("combT", [NE, S])
            u = self.to_tokens(("router_w", 0), self.hT, DC, 0, NE, score[:], "act")
            u["drain"] = lambda eng, bank, chain: nc.scalar.activation(
                score[:], bank.rearrange("p (t n) -> p t n", t=TT)[:, :, 0:NE], ACT.Sigmoid)
            self.products("router", [u])
            steps, ready, turned, copied, stored = (st.sem(x) for x in ("steps", "ready", "turned", "copied", "stored"))
            with nc.Block() as block:
                self.weight_loads(block, "route")

                @block.vector
                def _(dve):
                    v, ch = nc.vector, Chain(dve, steps)
                    ch.step(v.tensor_tensor(choice[:], score[:], self.rbias[:].unsqueeze(1).to_broadcast([P, TT, NE]), ALU.add))
                    ch.step(v.memset(cand[:], -BIG))
                    ch.step(v.memset(repl[:], -BIG))
                    for t in range(TT):
                        for g in range(NG):
                            ch.step(v.max(top[:, t, g, :], choice[:, t, g * EG:(g + 1) * EG]))
                    ch.step(v.tensor_tensor(cand[:, :, 0:NG], top[:, :, :, 0], top[:, :, :, 1], ALU.add))
                    for t in range(TT):
                        ch.step(v.max(best[:, t, :], cand[:, t, 0:NG]))
                    ch.step(v.tensor_copy(repl[:, :, 0:4], best[:, :, 0:4]))
                    for t in range(TT):
                        ch.step(v.match_replace(cand[:, t, :], repl[:, t, :], cand[:, t, :], TAKEN))
                    ch.step(v.tensor_scalar(gsel[:], cand[:, :, 0:NG], TAKEN / 1.5, None, ALU.is_lt))
                    gb = gsel[:].rearrange("p t g -> p (t g)").unsqueeze(2).to_broadcast([P, TT * NG, EG])
                    c3 = choice[:].rearrange("p t (g e) -> p (t g) e", e=EG)
                    s3 = sel[:].rearrange("p t (g e) -> p (t g) e", e=EG)
                    ch.step(v.tensor_tensor(c3, c3, gb, ALU.mult))
                    ch.step(v.tensor_scalar(gsel[:], gsel[:], -1.0, BIG, ALU.add, ALU.mult))
                    ch.step(v.tensor_tensor(c3, c3, gb, ALU.add))
                    for t in range(TT):
                        ch.step(v.max(best[:, t, :], choice[:, t, :]))
                        ch.step(v.match_replace(sel[:, t, :], best[:, t, :], choice[:, t, :], TAKEN))
                    ch.step(v.scalar_tensor_tensor(out=sel[:], in0=sel[:], scalar=TAKEN / 1.5, in1=score[:],
                                                   op0=ALU.is_lt, op1=ALU.mult))
                    ch.step(v.tensor_reduce(tot[:], sel[:], AX.X, ALU.add))
                    ch.step(v.reciprocal(tot[:], tot[:]))
                    ch.step(v.tensor_scalar(tot[:], tot[:], 2.5, None, ALU.mult))
                    v.tensor_tensor(sel[:], sel[:], tot[:].unsqueeze(2).to_broadcast([P, TT, NE]), ALU.mult).then_inc(ready, 1)
                    dve.wait_ge(turned, 1)
                    v.tensor_copy(combT[:], ps[0:NE, 0, 0:S]).then_inc(copied, 1)

                @block.tensor
                def _(pe):
                    pe.wait_ge(ready, 1)
                    for t in range(TT):
                        mm = nc.tensor.transpose(ps[0:NE, 0, t * P:(t + 1) * P], sel[:, t, :], self.ident[:, :])
                    mm.then_inc(turned, 1)

                @block.scalar
                def _(act):
                    act.wait_ge(copied, 1)
                    act.dma_start(self.comb, combT[:]).then_inc(stored, 16)
                    act.wait_ge(stored, 16)

    def experts(self):
        nc, ps, w, d = self.nc, self.psum, self.w, self.dram
        n0, base = w.index[("sh_gate", 0)], w.n_filled
        G = NE // 2
        N = 3 * NE + 3
        for i in range(N):
            w.done_at[n0 + i] = base + i + 1
        w.n_filled = base + N
        after = n0 + N
        down_of = lambda t, e: t[e].rearrange("(c p) n -> p c n", p=P)
        rows_of = lambda t, e: t[e].rearrange("(p c) n -> p c n", p=P)
        with Stage(nc, "moe") as st:
            silu, hid, cb = st.sbuf("silu", [P, 2, EC, S]), st.sbuf("hidden", [P, EC, S]), st.sbuf("combine", [P, 2, S])
            wh, wl = st.sbuf("weights_high", [P, 2, SLOT], FR), st.sbuf("weights_low", [P, 2, SLOT], FR)
            th, tl = st.sbuf("tokens_high", [P, DC, S], FR), st.sbuf("tokens_low", [P, DC, S], FR)
            hh, hl = st.sbuf("hidden_high", [P, 2, EC, S], FR), st.sbuf("hidden_low", [P, 2, EC, S], FR)
            silu_done, scaled, steps = st.sem("silu_done"), st.sem("hidden_scaled"), st.sem("dve_steps")
            th_made, tl_made, wh_made, wl_made, hh_made, hl_made = (st.sem(x) for x in (
                "tokens_high_made", "tokens_low_made", "weights_high_made", "weights_low_made", "hidden_high_made",
                "hidden_low_made"))
            cb_landed = [st.sem("combine_landed_even"), st.sem("combine_landed_odd")]
            y = [[ps[:, 4 + 2 * t + half, :] for half in range(2)] for t in range(TT)]

            def slot(n, chunks):
                return w.slots[:, n % RING, :].rearrange("p (c n) -> p c n", c=chunks)

            with nc.Block() as block:
                @block.sync
                def _(sp):
                    first_free = n0 + RING
                    while w.issued < first_free:
                        w.load(sp, w.issued)
                        w.issued += 1

                    def combine(e, par, free):
                        if free is not None:
                            sp.wait_ge(scaled, free)
                        sp.dma_start(cb[:, par, :], self.comb[e].partition_broadcast(P)).then_inc(cb_landed[par], 16)

                    def turn(g, first=False):
                        for q in range(RING):
                            n = first_free + q
                            e_off, j = divmod(n - n0 - 2, 3)
                            sp.wait_ge(w.filled, 6 * g + w.done_at[n - RING])
                            src = ((rows_of, "exp_gate", 0), (rows_of, "exp_up", 0), (down_of, "exp_down", -1))[j]
                            sp.dma_start(slot(n, 2 if j == 2 else 8),
                                         src[0](d[src[1]][0], 2 * g + e_off + src[2])).then_inc(w.landed[n % RING], 16)
                            if j == 1:
                                combine(2 * g + e_off, e_off % 2, None if first and e_off == 1 else 2 * g + e_off)
                    combine(0, 0, None)
                    turn(0, first=True)
                    with sp.Fori(1, G - 1) as g:
                        turn(g)
                    w.issued = first_free + RING * (G - 1)
                    while w.issued < len(w.items) and w.issued - RING < after:
                        w.load(sp, w.issued)
                        if w.issued == n0 + 2 + 3 * (NE - 1) + 1:
                            combine(NE - 1, 1, NE - 1)
                        w.issued += 1

                def half(t, par, chunks):
                    return t[:, par, :].rearrange("p (c n) -> p c n", c=chunks)

                def pe_up(q, qpar, b):
                    for j in range(2):
                        nc.tensor.wait_ge(wl_made, q + j + 1)
                        h, l = half(wh, (qpar + j) % 2, DC), half(wl, (qpar + j) % 2, DC)
                        for m in range(EC):
                            for k in range(DC):
                                at = slice(m * P, (m + 1) * P)
                                for i, (a, x) in enumerate(((h, th), (h, tl), (l, th))):
                                    mm = nc.tensor.matmul(ps[:, 2 * b + j, m * S:(m + 1) * S], a[:, k, at], x[:, k, :],
                                                          start=(k == 0 and i == 0), stop=(k == DC - 1 and i == 2))
                        mm.then_inc(w.filled, 1)

                def pe_down(q, qpar, b, hidden_at, first=False, last=False):
                    nc.tensor.wait_ge(wl_made, q + 1)
                    nc.tensor.wait_ge(hl_made, hidden_at)
                    h, l = half(wh, qpar, EC), half(wl, qpar, EC)
                    for t in range(TT):
                        at = slice(t * P, (t + 1) * P)
                        for k in range(EC):
                            for i, (a, x) in enumerate(((hh, h), (hh, l), (hl, h))):
                                for half_ in range(2):
                                    mm = nc.tensor.matmul(y[t][half_], a[:, b, k, at], x[:, k, half_ * 512:(half_ + 1) * 512],
                                                          start=(first and k == 0 and i == 0),
                                                          stop=(last and k == EC - 1 and i == 2), skip_group_check=True)
                    mm.then_inc(w.filled, 1)

                @block.tensor
                def _(pe):
                    pe.wait_ge(tl_made, 2)
                    pe_up(0, 0, 0)

                    def turn(g, first=False):
                        pe_up(6 * g + 2, 0, 1)
                        pe_down(6 * g + 4, 0, 0, 2 * g + 1, first=first)
                        pe_up(6 * g + 5, 1, 0)
                        pe_down(6 * g + 7, 1, 1, 2 * g + 2)
                    turn(0, first=True)
                    with pe.Fori(1, G) as g:
                        turn(g)
                    pe_down(N - 1, (N - 1) % 2, 0, NE + 1, last=True)

                @block.scalar
                def _(act):
                    def high_half(g, q0, free=True):
                        n = n0 + q0
                        act.wait_ge(w.landed[n % RING], 16 * (g + n // RING + 1))
                        if free:
                            act.wait_ge(w.filled, 6 * g + base + q0 - 1)
                        nc.scalar.activation(wh[:, q0 % 2, :], w.slots[:, n % RING, :], ACT.Copy).then_inc(wh_made, 1)

                    def unit(g, u0, next_up=True):
                        b, q0 = u0 % 2, 3 * u0
                        if u0:
                            high_half(g, q0 + 1)
                        act.wait_ge(w.filled, 6 * g + base + (q0 if u0 else 1))
                        if u0 > 1 or not isinstance(g, int):
                            act.wait_ge(scaled, 2 * g + u0 - 1)
                        nc.scalar.activation(silu[:, b].rearrange("p c s -> p (c s)"), ps[:, 2 * b, :], ACT.Silu).then_inc(silu_done, 1)
                        high_half(g, q0 + 2)
                        act.wait_ge(scaled, 2 * g + u0 + 1)
                        nc.scalar.activation(hh[:, b], hid[:], ACT.Copy).then_inc(hh_made, 1)
                        if next_up:
                            high_half(g, q0 + 3)
                    for i in range(2):
                        nc.scalar.activation(th[:, 4 * i:4 * i + 4], self.hT[:, 4 * i:4 * i + 4], ACT.Copy).then_inc(th_made, 1)
                    high_half(0, 0, free=False)
                    high_half(0, 1, free=False)
                    unit(0, 0)
                    unit(0, 1)
                    unit(0, 2)
                    with act.Fori(1, G - 1) as g:
                        unit(g, 1)
                        unit(g, 2)
                    unit(G - 1, 1)
                    unit(G - 1, 2, next_up=False)

                @block.vector
                def _(dve):
                    v = nc.vector

                    def low_half(g, q0):
                        dve.wait_ge(wh_made, 6 * g + q0 + 1)
                        v.tensor_tensor(wl[:, q0 % 2, :], w.slots[:, (n0 + q0) % RING, :], wh[:, q0 % 2, :].bitcast(F32),
                                        ALU.subtract).then_inc(wl_made, 1)

                    def unit(g, u0, next_up=True):
                        b, q0 = u0 % 2, 3 * u0
                        shared = isinstance(g, int) and g == 0 and u0 == 0
                        if not shared:
                            low_half(g, q0 + 1)
                            dve.wait_ge(hl_made, 2 * g + u0)
                        dve.wait_ge(w.filled, 6 * g + base + (2 if shared else q0 + 1))
                        dve.wait_ge(silu_done, 2 * g + u0 + 1)
                        up = ps[:, 2 * b + 1, :].rearrange("p (c s) -> p c s", c=EC)
                        last = v.tensor_tensor(hid[:], up, silu[:, b], ALU.mult)
                        if not shared:
                            last.then_inc(steps, 1)
                            dve.wait_ge(steps, 2 * g + u0)
                            par = (u0 - 1) % 2
                            dve.wait_ge(cb_landed[par], 16 * g + 16 * ((u0 - 1) // 2) + 16)
                            last = v.tensor_tensor(hid[:], hid[:], cb[:, par, :].unsqueeze(1).to_broadcast([P, EC, S]), ALU.mult)
                        last.then_inc(scaled, 1)
                        low_half(g, q0 + 2)
                        dve.wait_ge(hh_made, 2 * g + u0 + 1)
                        v.tensor_tensor(hl[:, b], hid[:], hh[:, b].bitcast(F32), ALU.subtract).then_inc(hl_made, 1)
                        if next_up:
                            low_half(g, q0 + 3)
                    for i in range(2):
                        dve.wait_ge(th_made, i + 1)
                        at = slice(4 * i, 4 * i + 4)
                        v.tensor_tensor(tl[:, at], self.hT[:, at], th[:, at].bitcast(F32), ALU.subtract).then_inc(tl_made, 1)
                    low_half(0, 0)
                    low_half(0, 1)
                    unit(0, 0)
                    unit(0, 1)
                    unit(0, 2)
                    with dve.Fori(1, G - 1) as g:
                        unit(g, 1)
                        unit(g, 2)
                    unit(G - 1, 1)
                    unit(G - 1, 2, next_up=False)
                    dve.wait_ge(w.filled, base + N)
                    ch = Chain(dve, st.sem("tail_steps"))
                    g2 = self.mod_row(3)
                    tmp = silu[:].rearrange("p b c s -> p (b c s)")
                    for t in range(TT):
                        for half_ in range(2):
                            ch.step(v.tensor_tensor(tmp[:, half_ * 512:(half_ + 1) * 512], y[t][half_],
                                                    g2[:, half_ * 512:(half_ + 1) * 512], ALU.mult))
                        ch.step(v.tensor_tensor(self.x[:, t, :], self.x[:, t, :], tmp, ALU.add))
            self.finished = frozenset(s for s, *_ in w.items[:after])

    def hybrid_layer(self):
        d = self.dram
        with ExitStack() as m1:
            mod1 = m1.enter_context(self.nc.sbuf_tensor("modulation_1", [P, 2 * D], F32))
            self.modulation("mod1", mod1, 0, 2 * D)
            self.await_constants()
            self.norm("norm1", self.x, self.hT, d["norm1_g"][0], modulate=(mod1[:, 0:D], mod1[:, D:2 * D]))
        self.rwkv()
        self.mod = self.keep("modulation_2", [P, 4 * D], layer=True)
        self.modulation("mod2", self.mod, 2 * D, 4 * D)
        self.project_z()
        self.sparse_attention()
        self.mix_and_project()
        self.norm("norm2", self.x, self.hT, d["norm2_g"][0], modulate=(self.mod_row(1), self.mod_row(2)))
        self.route()
        self.experts()

    def mod_row(self, i):
        return self.mod[:, i * D:(i + 1) * D]

    def unit(self, key, groups, dst, src_view, engine, first=True, last=True, scale=None, func=None):
        nc = self.nc

        def drain(eng, bank, chain):
            if engine == "act":
                return nc.scalar.activation(dst, src_view(bank), func or ACT.Copy, scale=scale or 1.0)
            if scale is not None:
                return nc.vector.tensor_scalar(dst, src_view(bank), scale, None, ALU.mult)
            return nc.vector.tensor_copy(dst, src_view(bank))
        return dict(key=key, mms=lambda bank, wv, _: groups(bank, wv), engine=engine, drain=drain, first=first, last=last)

    def rope(self, v, ch, src, dst, tmp, cos, sin):
        lo, hi = slice(0, 32), slice(32, 64)
        ix = (slice(None),) * (len(src.shape) - 1)
        ch.step(v.tensor_tensor(dst[ix + (lo,)], src[ix + (lo,)], cos, ALU.mult))
        ch.step(v.tensor_tensor(dst[ix + (hi,)], src[ix + (hi,)], cos, ALU.mult))
        ch.step(v.tensor_tensor(tmp[ix + (lo,)], src[ix + (hi,)], sin, ALU.mult))
        ch.step(v.tensor_tensor(tmp[ix + (hi,)], src[ix + (lo,)], sin, ALU.mult))
        ch.step(v.tensor_tensor(dst[ix + (lo,)], dst[ix + (lo,)], tmp[ix + (lo,)], ALU.subtract))
        return v.tensor_tensor(dst[ix + (hi,)], dst[ix + (hi,)], tmp[ix + (hi,)], ALU.add)

    def inverse_root(self, dve, ch, act_sem, wait_at, ms, root, tmp):
        v = self.nc.vector
        dve.wait_ge(act_sem, wait_at)
        ch.step(v.reciprocal(root, root))
        ch.step(v.tensor_tensor(tmp, root, root, ALU.mult))
        ch.step(v.tensor_tensor(tmp, tmp, ms, ALU.mult))
        ch.step(v.tensor_scalar(tmp, tmp, -0.5, 1.5, ALU.mult, ALU.add))
        ch.step(v.tensor_tensor(root, root, tmp, ALU.mult))

    def even_mixer(self):
        nc, ps, d = self.nc, self.psum, self.dram
        QR, QN = 192, 128
        with Stage(nc, "even") as top:
            mixT = top.sbuf("mixT", [P, DC, S])
            aqT, akT, av = top.sbuf("aqT", [P, 4, S]), top.sbuf("akT", [P, 4, S]), top.sbuf("av", [P, TT, 512])
            cq, ckr = top.sbuf("cq", [P, TT, 256]), top.sbuf("ckv_kr", [P, TT, 192])
            qnT, knT, vb = top.sbuf("qnT", [P, 4, S]), top.sbuf("knT", [P, 4, S]), top.sbuf("vb", [P, TT, 512])
            qrT, krT = top.sbuf("qrT", [P, 4, S]), top.sbuf("krT", [P, S])
            chunk, dist, rope = top.sbuf("chunk_mask", [P, TT, S]), top.sbuf("distance", [P, TT, S]), top.sbuf("rope", [P, 2, TT, 32])
            dbias = top.sbuf("distance_bias", [P, 4, TT, S])
            lam, lv = top.sbuf("lambda", [P, 4]), top.sbuf("lambda_vectors", [P, 4, DH])
            early = top.sem("constants_landed")
            with nc.Block() as block:
                @block.scalar
                def _(act):
                    loads = [(chunk[:], d["c_chunk"]), (dist[:], d["c_dist"]), (rope[:], d["c_rope"]),
                             (self.mem[:], d["mem_2"][0].rearrange("(t p) n -> p t n", p=P))]
                    for i, name in enumerate(("diff_lq1_2", "diff_lk1_2", "diff_lq2_2", "diff_lk2_2")):
                        loads.append((lv[:, i, :], d[name][0].partition_broadcast(P)))
                    for dst, src in loads:
                        act.dma_start(dst, src).then_inc(early, 16)
            self.norm_features("ev_norm", self.x, self.hT, d["ev_norm_2"][0])
            u = []
            for i in range(2):
                u.append(self.to_features(("ev_in", i), 2, self.hT, DC, (0, 1), aqT[:, 2 * i:2 * i + 2, :], ("act", "dve")[i]))
            for i in range(2):
                u.append(self.to_features(("ev_in", 2 + i), 2, self.hT, DC, (0, 1), akT[:, 2 * i:2 * i + 2, :], ("act", "dve")[i]))
            for i in range(2):
                u.append(self.to_tokens(("ev_in", 4 + i), self.hT, DC, 0, 256, av[:, :, i * 256:(i + 1) * 256], ("act", "dve")[i]))
            u.append(self.to_tokens(("ev_in", 6), self.hT, DC, 0, 256, cq[:], "act"))
            u.append(self.to_tokens(("ev_in", 7), self.hT, DC, 0, 192, ckr[:], "dve"))
            self.products("ev_in", u)

            with Stage(nc, "mlan") as st:
                cqT, ckvT = st.sbuf("cqT", [P, 2, S]), st.sbuf("ckvT", [P, S])
                sq, stat = st.sbuf("square", [P, TT, 256]), st.sbuf("stat", [P, 3, 4])
                kr, krt = st.sbuf("kr", [P, TT, DH]), st.sbuf("kr_tmp", [P, TT, DH])
                summed, rooted, steps, ready, turned = (st.sem(x) for x in (
                    "summed", "rooted", "steps", "ready", "turned"))
                with nc.Block() as block:
                    self.weight_loads(block, "mlan")

                    @block.scalar
                    def _(act):
                        act.wait_ge(summed, 1)
                        nc.scalar.activation(lam[:, 2:4], lam[:, 0:2], ACT.Exp).then_inc(rooted, 1)
                        nc.scalar.activation(stat[:, 1, :], stat[:, 0, :], ACT.Sqrt).then_inc(rooted, 1)

                    @block.vector
                    def _(dve):
                        v, ch = nc.vector, Chain(dve, steps)
                        for t in range(TT):
                            for j, (src, n) in enumerate(((cq[:, t, :], 256), (ckr[:, t, 0:P], P))):
                                ch.step(v.tensor_tensor_reduce(out=sq[:, t, 0:n], in0=src, in1=src, scale=1.0, scalar=0.0,
                                                               op0=ALU.mult, op1=ALU.add, accum_out=stat[:, 0, 2 * j + t:2 * j + t + 1]))
                        for j, n in enumerate((256, P)):
                            ch.step(v.tensor_scalar(stat[:, 0, 2 * j:2 * j + 2], stat[:, 0, 2 * j:2 * j + 2], 1.0 / n, 1e-6, ALU.mult, ALU.add))
                        dve.wait_ge(early, 16 * 8)
                        for j in range(2):
                            last = v.tensor_tensor_reduce(out=sq[:, 0, 0:DH], in0=lv[:, 2 * j, :], in1=lv[:, 2 * j + 1, :], scale=1.0,
                                                          scalar=0.0, op0=ALU.mult, op1=ALU.add, accum_out=lam[:, j:j + 1])
                            ch.step(last) if j == 0 else last.then_inc(summed, 1)
                        dve.wait_ge(summed, 1)
                        for h in range(4):
                            ch.step(v.scalar_tensor_tensor(out=dbias[:, h], in0=dist[:], scalar=2.0 ** (-2.0 * (h + 1)), in1=chunk[:],
                                                           op0=ALU.mult, op1=ALU.add))
                        ch.step(self.rope(v, ch, ckr[:, :, P:P + DH], kr, krt, rope[:, 0], rope[:, 1]))
                        self.inverse_root(dve, ch, rooted, 2, stat[:, 0, :], stat[:, 1, :], stat[:, 2, :])
                        ch.step(v.tensor_tensor(lam[:, 0:1], lam[:, 3:4], lam[:, 2:3], ALU.subtract))
                        ch.step(v.tensor_scalar(lam[:, 0:1], lam[:, 0:1], -LAMBDA_INIT, None, ALU.add))
                        for t in range(TT):
                            ch.step(v.tensor_scalar(cq[:, t, :], cq[:, t, :], stat[:, 1, t:t + 1], None, ALU.mult))
                            last = v.tensor_scalar(ckr[:, t, 0:P], ckr[:, t, 0:P], stat[:, 1, 2 + t:3 + t], None, ALU.mult)
                            ch.step(last) if t == 0 else last.then_inc(ready, 1)
                        dve.wait_ge(turned, 1)
                        for c in range(2):
                            ch.step(v.tensor_scalar(cqT[:, c, :], ps[:, 0, c * S:(c + 1) * S], self.column("mla_g_cq_2", c), None, ALU.mult))
                        ch.step(v.tensor_scalar(ckvT[:], ps[:, 1, 0:S], self.column("mla_g_ckv_2"), None, ALU.mult))
                        ch.step(v.tensor_copy(krT[0:DH, :], ps[0:DH, 2, 0:S]))
                        ch.step(v.memset(krT[DH:P, :], 0.0))
                        ch.step(v.memset(qrT[DH:P, :, :], 0.0))

                    @block.tensor
                    def _(pe):
                        pe.wait_ge(ready, 1)
                        for t in range(TT):
                            for c in range(2):
                                nc.tensor.transpose(ps[:, 0, c * S + t * P:c * S + (t + 1) * P], cq[:, t, c * P:(c + 1) * P], self.ident[:, :])
                            nc.tensor.transpose(ps[:, 1, t * P:(t + 1) * P], ckr[:, t, 0:P], self.ident[:, :])
                            mm = nc.tensor.transpose(ps[0:DH, 2, t * P:(t + 1) * P], kr[:, t, :], self.ident[:, :])
                        mm.then_inc(turned, 1)

                qr, qrt = st.sbuf("qr", [P, TT, 4, DH]), st.sbuf("qr_tmp", [P, TT, 4, DH])
                u = []
                two = lambda b: b.rearrange("p (c s) -> p c s", c=2)
                for i in range(2):
                    u.append(self.unit(("w_uq", 0), lambda bank, wv, i=i: [
                        (bank[:, j * S:(j + 1) * S], [(wv[:, k, (2 * i + j) * QR:(2 * i + j) * QR + QN], cqT[:, k, :]) for k in range(2)])
                        for j in range(2)], qnT[:, 2 * i:2 * i + 2, :], two, ("act", "dve")[i], first=(i == 0), last=False))
                u.append(self.unit(("w_uq", 0), lambda bank, wv: [
                    (bank[:, (4 * t + h) * DH:(4 * t + h + 1) * DH],
                     [(cqT[:, k, t * P:(t + 1) * P], wv[:, k, h * QR + QN:(h + 1) * QR]) for k in range(2)])
                    for t in range(TT) for h in range(4)],
                    qr[:].rearrange("p t h e -> p (t h e)"), lambda b: b, "act", first=False))
                for i in range(2):
                    u.append(self.unit(("w_ukv", 0), lambda bank, wv, i=i: [
                        (bank[:, j * S:(j + 1) * S], [(wv[:, 0, (2 * i + j) * 256:(2 * i + j) * 256 + P], ckvT[:, :])])
                        for j in range(2)], knT[:, 2 * i:2 * i + 2, :], two, ("act", "dve")[i], first=(i == 0), last=False))
                for t in range(TT):
                    u.append(self.unit(("w_ukv", 0), lambda bank, wv, t=t: [
                        (bank[:, h * P:(h + 1) * P], [(ckvT[:, t * P:(t + 1) * P], wv[:, 0, h * 256 + P:(h + 1) * 256])])
                        for h in range(4)], vb[:, t, :], lambda b: b, ("act", "dve")[t], first=False, last=(t == 1)))
                self.products("mla_up", u)
                out = st.sbuf("qr_turned", [P, TT, 4, DH])
                s3, r3, t3 = st.sem("rope_steps"), st.sem("rope_ready"), st.sem("rope_turned")
                with nc.Block() as block:
                    self.weight_loads(block, "qrope")

                    @block.vector
                    def _(dve):
                        v, ch = nc.vector, Chain(dve, s3)
                        for t in range(TT):
                            cos, sin = (rope[:, i, t, :].unsqueeze(1).to_broadcast([P, 4, 32]) for i in range(2))
                            last = self.rope(v, ch, qr[:, t], out[:, t], qrt[:, t], cos, sin)
                            last.then_inc(r3, 1)
                            dve.wait_ge(r3, t + 1)
                        dve.wait_ge(t3, 1)
                        for b in range(2):
                            ch.step(v.tensor_copy(qrT[0:DH, 2 * b:2 * b + 2, :], two(ps[0:DH, b, :])))

                    @block.tensor
                    def _(pe):
                        for t in range(TT):
                            pe.wait_ge(r3, t + 1)
                            for h in range(4):
                                o = (h % 2) * S + t * P
                                mm = nc.tensor.transpose(ps[0:DH, h // 2, o:o + P], out[:, t, h, :], self.ident[:, :])
                        mm.then_inc(t3, 1)

            with Stage(nc, "diffo") as st:
                od = st.sbuf("diff_out", [P, TT, 512])
                units = []
                for h in range(4):
                    units.append(dict(
                        scores=lambda banks, h=h: [
                            (banks[s][:, t * S:(t + 1) * S],
                             [(aqT[s * DH:(s + 1) * DH, h, t * P:(t + 1) * P], akT[s * DH:(s + 1) * DH, h, :])])
                            for s in range(2) for t in range(TT)],
                        bias=dbias[:, h],
                        values=lambda bank, pT, h=h: [
                            (bank[:, t * P:(t + 1) * P],
                             [(pT[:, kt, t * P:(t + 1) * P], av[:, kt, h * P:(h + 1) * P]) for kt in range(TT)]) for t in range(TT)],
                        result=lambda bank, h=h: (od[:, :, h * P:(h + 1) * P], bank[:, 0:S].rearrange("p (t e) -> p t e", t=TT))))
                self.attend("diff", units, DH ** -0.5, ns=2, neg_lam=lam[:, 0:1])
                sq, stat = st.sbuf("square", [P, TT * 4, P]), st.sbuf("stat", [P, 3, TT * 4])
                steps, summed, rooted, ready, turned = (st.sem(x) for x in ("steps", "summed", "rooted", "ready", "turned"))
                o8 = od[:].rearrange("p t (h e) -> p (t h) e", h=4)
                with nc.Block() as block:
                    self.weight_loads(block, "diffn")

                    @block.scalar
                    def _(act):
                        act.wait_ge(summed, 1)
                        nc.scalar.activation(stat[:, 1, :], stat[:, 0, :], ACT.Sqrt).then_inc(rooted, 1)

                    @block.vector
                    def _(dve):
                        v, ch = nc.vector, Chain(dve, steps)
                        ch.step(v.tensor_tensor(sq[:], o8, o8, ALU.mult))
                        ch.step(v.tensor_reduce(stat[:, 0, :], sq[:], AX.X, ALU.add))
                        v.tensor_scalar(stat[:, 0, :], stat[:, 0, :], 1.0 / P, 1e-6, ALU.mult, ALU.add).then_inc(summed, 1)
                        self.inverse_root(dve, ch, rooted, 1, stat[:, 0, :], stat[:, 1, :], stat[:, 2, :])
                        v.tensor_tensor(o8, o8, stat[:, 1, :].unsqueeze(2).to_broadcast([P, TT * 4, P]), ALU.mult).then_inc(ready, 1)
                        dve.wait_ge(turned, 1)
                        for b in range(2):
                            ch.step(v.tensor_scalar(mixT[:, 2 * b:2 * b + 2, :], ps[:, b, :].rearrange("p (c s) -> p c s", c=2),
                                                    self.column("diff_subln_2"), 1.0 - LAMBDA_INIT, ALU.mult, ALU.mult))

                    @block.tensor
                    def _(pe):
                        pe.wait_ge(ready, 1)
                        for h in range(4):
                            for t in range(TT):
                                o = (h % 2) * S + t * P
                                mm = nc.tensor.transpose(ps[:, h // 2, o:o + P], od[:, t, h * P:(h + 1) * P], self.ident[:, :])
                        mm.then_inc(turned, 1)
            units = []
            for h in range(4):
                units.append(dict(
                    scores=lambda banks, h=h: [
                        (banks[0][:, t * S:(t + 1) * S],
                         [(qnT[:, h, t * P:(t + 1) * P], knT[:, h, :]), (qrT[:, h, t * P:(t + 1) * P], krT[:, :])]) for t in range(TT)],
                    bias=chunk[:],
                    values=lambda bank, pT, h=h: [(bank[:, 0:S], [(vb[:, kt, h * P:(h + 1) * P], pT[:, kt, :]) for kt in range(TT)])],
                    result=lambda bank, h=h: (mixT[:, 4 + h, :], bank[:, 0:S])))
            self.attend("mla", units, QR ** -0.5)
            self.residual("ev_out", "ev_out", mixT, DC, 0)

    def odd_mixer(self):
        nc, ps = self.nc, self.psum
        NH = 16
        with Stage(nc, "odd") as top:
            qT, kT, vt = top.sbuf("qT", [P, DC, S]), top.sbuf("kT", [P, DC, S]), top.sbuf("v", [P, TT, D])
            oT = top.sbuf("oT", [P, DC, S])
            later, ones, outside = top.sbuf("later", [P, P]), top.sbuf("ones", [P, P]), top.sbuf("outside", [P, TT, S])
            self.norm_features("od_norm", self.x, self.hT, self.dram["od_norm_2"][0])
            u = []
            two = lambda b: b.rearrange("p (c s) -> p c s", c=2)
            for i in range(4):
                x = self.to_features(("sb_in", i), 2, self.hT, DC, (0, 1), qT[:, 2 * i:2 * i + 2, :], "act")
                x["drain"] = lambda eng, bank, chain, i=i: nc.scalar.activation(
                    qT[:, 2 * i:2 * i + 2, :], two(bank), ACT.Copy, scale=DH ** -0.5)
                u.append(x)
            for i in range(4):
                u.append(self.to_features(("sb_in", 4 + i), 2, self.hT, DC, (0, 1), kT[:, 2 * i:2 * i + 2, :], "dve"))
            for i in range(4):
                u.append(self.to_tokens(("sb_in", 8 + i), self.hT, DC, 0, 256, vt[:, :, i * 256:(i + 1) * 256], ("act", "dve")[i % 2]))
            self.products("sb_in", u)
            NU = NH // 2
            with Stage(nc, "sb") as st:
                ln, sp, pr = (st.sbuf(x, [P, 2, 2, TT * S]) for x in ("ln", "softplus", "prob"))
                zm = st.sbuf("z_masked", [P, 3, 2, TT * S])
                scored, lned, spd, summed, argd, exped, valued, stored, steps, asteps, cl, made = (st.sem(x) for x in (
                    "scored", "ln_done", "softplus_done", "summed", "arg_done", "exped", "valued", "stored", "steps", "act_steps",
                    "const_landed", "const_made"))
                flat = lambda t: t[:].rearrange("p t s -> p (t s)").unsqueeze(1).to_broadcast([P, 2, TT * S])
                with nc.Block() as block:
                    self.weight_loads(block, "sb")

                    @block.tensor
                    def _(pe):
                        def scores(u):
                            if u >= 2:
                                pe.wait_ge(spd, u - 1)
                            for h in range(2):
                                lo = DH * h
                                for kt in range(TT):
                                    mm = nc.tensor.matmul(ps[:, 2 * (u % 2) + h, kt * S:(kt + 1) * S],
                                                          kT[lo:lo + DH, u, kt * P:(kt + 1) * P], qT[lo:lo + DH, u, :],
                                                          start=True, stop=True)
                            mm.then_inc(scored, 1)

                        scores(0)
                        scores(1)
                        for i in range(1, NU + 2):
                            if i <= NU:
                                u = i - 1
                                pe.wait_ge(spd, u + 1)
                                if u == 0:
                                    pe.wait_ge(made, 1)
                                    pe.wait_ge(cl, 16)
                                else:
                                    pe.wait_ge(argd, u)
                                for h in range(2):
                                    s, b = sp[:, u % 2, h, :], ps[:, 4 + h, :]
                                    nc.tensor.matmul(b[:, 0:S], later[:, :], s[:, 0:S], start=True, stop=False)
                                    nc.tensor.matmul(b[:, 0:S], ones[:, :], s[:, S:2 * S], start=False, stop=True)
                                    mm = nc.tensor.matmul(b[:, S:2 * S], later[:, :], s[:, S:2 * S], start=True, stop=True)
                                mm.then_inc(summed, 1)
                            if i + 1 < NU:
                                scores(i + 1)
                            if i >= 2:
                                u = i - 2
                                pe.wait_ge(exped, u + 1)
                                if u >= 2:
                                    pe.wait_ge(stored, u - 1)
                                for h in range(2):
                                    lo = DH * h
                                    for kt in range(TT):
                                        mm = nc.tensor.matmul(ps[lo:lo + DH, 6 + u % 2, 0:S],
                                                              vt[:, kt, (2 * u + h) * DH:(2 * u + h + 1) * DH],
                                                              pr[:, u % 2, h, kt * S:(kt + 1) * S], start=(kt == 0), stop=(kt == TT - 1))
                                mm.then_inc(valued, 1)

                    @block.scalar
                    def _(act):
                        act.dma_start(later[:], self.dram["c_later"]).then_inc(cl, 16)
                        ch = Chain(act, asteps)
                        for i in range(NU + 2):
                            if i < NU:
                                b = i % 2
                                act.wait_ge(scored, i + 1)
                                if i >= 2:
                                    act.wait_ge(spd, i - 1)
                                ch.step(nc.scalar.activation(ln[:, b], ps[:, 2 * b:2 * b + 2, :], ACT.Abs))
                                ch.step(nc.scalar.activation(ln[:, b], ln[:, b], ACT.Exp, scale=-1.0))
                            if i >= 2:
                                u = i - 2
                                act.wait_ge(argd, u + 1)
                                if u >= 2:
                                    act.wait_ge(valued, u - 1)
                                nc.scalar.activation(pr[:, u % 2], zm[:, u % 3], ACT.Exp).then_inc(exped, 1)
                            if i < NU:
                                nc.scalar.activation(ln[:, b], ln[:, b], ACT.Ln, bias=1.0).then_inc(lned, 1)

                    @block.vector
                    def _(dve):
                        v, ch = nc.vector, Chain(dve, steps)
                        v.memset(ones[:], 1.0).then_inc(made, 1)
                        ch.step(v.tensor_scalar(outside[:], self.strict[:], -1.0, BIG, ALU.add, ALU.mult))
                        for i in range(NU + 2):
                            if i < NU:
                                b = i % 2
                                z = ps[:, 2 * b:2 * b + 2, :]
                                dve.wait_ge(lned, i + 1)
                                if i >= 2:
                                    dve.wait_ge(summed, i - 1)
                                if i >= 3:
                                    dve.wait_ge(exped, i - 2)
                                ch.step(v.scalar_tensor_tensor(out=sp[:, b], in0=z, scalar=0.0, in1=ln[:, b], op0=ALU.max, op1=ALU.add))
                                ch.step(v.tensor_tensor(zm[:, i % 3], z, flat(outside), ALU.add))
                                v.tensor_tensor(sp[:, b], sp[:, b], flat(self.strict), ALU.mult).then_inc(spd, 1)
                            if 1 <= i <= NU:
                                u = i - 1
                                dve.wait_ge(summed, u + 1)
                                v.tensor_tensor(zm[:, u % 3], zm[:, u % 3], ps[:, 4:6, :], ALU.subtract).then_inc(argd, 1)
                            if i >= 2:
                                u = i - 2
                                dve.wait_ge(valued, u + 1)
                                v.tensor_copy(oT[:, u, :], ps[:, 6 + u % 2, 0:S]).then_inc(stored, 1)
                        dve.wait_ge(stored, NU)
            self.residual("sb_out", "sb_out", oT, DC, 0)

    def cross(self, i):
        nc, d = self.nc, self.dram
        with Stage(nc, f"cross{i}") as top:
            memT, mkT = top.sbuf("memT", [P, DC, S]), top.sbuf("kT", [P, DC, S])
            mv, qT, oT = top.sbuf("v", [P, TT, D]), top.sbuf("qT", [P, DC, S]), top.sbuf("oT", [P, DC, S])
            self.norm_features(f"mem_norm{i}", self.mem, memT, d["xa_mem_norm_2"][i])
            u = []
            for j in range(4):
                u.append(self.to_features((("xa_wkv", i), j), 2, memT, DC, (0, 1), mkT[:, 2 * j:2 * j + 2, :], ("act", "dve")[j % 2]))
            for j in range(4):
                u.append(self.to_tokens((("xa_wkv", i), 4 + j), memT, DC, 0, 256, mv[:, :, j * 256:(j + 1) * 256], ("act", "dve")[j % 2]))
            self.products(f"xa_kv{i}", u)
            self.norm_features(f"xa_norm{i}", self.x, self.hT, d["xa_norm_2"][i])
            self.products(f"xa_q{i}", [
                self.to_features((("xa_wq", i), j), 2, self.hT, DC, (0, 1), qT[:, 2 * j:2 * j + 2, :], ("act", "dve")[j % 2])
                for j in range(4)])
            units = []
            for h in range(4):
                units.append(dict(
                    scores=lambda banks, h=h: [
                        (banks[0][:, t * S:(t + 1) * S],
                         [(qT[:, 2 * h + c, t * P:(t + 1) * P], mkT[:, 2 * h + c, :]) for c in range(2)]) for t in range(TT)],
                    bias=None,
                    values=lambda bank, pT, h=h: [
                        (bank[:, c * S:(c + 1) * S],
                         [(mv[:, kt, h * 256 + c * P:h * 256 + (c + 1) * P], pT[:, kt, :]) for kt in range(TT)]) for c in range(2)],
                    result=lambda bank, h=h: (oT[:, 2 * h:2 * h + 2, :], bank.rearrange("p (c s) -> p c s", c=2))))
            self.attend(f"xa{i}", units, 256 ** -0.5)
            self.residual(f"xa_o{i}", ("xa_wo", i), oT, DC, 0)

    def mlp(self, i):
        nc, ps, w = self.nc, self.psum, self.w
        NG = 16
        with Stage(nc, f"mlps{i}") as st:
            hid = st.sbuf("hidden", [P, 2 * NG, S])
            self.norm_features(f"mlp_norm{i}", self.x, self.hT, self.dram["mlp_norm_2"][i])
            units = []
            for g in range(NG):
                u = self.to_features((("mlp_w1", i), g), 2, self.hT, DC, (0, 1), None, "act")

                def drain(eng, bank, chain, g=g):
                    h = hid[:, 2 * g:2 * g + 2, :]
                    chain.step(nc.scalar.activation(h, bank.rearrange("p (c s) -> p c s", c=2), ACT.Relu))
                    return nc.scalar.activation(h, h, ACT.Square)
                u["drain"] = drain
                units.append(u)
            self.products(f"mlp{i}", units)
            base, n0 = w.n_filled, w.index[(("mlp_w2", i), 0)]
            for g in range(NG):
                w.done_at[n0 + g] = base + g + 1
            w.n_filled = base + NG
            wh, wl = st.sbuf("weights_high", [P, 2, 2, D], FR), st.sbuf("weights_low", [P, 2, 2, D], FR)
            hh, hl = st.sbuf("hidden_high", [P, 2, 2, S], FR), st.sbuf("hidden_low", [P, 2, 2, S], FR)
            added, high_made, low_made = st.sem("added"), st.sem("high_made"), st.sem("low_made")
            with nc.Block() as block:
                self.weight_loads(block, f"mlpd{i}")

                @block.tensor
                def _(pe):
                    for g in range(NG):
                        key, b = (("mlp_w2", i), g), g % 2
                        if g == 0:
                            w.arrived(pe, key)
                            steps = [(hid[:, 0:2, :], w.view(key))]
                        else:
                            pe.wait_ge(low_made, 2 * g)
                            steps = [(hh[:, b], wh[:, b]), (hh[:, b], wl[:, b]), (hl[:, b], wh[:, b])]
                        for t in range(TT):
                            for c in range(2):
                                for s, (a, x) in enumerate(steps):
                                    for half in range(2):
                                        mm = nc.tensor.matmul(ps[:, 2 * t + half, :], a[:, c, t * P:(t + 1) * P],
                                                              x[:, c, half * 512:(half + 1) * 512], start=(g == 0 and c == 0),
                                                              stop=(g == NG - 1 and c == 1 and s == len(steps) - 1),
                                                              skip_group_check=True)
                        mm.then_inc(w.filled, 1)

                @block.scalar
                def _(act):
                    for g in range(1, NG):
                        w.arrived(act, (("mlp_w2", i), g))
                        if g >= 3:
                            act.wait_ge(w.filled, base + g - 1)
                        nc.scalar.activation(wh[:, g % 2], w.view((("mlp_w2", i), g)), ACT.Copy).then_inc(high_made, 1)
                        nc.scalar.activation(hh[:, g % 2], hid[:, 2 * g:2 * g + 2, :], ACT.Copy).then_inc(high_made, 1)

                @block.vector
                def _(dve):
                    for g in range(1, NG):
                        b = g % 2
                        dve.wait_ge(high_made, 2 * g - 1)
                        nc.vector.tensor_tensor(wl[:, b], w.view((("mlp_w2", i), g)), wh[:, b].bitcast(F32),
                                                ALU.subtract).then_inc(low_made, 1)
                        dve.wait_ge(high_made, 2 * g)
                        nc.vector.tensor_tensor(hl[:, b], hid[:, 2 * g:2 * g + 2, :], hh[:, b].bitcast(F32),
                                                ALU.subtract).then_inc(low_made, 1)
                    dve.wait_ge(w.filled, base + NG)
                    for t in range(TT):
                        for half in range(2):
                            x = self.x[:, t, half * 512:(half + 1) * 512]
                            nc.vector.tensor_tensor(x, x, ps[:, 2 * t + half, :], ALU.add).then_inc(added, 1)
                    dve.wait_ge(added, 4)

    def run(self):
        nc, d = self.nc, self.dram
        self.load_constants()
        self.hybrid_layer()
        self.layer.close()
        self.norm("final_g", self.x, None, d["final_g"], tokens=self.x)
        self.mem = self.keep("memory", [P, TT, D])
        self.even_mixer()
        for i in range(2):
            if i == 1:
                self.odd_mixer()
            self.cross(i)
            self.mlp(i)
        self.norm("final", self.x, None, d["final_norm_2"], out_dram=self.out[0].rearrange("(t p) n -> p t n", p=P))


def hybrid_program(nc, dram, out):
    k = Hybrid(nc, dram, out)
    k.run()
    k.layer.close()
    k.ctx.close()


def kernel(**inputs):
    import concourse.bacc as bacc
    from concourse.bass_utils import run_bass_kernel_spmd

    nc = bacc.Bacc("TRN2", target_bir_lowering=False, num_devices=1)
    arrays, dram = {}, {}
    for name, a in list(inputs.items()) + list(shape_constants().items()):
        a = np.ascontiguousarray(a)
        arrays[f"in_{name}"] = a
        dram[name] = nc.dram_tensor(f"in_{name}", a.shape, mybir.dt.from_np(a.dtype), kind="ExternalInput").ap()
    out = nc.dram_tensor("out_0", (1, S, D), F32, kind="ExternalOutput").ap()
    hybrid_program(nc, dram, out)
    r = run_bass_kernel_spmd(nc, [arrays], core_ids=[0])
    return r.results[0]["out_0"]
```
